# Optimizing a Trainium2 kernel written in Bass

```python
import jax, jax.numpy as jnp
from jax import lax
import numpy as np

D_MODEL = 1024
BATCH = 1
SEQ = 1024
DEPTH = 1
DEC_BATCH = 8
DEC_SEQ = 1
PAST_LEN = 8192
PAGE_SIZE = 128

D_MIX = D_MODEL
D_A = D_MIX // 2
HEAD_A = 64
H_A = D_A // HEAD_A
LORA_W = 64
LORA_A = 64
LORA_G = 128
P_A = 3 * D_A + LORA_W + LORA_A + LORA_G
A_SPLITS = [D_A, 2 * D_A, 3 * D_A, 3 * D_A + LORA_W, 3 * D_A + LORA_W + LORA_A]
D_C = D_MIX - D_A
G_C = 8
HEAD_C = D_C // G_C
CHUNK = 128
P_C = 2 * D_C
P_TOTAL = P_A + P_C
N_KEYS = 128
N_EXPERTS = N_KEYS * N_KEYS
PEER_HEADS = 8
PEER_TOPK = 16
D_KEY = 256
D_HALF = D_KEY // 2
PEER_BLOCK = 128
D_PLE = 256
RMS_EPS = 1e-6
LN_EPS = 1e-5
GN_EPS = 64e-5

kernel_name = 'rwkv7_chunkgmlp_peer_hybrid_step'

def rmsnorm(x, g):
    xf = x.astype(jnp.float32)
    y = xf * lax.rsqrt(jnp.mean(xf * xf, axis=-1, keepdims=True) + RMS_EPS) * g
    return y.astype(x.dtype)

def rwkv_group(pa, shift_prev, wkv_prev, mu, w0, w2, a0, a2, g2, k_k, k_a, r_k, ln_g, ln_b):
    B, L, _ = pa.shape
    f32 = jnp.float32
    prev_rows = jnp.concatenate([shift_prev[:, None, :].astype(pa.dtype), pa[:, :-1]], axis=1)
    xm = pa + (prev_rows - pa) * mu
    r, k, v, wl, al, gl = jnp.split(xm, A_SPLITS, axis=-1)
    w = -jax.nn.softplus(-(w0 + jnp.tanh(wl) @ w2).astype(f32)) - 0.5
    decay = jnp.exp(-jnp.exp(w))
    a = jax.nn.sigmoid((a0 + al @ a2).astype(f32))
    g = jax.nn.sigmoid(gl) @ g2
    heads = lambda t: t.astype(f32).reshape(B, L, H_A, HEAD_A)
    kk = heads(k * k_k)
    kk = kk / jnp.maximum(jnp.sqrt(jnp.sum(kk * kk, axis=-1, keepdims=True)), 1e-12)
    k_h = heads(k.astype(f32) * (1.0 + (a - 1.0) * k_a))
    r_h, v_h, a_h, w_h = heads(r), heads(v), heads(a), heads(decay)
    to_time = lambda t: jnp.swapaxes(t, 0, 1)

    def step(S, inp):
        r_t, k_t, v_t, w_t, kk_t, a_t = inp
        sa = jnp.einsum('bhvk,bhk->bhv', S, -kk_t)
        S = (S * w_t[:, :, None, :] + sa[..., None] * (kk_t * a_t)[:, :, None, :]
             + v_t[..., None] * k_t[:, :, None, :])
        return S, jnp.einsum('bhvk,bhk->bhv', S, r_t)

    xs = tuple(to_time(t) for t in (r_h, k_h, v_h, w_h, kk, a_h))
    S_fin, ys = lax.scan(step, wkv_prev.astype(f32), xs)
    y = jnp.swapaxes(ys, 0, 1)
    mean = jnp.mean(y, axis=-1, keepdims=True)
    var = jnp.mean(jnp.square(y - mean), axis=-1, keepdims=True)
    yn = ((y - mean) * lax.rsqrt(var + GN_EPS)).reshape(B, L, D_A) * ln_g + ln_b
    bonus = (jnp.sum(r_h * k_h * r_k, axis=-1, keepdims=True) * v_h).reshape(B, L, D_A)
    out = ((yn + bonus) * g).astype(pa.dtype)
    return out, S_fin.astype(wkv_prev.dtype), pa[:, -1]

def chunk_mlp(pc, ln_g, ln_b, ws, bs):
    B, L, _ = pc.shape
    u, v = jnp.split(jax.nn.gelu(pc, approximate=False), 2, axis=-1)
    vg = v.astype(jnp.float32).reshape(B, L, G_C, HEAD_C)
    mean = jnp.mean(vg, axis=-1, keepdims=True)
    var = jnp.mean(jnp.square(vg - mean), axis=-1, keepdims=True)
    vn = (vg - mean) * lax.rsqrt(var + LN_EPS) * ln_g.reshape(G_C, HEAD_C) + ln_b.reshape(G_C, HEAD_C)
    n_chunks = -(-L // CHUNK)
    pad = n_chunks * CHUNK - L
    vp = jnp.pad(vn, ((0, 0), (0, pad), (0, 0), (0, 0))).reshape(B, n_chunks, CHUNK, G_C, HEAD_C)
    causal = jnp.tril(jnp.ones((CHUNK, CHUNK), dtype=bool))
    wsm = jnp.where(causal[None], ws, jnp.zeros_like(ws))
    s = jnp.einsum('gij,bcjgd->bcigd', wsm, vp) + jnp.swapaxes(bs, 0, 1)[None, None, :, :, None]
    s = s.reshape(B, n_chunks * CHUNK, D_C)[:, :L]
    out = (u * s).astype(pc.dtype)
    return out, vn.reshape(B, L, D_C).astype(pc.dtype)

def peer_ffn(h, wq, subkeys, U, V):
    B, L, D = h.shape
    T = B * L
    xt = h.reshape(T, D)
    q = (xt @ wq).reshape(T, PEER_HEADS, 2, D_HALF)
    sc = jnp.einsum('thcd,cnd->thcn', q, subkeys).astype(jnp.float32)
    sv, si = lax.top_k(sc, PEER_TOPK)
    cand = sv[:, :, 0, :, None] + sv[:, :, 1, None, :]
    cand_idx = si[:, :, 0, :, None] * N_KEYS + si[:, :, 1, None, :]
    cv, ci = lax.top_k(cand.reshape(T, PEER_HEADS, PEER_TOPK * PEER_TOPK), PEER_TOPK)
    eidx = jnp.take_along_axis(cand_idx.reshape(T, PEER_HEADS, PEER_TOPK * PEER_TOPK), ci, axis=-1)
    gate = jax.nn.softmax(cv, axis=-1)
    HK = PEER_HEADS * PEER_TOPK
    nb = -(-T // PEER_BLOCK)
    pad = nb * PEER_BLOCK - T
    xb = jnp.pad(xt, ((0, pad), (0, 0))).reshape(nb, PEER_BLOCK, D)
    eb = jnp.pad(eidx.reshape(T, HK), ((0, pad), (0, 0))).reshape(nb, PEER_BLOCK, HK)
    gb = jnp.pad(gate.reshape(T, HK), ((0, pad), (0, 0))).reshape(nb, PEER_BLOCK, HK)

    def block(args):
        x_b, e_b, g_b = args
        u_rows = jnp.take(U, e_b, axis=0)
        act = jax.nn.gelu(jnp.einsum('tkd,td->tk', u_rows, x_b).astype(jnp.float32), approximate=False) * g_b
        v_rows = jnp.take(V, e_b, axis=0)
        return jnp.einsum('tk,tkd->td', act.astype(v_rows.dtype), v_rows)

    out = lax.map(block, (xb, eb, gb)).reshape(nb * PEER_BLOCK, D)[:T]
    return out.reshape(B, L, D).astype(h.dtype)

def decoder_layer(x, p, wkv_prev, shift_prev, lp):
    (norm_mix_g, w_in, shift_mu, rwkv_w0, rwkv_w2, rwkv_a0, rwkv_a2, rwkv_g2,
     rwkv_k_k, rwkv_k_a, rwkv_r_k, rwkv_ln_g, rwkv_ln_b, cmlp_ln_g, cmlp_ln_b,
     cmlp_ws, cmlp_bs, w_out, norm_ffn_g, peer_wq, peer_subkeys, peer_u, peer_v,
     norm_ple_g, ple_w, ple_gate_w) = lp
    proj = rmsnorm(x, norm_mix_g) @ w_in
    ya, wkv_new, shift_new = rwkv_group(proj[..., :P_A], shift_prev, wkv_prev, shift_mu,
                                        rwkv_w0, rwkv_w2, rwkv_a0, rwkv_a2, rwkv_g2,
                                        rwkv_k_k, rwkv_k_a, rwkv_r_k, rwkv_ln_g, rwkv_ln_b)
    yc, v_rows = chunk_mlp(proj[..., P_A:], cmlp_ln_g, cmlp_ln_b, cmlp_ws, cmlp_bs)
    x = x + jnp.concatenate([ya, yc], axis=-1) @ w_out
    x = x + peer_ffn(rmsnorm(x, norm_ffn_g), peer_wq, peer_subkeys, peer_u, peer_v)
    gate = jax.nn.sigmoid((rmsnorm(x, norm_ple_g) @ ple_gate_w).astype(jnp.float32))
    x = x + ((p @ ple_w) * gate).astype(x.dtype)
    return x, wkv_new, shift_new, v_rows

def setup_inputs(seed: int = 0) -> dict:
    key = jax.random.key(seed)
    ks = iter(jax.random.split(key, 40))
    nrm = lambda shape, scale: jax.random.normal(next(ks), shape, jnp.float32) * scale
    uni = lambda shape, lo, hi: jax.random.uniform(next(ks), shape, jnp.float32, lo, hi)
    gain = lambda shape: 1.0 + nrm(shape, 0.02)
    return {
        'x_prompt': nrm((BATCH, SEQ, D_MODEL), 1.0),
        'x_sample': nrm((DEC_BATCH, DEC_SEQ, D_MODEL), 1.0),
        'state_wkv': nrm((DEPTH, DEC_BATCH, H_A, HEAD_A, HEAD_A), 0.3),
        'state_shift': nrm((DEPTH, DEC_BATCH, P_A), 1.0),
        'p_prompt': nrm((DEPTH, BATCH, SEQ, D_PLE), 1.0),
        'p_sample': nrm((DEPTH, DEC_BATCH, DEC_SEQ, D_PLE), 1.0),
        'norm_mix_g': gain((DEPTH, D_MODEL)),
        'w_in': nrm((DEPTH, D_MODEL, P_TOTAL), D_MODEL ** -0.5),
        'shift_mu': uni((DEPTH, P_A), 0.0, 1.0),
        'rwkv_w0': uni((DEPTH, D_A), -4.0, 1.0),
        'rwkv_w2': nrm((DEPTH, LORA_W, D_A), 0.5 * LORA_W ** -0.5),
        'rwkv_a0': nrm((DEPTH, D_A), 0.1),
        'rwkv_a2': nrm((DEPTH, LORA_A, D_A), 0.5 * LORA_A ** -0.5),
        'rwkv_g2': nrm((DEPTH, LORA_G, D_A), LORA_G ** -0.5),
        'rwkv_k_k': 0.85 + nrm((DEPTH, D_A), 0.05),
        'rwkv_k_a': 1.0 + nrm((DEPTH, D_A), 0.05),
        'rwkv_r_k': nrm((DEPTH, H_A, HEAD_A), 0.1),
        'rwkv_ln_g': gain((DEPTH, D_A)),
        'rwkv_ln_b': nrm((DEPTH, D_A), 0.02),
        'cmlp_ln_g': gain((DEPTH, D_C)),
        'cmlp_ln_b': nrm((DEPTH, D_C), 0.02),
        'cmlp_ws': nrm((DEPTH, G_C, CHUNK, CHUNK), CHUNK ** -0.5),
        'cmlp_bs': 1.0 + nrm((DEPTH, G_C, CHUNK), 0.05),
        'w_out': nrm((DEPTH, D_MIX, D_MODEL), D_MIX ** -0.5),
        'norm_ffn_g': gain((DEPTH, D_MODEL)),
        'peer_wq': nrm((DEPTH, D_MODEL, PEER_HEADS * D_KEY), D_MODEL ** -0.5),
        'peer_subkeys': nrm((DEPTH, 2, N_KEYS, D_HALF), D_HALF ** -0.5),
        'peer_u': nrm((DEPTH, N_EXPERTS, D_MODEL), D_MODEL ** -0.5),
        'peer_v': nrm((DEPTH, N_EXPERTS, D_MODEL), 0.3),
        'norm_ple_g': gain((DEPTH, D_MODEL)),
        'ple_w': nrm((DEPTH, D_PLE, D_MODEL), D_PLE ** -0.5),
        'ple_gate_w': nrm((DEPTH, D_MODEL, D_MODEL), D_MODEL ** -0.5),
        'norm_final_g': gain((D_MODEL,)),
    }

def reference(x_prompt, x_sample, state_wkv, state_shift, p_prompt, p_sample,
              norm_mix_g, w_in, shift_mu, rwkv_w0, rwkv_w2, rwkv_a0, rwkv_a2, rwkv_g2,
              rwkv_k_k, rwkv_k_a, rwkv_r_k, rwkv_ln_g, rwkv_ln_b, cmlp_ln_g, cmlp_ln_b,
              cmlp_ws, cmlp_bs, w_out, norm_ffn_g, peer_wq, peer_subkeys, peer_u, peer_v,
              norm_ple_g, ple_w, ple_gate_w, norm_final_g):
    layer_weights = (norm_mix_g, w_in, shift_mu, rwkv_w0, rwkv_w2, rwkv_a0, rwkv_a2, rwkv_g2,
                     rwkv_k_k, rwkv_k_a, rwkv_r_k, rwkv_ln_g, rwkv_ln_b, cmlp_ln_g, cmlp_ln_b,
                     cmlp_ws, cmlp_bs, w_out, norm_ffn_g, peer_wq, peer_subkeys, peer_u, peer_v,
                     norm_ple_g, ple_w, ple_gate_w)
    B = x_prompt.shape[0]
    hp, hs = x_prompt, x_sample
    wkv_p, shift_p, wkv_s, shift_s, cv_s = [], [], [], [], []
    for i in range(DEPTH):
        lp = tuple(w[i] for w in layer_weights)
        wkv0 = jnp.zeros((B, H_A, HEAD_A, HEAD_A), x_prompt.dtype)
        shift0 = jnp.zeros((B, P_A), x_prompt.dtype)
        hp, wkv_pi, shift_pi, _ = decoder_layer(hp, p_prompt[i], wkv0, shift0, lp)
        hs, wkv_si, shift_si, v_si = decoder_layer(hs, p_sample[i], state_wkv[i], state_shift[i], lp)
        wkv_p.append(wkv_pi)
        shift_p.append(shift_pi)
        wkv_s.append(wkv_si)
        shift_s.append(shift_si)
        cv_s.append(v_si)
    y_prompt = rmsnorm(hp, norm_final_g)
    y_sample = rmsnorm(hs, norm_final_g)
    return (y_prompt, y_sample, jnp.stack(wkv_p), jnp.stack(shift_p),
            jnp.stack(wkv_s), jnp.stack(shift_s), jnp.stack(cv_s))


_drawn_inputs = setup_inputs


def setup_inputs(seed=0):
    import zlib

    import numpy as np

    out = dict(_drawn_inputs(seed))
    spreads = {}
    factors = {'rwkv_ln_g': 4.907,
     'rwkv_ln_b': 5.019,
     'cmlp_ln_g': 27.047,
     'cmlp_ln_b': 25.454,
     'norm_ffn_g': 3.275,
     'norm_ple_g': 200.0,
     'norm_final_g': 19.788}
    for name, (base, spread) in spreads.items():
        noise = np.random.default_rng([zlib.crc32(name.encode()), seed]).standard_normal(out[name].shape)
        drawn = base * np.exp(spread * noise) if base else spread * noise
        out[name] = __import__('jax').numpy.asarray(drawn.astype(out[name].dtype))
    for name, factor in factors.items():
        out[name] = (out[name] * factor).astype(out[name].dtype)
    return out
```

```python
from contextlib import ExitStack
import math

import concourse.bass as bass
from concourse import mybir

F32 = mybir.dt.float32
U32 = mybir.dt.uint32
I32 = mybir.dt.int32
ALU = mybir.AluOpType
ACT = mybir.ActivationFunctionType
AX = mybir.AxisListType

P = 128
D = 1024
KT = D // P
T_PROMPT = 1024
NB = T_PROMPT // P
NS = 8
DA = 512
H = 8
HD = 64
PA = 1792
CH = 64
TOPK = 16
NK = 128
HK = H * TOPK
WC = 256
LEVELS = 6
NU, NV = 8, 4
NI = 4
UNIT = 4
PAIRS = HK // (2 * UNIT)
RMS_EPS, LN_EPS, GN_EPS = 1e-6, 1e-5, 64e-5
NEG = -3.0e38

HALF = lambda g: {
    0: [f"MT{g}"] + [f"TXt{g}{m}" for m in range(LEVELS)] + [f"Y{g}"],
    1: [f"MakT{g}", f"U0{g}"],
    2: [f"aT{g}", f"MrbT{g}", f"U1{g}"],
    3: [f"bT{g}", f"MrkT{g}", f"WT{g}"],
    4: [f"kT{g}"] + [f"X{g}{m}" for m in range(LEVELS)] + [f"SR{g}{q}" for q in range(2)],
    5: [f"rT{g}"] + [f"TX{g}{m}" for m in range(LEVELS - 1)] + [f"dS{g}{q}" for q in range(2)],
}
SETUP_USES = {0: ["s_sk"], 1: ["s_ws0"], 2: ["s_ws1"], 3: ["s_vec"], 4: [], 5: []}
TAIL_USES = {
    0: ["t_xT0", "gate0", "gate2"], 1: ["t_xT1", "gate1", "gate3"], 2: ["ple0"], 3: ["ple1"], 4: ["t_pT"], 5: [],
}
_IN = {b: [f"xT{b}"] + [f"win{c}" for c in range(11) if c % 2 == b] for b in (0, 1)}
_OUT = {b: [f"zT{b}"] + [f"wout{c}" for c in range(4) if c % 2 == b] + [f"x2T{b}"] for b in (0, 1)}
_Q = {2 + b: [f"q{h}" for h in range(H) if h % 2 == b] for b in (0, 1)}
_Q |= {4 + b: [f"sc{h}" for h in range(H) if h % 2 == b] for b in (0, 1)}
FRONT_USES = {
    0: _IN[0] + HALF(0)[0] + HALF(1)[0] + _OUT[0],
    1: _IN[1] + HALF(0)[1] + HALF(1)[1] + _OUT[1],
    2: ["spatial"] + HALF(0)[2] + HALF(1)[2] + _Q[2],
    3: ["loraT", "g_lora"] + HALF(0)[3] + HALF(1)[3] + _Q[3],
    4: ["w_lora", "cum"] + HALF(0)[4] + HALF(1)[4] + _Q[4],
    5: ["a_lora", "pl"] + HALF(0)[5] + HALF(1)[5] + _Q[5],
}
SAMPLE_USES = {
    0: _IN[0] + _OUT[0], 1: _IN[1] + _OUT[1], 2: _Q[2], 3: ["loraT", "g_lora"] + _Q[3],
    4: ["w_lora"] + _Q[4], 5: ["a_lora"] + _Q[5] + ["eT"],
}
W_TAIL = ["ple"] + [f"gate{c}" for c in range(4)]
W_FRONT = [f"win{c}" for c in range(11)] + [f"wout{c}" for c in range(4)] + [f"wq{h}" for h in range(H)]


def uses_before(i, name, setup, tail, front, sample):
    if not isinstance(i, int):
        return (len(front) + len(tail)) * i + (len(setup) - 2 * len(tail) + (tail + front).index(name))
    here = (tail if i >= 2 else []) + (front if i < NB else sample if i == NB else [])
    before = len(setup) + len(front) * min(i, NB) + (len(sample) if i > NB else 0) + len(tail) * max(i - 2, 0)
    return before + here.index(name)


def build(nc, a, outs):
    y_prompt, y_sample, wkv_prompt, shift_prompt, wkv_sample, shift_sample, chunk_v = outs
    flat = lambda ap: ap.rearrange("a b d -> (a b) d")
    x_dram = {"p": flat(a["x_prompt"]), "s": flat(a["x_sample"])}
    ple_dram = {"p": a["p_prompt"][0, 0], "s": a["p_sample"][0].rearrange("b s d -> (b s) d")}
    y_dram = {"p": flat(y_prompt), "s": flat(y_sample)}
    peer_u, peer_v = a["peer_u"][0], a["peer_v"][0]
    scratch = lambda name, shape: nc.dram_tensor(name, shape, F32, kind="Internal").ap()
    proj_s = scratch("proj_s", (1 + T_PROMPT, PA))
    x1_s = scratch("x1_s", (T_PROMPT + NS, D))
    feat_s = scratch("feat_s", (6, NS, DA))
    ysamp_s = scratch("ysamp_s", (NS, DA))
    xn2_s = scratch("xn2_s", (NS, D))

    ctx = ExitStack()
    with ctx:
        sb = lambda name, shape, dt=F32: ctx.enter_context(nc.sbuf_tensor(name, shape, dt))
        sems = {}

        def sig(name):
            if name not in sems:
                sems[name] = ctx.enter_context(nc.semaphore(name))
            return sems[name]

        bank = [ctx.enter_context(nc.psum_tensor(f"bank{k}", [P, 512], F32)) for k in range(6)]
        acc = [ctx.enter_context(nc.psum_tensor(f"peer_acc{k}", [P, 512], F32)) for k in range(2)]

        ident = sb("ident", [P, P])
        m_incl = sb("m_incl", [P, P])
        m_strict = sb("m_strict", [P, P])
        m_causal = sb("m_causal", [P, P])
        m_level = sb("m_level", [P, LEVELS, P])
        chunk_of = sb("chunk_of", [P, 2])
        diag8 = sb("diag8", [P, NS, NS])
        iota_i = sb("iota_i", [P, TOPK], I32)
        iota16 = sb("iota16", [P, TOPK])
        bcast_names = ["rwkv_w0", "rwkv_a0", "rwkv_k_k", "rwkv_k_a", "rwkv_r_k", "rwkv_ln_g", "rwkv_ln_b", "cmlp_ln_g", "cmlp_ln_b"]
        par = {nm: sb("p_" + nm, [P, DA]) for nm in bcast_names}
        w2 = sb("w2", [64, DA])
        a2 = sb("a2", [64, DA])
        g2 = sb("g2", [P, DA])
        wsT = sb("wsT", [P, H, P])
        skT = sb("skT", [P, 2, NK])
        vecs = sb("vecs", [P, 3, KT])
        ws00 = sb("ws00", [NS, H])
        bs00 = sb("bs00", [NS, H])
        wbuf = sb("wbuf", [P, 2, KT * WC])
        uring = sb("uring", [P, NU, D])
        vring = sb("vring", [P, NV, D])
        idx_c = sb("idx_c", [P, NI, UNIT], U32)
        x = sb("x", [P, D])
        xT = sb("xT", [P, KT, P])
        z = sb("z", [P, D])
        uv = sb("uv", [P, D])
        xn2 = sb("xn2", [P, D])
        pa = sb("pa", [P, PA])
        xm = sb("xm", [P, PA])
        feat = sb("feat", [P, 8, DA])
        yv = sb("yv", [P, DA])
        ft = sb("ft", [P, 4, 512])
        ms = sb("ms", [P, 5, 512])
        wT = sb("wT", [64, 512])
        sm = sb("sm", [P, 5, 256])
        loraT = sb("loraT", [P, 3, P])
        ST = sb("ST", [64, H, HD])
        PL = sb("PL", [64, H, 2])
        st = sb("st", [P, 64])
        sv = sb("sv", [P, H, 2, TOPK])
        si = sb("si", [P, H, 2, TOPK], U32)
        sif = sb("sif", [P, H, 2, TOPK])
        cv = sb("cv", [P, HK])
        ci = sb("ci", [P, HK], U32)
        hi = sb("hi", [P, HK], U32)
        e1 = sb("e1", [P, HK])
        e2 = sb("e2", [P, HK])
        gate = sb("gate", [P, HK])
        eidx = sb("eidx", [P, HK], U32)
        tkv = sb("tkv", [P, 256])
        px = sb("px", [P, D])
        pgate = sb("pgate", [P, HK])
        pidx = sb("pidx", [P, HK], U32)
        ph = sb("ph", [P, 2, UNIT])
        pg = sb("pg", [P, 2, UNIT])
        pact = sb("pact", [P, 2, UNIT])
        dg = sb("dg", [P, 2, UNIT, P])

        mu = feat[:, 0:4, :].rearrange("p a n -> p (a n)")[:, 0:PA]
        sc_all = feat[:, 0:4, :].rearrange("p a n -> p (a n)")
        oneh = feat[:, 4:8, :].rearrange("p a n -> p (a n)")
        F_LW, F_A, F_G, F_KK, F_KH, F_PC, F_PI, F_PX = range(8)
        scr = lambda k: ft[:, k, :]
        MT, MakT, MrbT = (pa[:, 512 * k:512 * k + 512] for k in range(3))
        MrkT, TI, TT, XX, CT = (ms[:, k, :] for k in range(5))
        gain = pa[:, 0:D]
        KM, KN, KO = 0, 1, 2
        V0, V1 = F_KK, F_KH

        def settle(eng):
            eng.sem_inc(sig("settled_" + eng_name[id(eng)]), 1)

        eng_name = {}

        def seq(i, b, use):
            return uses_before(i, use, SETUP_USES[b], TAIL_USES[b], FRONT_USES[b], SAMPLE_USES[b])

        def bank_of(i, use):
            for table in (SETUP_USES, TAIL_USES, SAMPLE_USES if isinstance(i, int) and i >= NB else FRONT_USES):
                for b in table:
                    if use in table[b]:
                        return b
            raise KeyError(use)

        def wait_pos(eng, s, v):
            if not isinstance(v, int) or v > 0:
                eng.wait_ge(s, v)

        def count(i, use):
            b = bank_of(i, use)
            return b, (0 if use.startswith("s_") else seq(i, b, use))

        def take(pe, i, use):
            b, n = count(i, use)
            wait_pos(pe, sig(f"bank{b}_read"), n)
            return bank[b]

        def filled(i, use, ins):
            ins.then_inc(sig(f"bank{count(i, use)[0]}_filled"), 1)

        def see(eng, i, use):
            b, n = count(i, use)
            eng.wait_ge(sig(f"bank{b}_filled"), n + 1)
            return bank[b]

        def has_read(i, use, ins):
            ins.then_inc(sig(f"bank{count(i, use)[0]}_read"), 1)

        def after_read(eng, i, use):
            b, n = count(i, use)
            eng.wait_ge(sig(f"bank{b}_read"), n + 1)

        def wseq(i, name):
            if not isinstance(i, int):
                at = (W_TAIL + W_FRONT).index(name) - 2 * len(W_TAIL)
                per = len(W_TAIL) + len(W_FRONT)
                assert per % 2 == 0
                return at % 2, (per // 2) * i + at // 2
            n = uses_before(i, name, [], W_TAIL, W_FRONT, W_FRONT)
            return n % 2, n // 2

        def wchunk(pe, i, name):
            b, n = wseq(i, name)
            pe.wait_ge(sig(f"w{b}_loaded"), 16 * n + 16)
            return wbuf[:, b, :], sig(f"w{b}_used")

        def load_w(sp, i, name):
            b, n = wseq(i, name)
            wait_pos(sp, sig(f"w{b}_used"), n)
            if not isinstance(n, int):
                settle(sp)
            if name == "ple":
                src, dst = a["ple_w"][0].rearrange("(k p) n -> p k n", p=P), wbuf[:, b, :].rearrange("p (k n) -> p k n", k=2)
            else:
                c = int(name.lstrip("abcdefghijklmnopqrstuvwxyz"))
                w = {"win": "w_in", "wout": "w_out", "wq": "peer_wq", "gate": "ple_gate_w"}[name.rstrip("0123456789")]
                src = a[w][0].rearrange("(k p) n -> p k n", p=P)[:, :, c * WC:(c + 1) * WC]
                dst = wbuf[:, b, :].rearrange("p (k n) -> p k n", k=KT)
            sp.dma_start(dst, src).then_inc(sig(f"w{b}_loaded"), 16)

        def rows(i):
            return "s" if isinstance(i, int) and i == NB else "p"

        def tok(i, ap):
            if rows(i) == "s":
                return ap[0:NS, :]
            return ap[i * P:(i + 1) * P, :] if isinstance(i, int) else ap[bass.ds(i * P, P), :]

        def bc(ap, shape, axis):
            return ap.unsqueeze(axis).to_broadcast(shape)

        def drive(eng, front, tail, pair, handoff, peer_sample):
            def iteration(i, has_tail, has_peer):
                handoff(i)
                stages = []
                if has_tail:
                    stages.append(tail(i))
                if not isinstance(i, int) or i <= NB:
                    stages.append(front(i))
                order = (s for gen in stages for s in gen)
                if has_peer:
                    for m in range(PAIRS):
                        pair(i, m)
                        next(order, None)
                for _ in order:
                    pass
            iteration(0, False, False)
            iteration(1, False, True)
            with eng.Fori(2, NB) as i:
                iteration(i, True, True)
            iteration(NB, True, True)
            handoff(NB + 1)
            for _ in tail(NB + 1):
                pass
            peer_sample()
            handoff(NB + 2)
            for _ in tail(NB + 2):
                pass

        def xn_gate(c):
            return feat[:, c // 2, (c % 2) * WC:(c % 2 + 1) * WC]

        block = ctx.enter_context(nc.Block())

        @block.sync
        def _(sp):
            eng_name[id(sp)] = "sp"

            def hold(s, value):
                sp.wait_ge(s, value)
                if not isinstance(value, int):
                    settle(sp)

            s_par = sig("params_loaded")
            sp.dma_start(w2[:, :], a["rwkv_w2"][0]).then_inc(s_par, 16)
            sp.dma_start(a2[:, :], a["rwkv_a2"][0]).then_inc(s_par, 16)
            sp.dma_start(g2[:, :], a["rwkv_g2"][0]).then_inc(s_par, 16)
            sp.dma_start(ws00[:, :], a["cmlp_ws"][0, :, 0, 0:1].rearrange("g a -> a g").partition_broadcast(NS).rearrange("p a g -> p (a g)"),
                         allow_slow_non_contiguous=True).then_inc(s_par, 16)
            sp.dma_start(bs00[:, :], a["cmlp_bs"][0, :, 0:1].rearrange("g a -> a g").partition_broadcast(NS).rearrange("p a g -> p (a g)"),
                         allow_slow_non_contiguous=True).then_inc(s_par, 16)
            sp.dma_start(ft[:, 0:2, 0:P], a["peer_subkeys"][0].rearrange("c n d -> n c d")).then_inc(sig("raw_loaded"), 16)
            sp.dma_start(pa[:, 0:H * P].rearrange("p (g j) -> p g j", g=H), a["cmlp_ws"][0].rearrange("g i j -> i g j")).then_inc(sig("raw_loaded"), 16)
            sp.dma_start(uv[0:KT, 0:P], a["norm_mix_g"][0].rearrange("(k p) -> k p", p=P)).then_inc(sig("raw_loaded"), 16)
            sp.dma_start(uv[0:KT, P:2 * P], a["norm_ple_g"][0].rearrange("(k p) -> k p", p=P)).then_inc(sig("raw_loaded"), 16)
            sp.dma_start(uv[0:KT, 2 * P:3 * P], a["cmlp_bs"][0]).then_inc(sig("raw_loaded"), 16)
            for nm in bcast_names:
                src = a[nm][0].rearrange("h d -> (h d)") if nm == "rwkv_r_k" else a[nm][0]
                sp.dma_start(par[nm][:, :], src.partition_broadcast(P)).then_inc(s_par, 16)
            hold(sig("zero_row"), 1)
            sp.dma_start(proj_s[0:1, :], xm[0:1, :]).then_inc(sig("zero_stored"), 16)

            def front(i):
                n = NS if rows(i) == "s" else P
                load_w(sp, i, "win0")
                load_w(sp, i, "win1")
                sp.dma_start(x[0:n, :], tok(i, x_dram[rows(i)])).then_inc(sig("x_loaded"), 16)
                yield
                for c in range(2, 11):
                    load_w(sp, i, f"win{c}")
                    if c in (5, 8):
                        yield
                load_w(sp, i, "wout0")
                load_w(sp, i, "wout1")
                wait_pos(sp, sig("topk_done"), i)
                sp.dma_start(mu, a["shift_mu"][0].partition_broadcast(P)).then_inc(sig("mu_loaded"), 16)
                if rows(i) == "p":
                    hold(sig("proj_ready"), i + 1)
                    sp.dma_start(proj_s[1 + i * P:1 + (i + 1) * P, :] if isinstance(i, int) else proj_s[bass.ds(i * P + 1, P), :], pa[:, :]).then_inc(sig("proj_stored"), 16)
                    hold(sig("proj_stored"), 16 * i + 16)
                    if isinstance(i, int) and i == 0:
                        hold(sig("zero_stored"), 16)
                    sp.dma_start(xm[:, :], tok(i, proj_s)).then_inc(sig("prev_loaded"), 16)
                else:
                    hold(sig("proj_ready"), i + 1)
                    sp.dma_start(shift_sample[0], pa[0:NS, :]).then_inc(sig("out_stored"), 16)
                    sp.dma_start(xm[0:NS, :], a["state_shift"][0]).then_inc(sig("prev_loaded"), 16)
                    hold(sig("vn_ready"), i + 1)
                    sp.dma_start(chunk_v[0].rearrange("b s d -> (b s) d"), uv[0:NS, DA:D]).then_inc(sig("out_stored"), 16)
                yield
                yield
                if rows(i) == "s":
                    hold(sig("sfeat_ready"), 1)
                    for k, src in enumerate((xm[0:NS, 0:DA], feat[0:NS, F_KH, :], xm[0:NS, 2 * DA:3 * DA], feat[0:NS, F_PC, :], feat[0:NS, F_KK, :], feat[0:NS, F_A, :])):
                        sp.dma_start(feat_s[k], src).then_inc(sig("sfeat_stored"), 16)
                    hold(sig("sfeat_stored"), 96)
                    sp.dma_start(ms[0:64, 0, 0:384].rearrange("p (k d) -> p k d", k=6), feat_s.rearrange("k b (h d) -> (b h) k d", h=H)).then_inc(sig("sfeat_loaded"), 16)
                    for v4 in range(4):
                        if v4:
                            hold(sig("swkv_used"), v4)
                        sp.dma_start(ft[0:64, 0:2, :].rearrange("p a n -> p (a n)"), a["state_wkv"][0, :, :, 16 * v4:16 * v4 + 16, :].rearrange("b h v k -> (b h) (v k)")).then_inc(sig("swkv_loaded"), 16)
                        hold(sig("swkv_new"), v4 + 1)
                        sp.dma_start(wkv_sample[0, :, :, 16 * v4:16 * v4 + 16, :].rearrange("b h v k -> (b h) (v k)"), ft[0:64, 0:2, :].rearrange("p a n -> p (a n)")).then_inc(sig("swkv_stored"), 16)
                        hold(sig("swkv_stored"), 16 * v4 + 16)
                        sp.sem_inc(sig("swkv_used"), 1)
                    sp.dma_start(ysamp_s.rearrange("b (h d) -> (b h) d", h=H), ms[0:64, 1, 0:64]).then_inc(sig("sy_stored"), 16)
                    hold(sig("sy_stored"), 16)
                    sp.dma_start(yv[0:NS, :], ysamp_s).then_inc(sig("sy_loaded"), 16)
                yield
                yield
                yield
                yield
                load_w(sp, i, "wout2")
                load_w(sp, i, "wout3")
                load_w(sp, i, "wq0")
                load_w(sp, i, "wq1")
                hold(sig("gain_free"), i + 1)
                sp.dma_start(gain, a["norm_ffn_g"][0].partition_broadcast(P)).then_inc(sig("gain_loaded"), 16)
                hold(sig("x1_ready"), i + 1)
                sp.dma_start(x1_s[T_PROMPT:T_PROMPT + NS, :] if rows(i) == "s" else tok(i, x1_s), x[0:n, :]).then_inc(sig("x1_stored"), 16)
                yield
                for h in range(2, H):
                    load_w(sp, i, f"wq{h}")
                    if h in (3, 5):
                        yield
                if rows(i) == "s":
                    hold(sig("xn2_ready"), i + 1)
                    sp.dma_start(xn2_s, xn2[0:NS, :]).then_inc(sig("sxn2_stored"), 16)
                hold(sig("x1_stored"), 16 * i + 16)
                hold(sig("x_norm_done"), i + 1)
                yield

            def tail(i):
                j = i - 2
                sample = isinstance(i, int) and j == NB
                n = NS if sample else P
                load_w(sp, i, "ple")
                load_w(sp, i, "gate0")
                src = x1_s[T_PROMPT:T_PROMPT + NS, :] if sample else tok(j, x1_s)
                sp.dma_start(x[0:n, :], src).then_inc(sig("x1_loaded"), 16)
                sp.dma_start(yv[0:n, 0:256], tok(j, ple_dram["s" if sample else "p"])).then_inc(sig("p_loaded"), 16)
                sp.dma_start(gain, a["norm_final_g"].partition_broadcast(P)).then_inc(sig("fgain_loaded"), 16)
                yield
                load_w(sp, i, "gate1")
                load_w(sp, i, "gate2")
                load_w(sp, i, "gate3")
                yield
                hold(sig("y_ready"), j + 1)
                sp.dma_start(tok(NB if sample else j, y_dram["s" if sample else "p"]), x[0:n, :]).then_inc(sig("y_stored"), 16)
                hold(sig("y_stored"), 16 * j + 16)
                yield

            def peer_sample():
                hold(sig("sxn2_stored"), 16)
                for t in range(NS):
                    if t < NV:
                        if t == 0:
                            hold(sig("v_used"), NB * HK)
                    else:
                        hold(sig("sxt_used"), t - NV + 1)
                    sp.dma_start(vring[:, t % NV, :], xn2_s[t].partition_broadcast(P)).then_inc(sig(f"sxt{t % NV}_loaded"), 16)

            drive(sp, front, tail, lambda i, m: None, lambda i: None, peer_sample)
            sp.dma_start(shift_prompt[0], proj_s[T_PROMPT:T_PROMPT + 1, :]).then_inc(sig("out_stored"), 16)
            hold(sig("wkv_rows"), 1)
            sp.dma_start(wkv_prompt[0, 0].rearrange("h v k -> v h k"), ms[0:64, 0, :].rearrange("v (h k) -> v h k", h=H)).then_inc(sig("out_stored"), 16)
            hold(sig("out_stored"), 16 * 4)

        @block.gpsimd
        def _(gp):
            eng_name[id(gp)] = "gp"
            steps = [0]

            def link(ins):
                steps[0] += 1
                ins.then_inc(sig("gp_step"), 1)
                gp.wait_ge(sig("gp_step"), steps[0])

            def select(out, pattern, base, mult, op=ALU.is_ge, fill=0.0):
                link(gp.affine_select(out=out, in_=out, compare_op=op, fill=fill, base=base, pattern=pattern, channel_multiplier=mult))

            link(gp.memset(xm[0:1, :], 0.0))
            gp.sem_inc(sig("zero_row"), 1)
            link(gp.memset(ident[:, :], 0.0))
            select(ident[:, :], [[-1, P]], 0, 1, ALU.not_equal, 1.0)
            link(gp.memset(diag8[:, :, :], 0.0))
            select(diag8[:, :, :], [[1, NS], [-1, NS]], 0, 0, ALU.not_equal, 1.0)
            for m, off in ((m_causal, 0), (m_incl, 0), (m_strict, -1)):
                link(gp.memset(m[:, :], 1.0))
                select(m[:, :], [[1, P]], off, -1)
                if m is not m_causal:
                    select(m[:, CH:P], [[0, CH]], -CH, 1)
            link(gp.memset(chunk_of[:, :], 1.0))
            select(chunk_of[:, 0:1], [[0, 1]], CH - 1, -1)
            select(chunk_of[:, 1:2], [[0, 1]], -CH, 1)
            link(gp.memset(m_level[:, :, :], 0.0))
            for m in range(LEVELS):
                w = 1 << m
                up = m_level[:, m, :].rearrange("p (b u w) -> p b u w", u=2, w=w)[:, :, 1, :]
                nb = P // (2 * w)
                link(gp.memset(up, 1.0))
                select(up, [[-2 * w, nb], [0, w]], 0, 1)
                select(up, [[2 * w, nb], [0, w]], w - 1, -1)
            link(gp.iota(iota_i[:, :], pattern=[[1, TOPK]], base=0, channel_multiplier=0))
            gp.sem_inc(sig("consts_ready"), 1)

            def pair(i, m):
                for u in range(2):
                    k0 = (2 * m + u) * UNIT
                    g0 = (i - 1) * HK + k0
                    if k0 == 0:
                        gp.wait_ge(sig("handed"), i)
                        settle(gp)
                        copy_idx(i, 0)
                        gather_u(i, 0)
                    if k0 + UNIT < HK:
                        copy_idx(i, k0 + UNIT)
                        gather_u(i, k0 + UNIT)
                    for j in range(UNIT):
                        wait_pos(gp, sig("v_used"), g0 + j - NV + 1)
                        settle(gp)
                        gp.indirect_dma_start(vring[:, (k0 + j) % NV, :], None, peer_v, bass.IndirectOffsetOnAxis(ap=idx_c[:, (k0 // UNIT) % NI, j:j + 1], axis=0)).then_inc(sig(f"v{(k0 + j) % NV}_full"), 16)

            def copy_idx(i, k0):
                g0 = (i - 1) * HK + k0
                if not isinstance(i, int) or i > 1 or k0 >= NI * UNIT:
                    gp.wait_ge(sig("u_used"), g0 - (NI - 1) * UNIT)
                    gp.wait_ge(sig("v_used"), g0 - (NI - 1) * UNIT)
                settle(gp)
                gp.tensor_copy(idx_c[:, (k0 // UNIT) % NI, :], pidx[:, k0:k0 + UNIT]).then_inc(sig("idx_copied"), 1)
                gp.wait_ge(sig("idx_copied"), (i - 1) * (HK // UNIT) + k0 // UNIT + 1)
                settle(gp)

            def gather_u(i, k0):
                g0 = (i - 1) * HK + k0
                for j in range(UNIT):
                    wait_pos(gp, sig("u_used"), g0 + j - NU + 1)
                    settle(gp)
                    s = (k0 + j) % NU
                    gp.indirect_dma_start(uring[:, s, :], None, peer_u, bass.IndirectOffsetOnAxis(ap=idx_c[:, (k0 // UNIT) % NI, j:j + 1], axis=0)).then_inc(sig(f"u{s}_full"), 16)

            def peer_sample():
                gp.wait_ge(sig("handed"), NB + 1)
                for t in range(NS):
                    gp.indirect_dma_start(uring[:, t, :], None, peer_u, bass.IndirectOffsetOnAxis(ap=pidx[:, t:t + 1], axis=0)).then_inc(sig(f"u{t}_full"), 16)
                for t in range(NS):
                    if t < NV:
                        gp.wait_ge(sig("sxt_used"), NS - NV + t + 1)
                    else:
                        gp.wait_ge(sig("v_used"), NB * HK + t - NV + 1)
                    gp.indirect_dma_start(vring[:, t % NV, :], None, peer_v, bass.IndirectOffsetOnAxis(ap=pidx[:, t:t + 1], axis=0)).then_inc(sig(f"v{t % NV}_full"), 16)

            def nothing(i):
                return
                yield

            drive(gp, nothing, nothing, pair, lambda i: None, peer_sample)

        @block.tensor
        def _(pe):
            eng_name[id(pe)] = "pe"
            mm = nc.tensor.matmul

            def turn(out, in_):
                n = in_.shape[0]
                return nc.tensor.transpose(out, in_, ident[0:n, 0:n])

            pe.wait_ge(sig("consts_ready"), 1)
            pe.wait_ge(sig("raw_loaded"), 16 * 5)
            for c in range(2):
                last = turn(bank[0][:, c * P:(c + 1) * P], ft[:, c, 0:P])
            filled(0, "s_sk", last)
            for g in range(H):
                last = turn(bank[1 + g // 4][:, (g % 4) * P:(g % 4 + 1) * P], pa[:, g * P:(g + 1) * P])
                if g % 4 == 3:
                    filled(0, f"s_ws{g // 4}", last)
            for k in range(3):
                last = turn(bank[3][:, k * KT:(k + 1) * KT], uv[0:KT, k * P:(k + 1) * P])
            filled(0, "s_vec", last)
            pe.wait_ge(sig("params_loaded"), 16 * (5 + len(bcast_names)))

            def turn_rows(i, use, src, n):
                for half in range(2):
                    b = take(pe, i, f"{use}{half}")
                    settle(pe)
                    for k in range(4):
                        last = turn(b[:, k * n:(k + 1) * n], src[0:n, (4 * half + k) * P:(4 * half + k + 1) * P])
                    filled(i, f"{use}{half}", last)

            def stream(i, names, n):
                for name in names:
                    w, used = wchunk(pe, i, name)
                    w = w.rearrange("p (k n) -> p k n", k=KT)
                    b = take(pe, i, name)
                    settle(pe)
                    for k in range(KT):
                        last = mm(b[0:n, 0:WC], xT[:, k, 0:n], w[:, k, :], start=(k == 0), stop=(k == KT - 1))
                    filled(i, name, last)
                    pe.wait_ge(sig(f"bank{bank_of(i, name)}_filled"), count(i, name)[1] + 1)
                    pe.sem_inc(used, 1)

            def heads4(i, use, fn, g):
                b = take(pe, i, use)
                settle(pe)
                for h in range(4):
                    last = fn(b, h, 4 * g + h)
                filled(i, use, last)

            def front(i):
                n = NS if rows(i) == "s" else P
                prompt = rows(i) == "p"
                pe.wait_ge(sig("xn_ready"), i + 1)
                turn_rows(i, "xT", z, n)
                yield
                after_read(pe, i, "xT0")
                after_read(pe, i, "xT1")
                stream(i, [f"win{c}" for c in range(0, 4)], n)
                yield
                stream(i, [f"win{c}" for c in range(4, 7)], n)
                yield
                stream(i, [f"win{c}" for c in range(7, 11)], n)
                yield
                if prompt:
                    pe.wait_ge(sig("vn_ready"), i + 1)
                    b = take(pe, i, "spatial")
                    settle(pe)
                    for g in range(H):
                        last = mm(b[:, g * HD:(g + 1) * HD], wsT[:, g, :], uv[:, DA + g * HD:DA + (g + 1) * HD], start=True, stop=True)
                    filled(i, "spatial", last)
                pe.wait_ge(sig("lora_in"), i + 1)
                b = take(pe, i, "loraT")
                settle(pe)
                turn(b[0:64, 0:n], xm[0:n, 3 * DA:3 * DA + 64])
                turn(b[0:64, P:P + n], xm[0:n, 3 * DA + 64:3 * DA + 128])
                last = turn(b[:, 2 * P:2 * P + n], xm[0:n, 3 * DA + 128:PA])
                filled(i, "loraT", last)
                after_read(pe, i, "loraT")
                for use, w, k, rank in (("w_lora", w2, 0, 64), ("a_lora", a2, 1, 64), ("g_lora", g2, 2, P)):
                    b = take(pe, i, use)
                    settle(pe)
                    filled(i, use, mm(b[0:n, :], loraT[0:rank, k, 0:n], w[:, :], start=True, stop=True))
                yield
                if prompt:
                    pe.wait_ge(sig("lw_ready"), i + 1)
                    b = take(pe, i, "cum")
                    settle(pe)
                    filled(i, "cum", mm(b[:, :], m_incl[:, :], feat[:, F_LW, :], start=True, stop=True))
                    b = take(pe, i, "pl")
                    settle(pe)
                    for h in range(H):
                        last = mm(b[0:64, 2 * h:2 * h + 2], feat[:, F_LW, h * HD:(h + 1) * HD], chunk_of[:, :], start=True, stop=True)
                    filled(i, "pl", last)
                    pe.wait_ge(sig("hats_ready"), i + 1)
                for g in range(2):
                    if prompt:
                        half(i, g)
                    yield
                pe.wait_ge(sig("z_ready"), i + 1)
                turn_rows(i, "zT", z, n)
                yield
                after_read(pe, i, "zT0")
                after_read(pe, i, "zT1")
                stream(i, [f"wout{c}" for c in range(4)], n)
                yield
                pe.wait_ge(sig("xn2_ready"), i + 1)
                turn_rows(i, "x2T", xn2, n)
                after_read(pe, i, "x2T0")
                after_read(pe, i, "x2T1")
                for h in range(H):
                    w, used = wchunk(pe, i, f"wq{h}")
                    w = w.rearrange("p (k n) -> p k n", k=KT)
                    b = take(pe, i, f"q{h}")
                    settle(pe)
                    for c in range(2):
                        for k in range(KT):
                            last = mm(b[:, c * P:c * P + n], w[:, k, c * P:(c + 1) * P], xT[:, k, 0:n], start=(k == 0), stop=(k == KT - 1))
                    filled(i, f"q{h}", last)
                    if h:
                        keys(i, h - 1, n)
                    pe.wait_ge(sig(f"bank{bank_of(i, f'q{h}')}_filled"), count(i, f"q{h}")[1] + 1)
                    pe.sem_inc(used, 1)
                    if h in (2, 4):
                        yield
                keys(i, H - 1, n)
                if not prompt:
                    pe.wait_ge(sig("topk_done"), i + 1)
                    b = take(pe, i, "eT")
                    turn(b[:, 0:NS], e1[0:NS, :])
                    filled(i, "eT", turn(b[:, NS:2 * NS], gate[0:NS, :]))
                yield

            def keys(i, h, n):
                after_read(pe, i, f"q{h}")
                b = take(pe, i, f"sc{h}")
                settle(pe)
                for c in range(2):
                    last = mm(b[0:n, c * NK:(c + 1) * NK], XX_q(h)[:, c, 0:n], skT[:, c, :], start=True, stop=True)
                filled(i, f"sc{h}", last)

            def half(i, g):
                hd = lambda ap, h: ap[:, h * P:(h + 1) * P]
                hv = lambda ap, h: ap[:, h * HD:(h + 1) * HD]
                for kind, src in (("aT", F_PX), ("bT", F_A), ("kT", F_PI), ("rT", F_PC)):
                    heads4(i, f"{kind}{g}", lambda b, h, hh: turn(b[0:64, h * P:(h + 1) * P], hv(feat[:, src, :], hh)), g)
                A, B, K, R = (ft[0:64, k, :] for k in range(4))
                for nm in ("aT", "bT", "kT", "rT"):
                    after_read(pe, i, f"{nm}{g}")
                for use, l, r in (("MT", B, A), ("MakT", K, A), ("MrbT", B, R), ("MrkT", K, R)):
                    heads4(i, f"{use}{g}", lambda b, h, hh: mm(hd(b, h), hd(l, h), hd(r, h), start=True, stop=True), g)
                for m in range(LEVELS):
                    pe.wait_ge(sig("CT_ready"), (2 * i + g) * LEVELS + m + 1)
                    heads4(i, f"X{g}{m}", lambda b, h, hh: mm(hd(b, h), hd(CT, h), hd(TI, h), start=True, stop=True), g)
                    after_read(pe, i, f"X{g}{m}")
                    if m < LEVELS - 1:
                        heads4(i, f"TX{g}{m}", lambda b, h, hh: mm(hd(b, h), hd(TT, h), hd(XX, h), start=True, stop=True), g)
                    heads4(i, f"TXt{g}{m}", lambda b, h, hh: mm(hd(b, h), hd(XX, h), hd(TT, h), start=True, stop=True), g)
                v = xm[:, 2 * DA:3 * DA]
                after_read(pe, i, f"MakT{g}")
                heads4(i, f"U0{g}", lambda b, h, hh: mm(hv(b, h), hd(MakT, h), hv(v, hh), start=True, stop=True), g)
                after_read(pe, i, f"U0{g}")
                after_read(pe, i, f"TXt{g}{LEVELS - 1}")
                heads4(i, f"U1{g}", lambda b, h, hh: mm(hv(b, h), hd(TT, h), hv(sm[:, 0, :], h), start=True, stop=True), g)
                heads4(i, f"WT{g}", lambda b, h, hh: mm(hd(b, h)[0:64, :], hv(feat[:, F_PX, :], hh), hd(TT, h), start=True, stop=True), g)
                after_read(pe, i, f"WT{g}")
                after_read(pe, i, f"MrkT{g}")
                pe.wait_ge(sig("v01_ready"), i + 1)
                for q in range(2):
                    pe.wait_ge(sig("ST_ready"), (2 * i + g) * 2 + q + 1)
                    b = take(pe, i, f"SR{g}{q}")
                    settle(pe)
                    for h in range(4):
                        mm(hv(b, h), hd(wT, h), ST[:, 4 * g + h, :], start=True, stop=True)
                    for h in range(4):
                        last = mm(hv(b, 4 + h), hd(R, h), ST[:, 4 * g + h, :], start=True, stop=True)
                    filled(i, f"SR{g}{q}", last)
                    after_read(pe, i, f"SR{g}{q}")
                    b = take(pe, i, f"dS{g}{q}")
                    settle(pe)
                    for h in range(4):
                        hh = 4 * g + h
                        mm(hv(b, h)[0:64, :], hv(feat[:, F_A, :], hh), hv(sm[:, 2 + q, :], h), start=True, stop=False)
                        last = mm(hv(b, h)[0:64, :], hv(feat[:, F_PI, :], hh), hv(feat[:, V0 if q == 0 else V1, :], hh), start=False, stop=True)
                    filled(i, f"dS{g}{q}", last)
                b = take(pe, i, f"Y{g}")
                settle(pe)
                for h in range(4):
                    hh = 4 * g + h
                    mm(hv(b, h), hd(MrbT, h), hv(sm[:, 2, :], h), start=True, stop=False)
                    mm(hv(b, h), hd(MrbT, h), hv(sm[:, 3, :], h), start=False, stop=False)
                    last = mm(hv(b, h), hd(MrkT, h), hv(v, hh), start=False, stop=True)
                filled(i, f"Y{g}", last)

            def tail(i):
                j = i - 2
                n = NS if isinstance(i, int) and j == NB else P
                pe.wait_ge(sig("p_loaded"), 16 * j + 16)
                b = take(pe, i, "t_pT")
                settle(pe)
                turn(b[:, 0:n], yv[0:n, 0:P])
                filled(i, "t_pT", turn(b[:, P:P + n], yv[0:n, P:2 * P]))
                after_read(pe, i, "t_pT")
                w, used = wchunk(pe, i, "ple")
                w = w.rearrange("p (k n) -> p k n", k=2)
                for c in range(2):
                    b = take(pe, i, f"ple{c}")
                    settle(pe)
                    for k in range(2):
                        last = mm(b[0:n, :], loraT[:, k, 0:n], w[:, k, c * 512:(c + 1) * 512], start=(k == 0), stop=(k == 1))
                    filled(i, f"ple{c}", last)
                pe.wait_ge(sig("bank3_filled"), count(i, "ple1")[1] + 1)
                pe.sem_inc(used, 1)
                pe.wait_ge(sig("t_xn_ready"), j + 1)
                turn_rows(i, "t_xT", z, n)
                yield
                after_read(pe, i, "t_xT0")
                after_read(pe, i, "t_xT1")
                stream(i, [f"gate{c}" for c in range(4)], n)
                yield
                yield

            def pair(i, m):
                for u in range(2):
                    k0 = (2 * m + u) * UNIT
                    g0 = (i - 1) * HK + k0
                    pe.wait_ge(sig("diag_ready"), (i - 1) * (HK // UNIT) + k0 // UNIT + 1)
                    if k0 == 0:
                        wait_pos(pe, sig("acc_read"), i - 1)
                        settle(pe)
                    for j in range(UNIT):
                        s = (k0 + j) % NV
                        pe.wait_ge(sig(f"v{s}_full"), 16 * ((i - 1) * (HK // NV) + (k0 + j) // NV + 1))
                        for c in range(2):
                            last = mm(acc[c][:, :], dg[:, u, j, :], vring[:, s, c * 512:(c + 1) * 512], start=(k0 + j == 0), stop=(k0 + j == HK - 1))
                        last.then_inc(sig("v_used"), 1)

            def peer_sample():
                pe.wait_ge(sig("acc_read"), NB)
                for t in range(NS):
                    if t % UNIT == 0:
                        pe.wait_ge(sig("diag_ready"), NB * (HK // UNIT) + t // UNIT + 1)
                    pe.wait_ge(sig(f"v{t % NV}_full"), 16 * (NB * (HK // NV) + t // NV + 1))
                    for c in range(2):
                        last = mm(acc[c][0:NS, :], dg[:, t // UNIT, t % UNIT, 0:NS], vring[:, t % NV, c * 512:(c + 1) * 512], start=(t == 0), stop=(t == NS - 1))
                    last.then_inc(sig("v_used"), 1)

            def qbuf(h):
                return xm[:, (h % 2) * 256:(h % 2) * 256 + 256].rearrange("p (c t) -> p c t", c=2)
            XX_q = qbuf
            drive(pe, front, tail, pair, lambda i: None, peer_sample)
            pe.wait_ge(sig("ST_ready"), NB * 4 + 1)
            pe.wait_ge(sig("bank1_read"), count(NB + 2, "gate3")[1] + 1)
            for h in range(H):
                last = turn(bank[1][0:64, h * HD:(h + 1) * HD], ST[:, h, :])
            last.then_inc(sig("wkv_turned"), 1)

        @block.scalar
        def _(act):
            eng_name[id(act)] = "act"
            steps = [0]

            def fn(out, in_, f, **kw):
                return nc.scalar.activation(out, in_, f, **kw)

            def link(ins):
                steps[0] += 1
                ins.then_inc(sig("act_step"), 1)
                act.wait_ge(sig("act_step"), steps[0])

            def restart():
                if steps[0]:
                    act.wait_ge(sig("act_step"), steps[0])
                    settle(act)
                    act.sem_clear(sig("act_step"))
                steps[0] = 0

            def evac(i, use, dst, cols, parts=P, f=ACT.Copy, **kw):
                b = see(act, i, use)
                has_read(i, use, fn(dst, b[0:parts, 0:cols], f, **kw))

            def sqrt_of(i, name, src, dst, eps_done=True):
                act.wait_ge(sig(name + "_var"), i)
                fn(dst, src, ACT.Sqrt).then_inc(sig(name + "_root"), 1)

            def front(i):
                n = NS if rows(i) == "s" else P
                prompt = rows(i) == "p"
                act.wait_ge(sig("x_loaded"), 16 * i + 16)
                fn(z[0:n, :], x[0:n, :], ACT.Square, accum_out=st[0:n, 0:1]).then_inc(sig("n1_ss"), 1)
                sqrt_of(i + 1, "n1", st[0:n, 1:2], st[0:n, 2:3])
                yield
                for c in range(11):
                    if c == 0:
                        wait_pos(act, sig("gain_used"), i)
                        if not isinstance(i, int) or i >= 2:
                            act.wait_ge(sig("y_ready"), i - 1)
                    if c < 7:
                        evac(i, f"win{c}", pa[0:n, c * WC:(c + 1) * WC], WC, n)
                    else:
                        evac(i, f"win{c}", uv[0:n, (c - 7) * WC:(c - 6) * WC], WC, n, ACT.Gelu)
                    if c == 6:
                        act.wait_ge(sig("bank0_read"), count(i, "win6")[1] + 1)
                        act.wait_ge(sig("bank1_read"), count(i, "win5")[1] + 1)
                        act.sem_inc(sig("proj_ready"), 1)
                    if c in (3, 6):
                        yield
                act.wait_ge(sig("bank0_read"), count(i, "win10")[1] + 1)
                act.wait_ge(sig("bank1_read"), count(i, "win9")[1] + 1)
                act.sem_inc(sig("uv_ready"), 1)
                sqrt_of(i + 1, "ln", st[0:n, 16:24], st[0:n, 24:32])
                yield
                act.wait_ge(sig("xm_ready"), i + 1)
                link(fn(xm[0:n, 3 * DA:3 * DA + 64], xm[0:n, 3 * DA:3 * DA + 64], ACT.Tanh))
                fn(xm[0:n, 3 * DA + 128:PA], xm[0:n, 3 * DA + 128:PA], ACT.Sigmoid).then_inc(sig("lora_in"), 1)
                b = see(act, i, "loraT")
                link(fn(loraT[0:64, 0:2, 0:n], b[0:64, 0:2 * P].rearrange("p (k t) -> p k t", k=2)[:, :, 0:n], ACT.Copy))
                has_read(i, "loraT", fn(loraT[:, 2, 0:n], b[:, 2 * P:2 * P + n], ACT.Copy))
                act.wait_ge(sig("wz_ready"), i + 1)
                fn(feat[0:n, F_LW, :], feat[0:n, F_LW, :], ACT.Sigmoid).then_inc(sig("w_sig"), 1)
                act.wait_ge(sig("az_ready"), i + 1)
                fn(feat[0:n, F_A, :], feat[0:n, F_A, :], ACT.Sigmoid).then_inc(sig("a_sig"), 1)
                evac(i, "g_lora", feat[0:n, F_G, :], DA, n)
                sqrt_of(i + 1, "kk", st[0:n, 32:40], st[0:n, 40:48])
                yield
                if prompt:
                    act.wait_ge(sig("cex_ready"), i + 1)
                    b = see(act, i, "cum")
                    link(fn(feat[:, F_PC, :], b[:, :], ACT.Exp))
                    has_read(i, "cum", fn(feat[:, F_PI, :], b[:, :], ACT.Exp, scale=-1.0))
                    link(fn(feat[:, F_PX, :], feat[:, F_PX, :], ACT.Exp))
                    b = see(act, i, "pl")
                    has_read(i, "pl", fn(PL[:, :, :].rearrange("p h q -> p (h q)"), b[0:64, 0:2 * H], ACT.Exp))
                    act.wait_ge(sig("bank4_read"), count(i, "cum")[1] + 1)
                    act.sem_inc(sig("exps_ready"), 1)
                else:
                    act.wait_ge(sig("lw_ready"), i + 1)
                    fn(feat[0:n, F_PC, :], feat[0:n, F_LW, :], ACT.Exp).then_inc(sig("exps_ready"), 1)
                for g in range(2):
                    if prompt:
                        if g == 0:
                            act.wait_ge(sig("hats_ready"), i + 1)
                        for k, kind in enumerate(("aT", "bT", "kT", "rT")):
                            evac(i, f"{kind}{g}", ft[0:64, k, :], 512, 64)
                        for m in range(LEVELS):
                            evac(i, f"X{g}{m}", XX, 512)
                        evac(i, f"U0{g}", sm[:, 0, :], 256)
                        evac(i, f"U1{g}", sm[:, 1, :], 256)
                        evac(i, f"WT{g}", wT[:, :], 512, 64)
                    yield
                sqrt_of(i + 1, "gn", st[0:n, 16:24], st[0:n, 24:32])
                for k in range(2):
                    b = see(act, i, f"zT{k}")
                    has_read(i, f"zT{k}", fn(xT[:, 4 * k:4 * k + 4, 0:n], b[:, 0:4 * n].rearrange("p (k t) -> p k t", k=4), ACT.Copy))
                yield
                act.wait_ge(sig("x1_ready"), i + 1)
                fn(z[0:n, :], x[0:n, :], ACT.Square, accum_out=st[0:n, 3:4]).then_inc(sig("n2_ss"), 1)
                sqrt_of(i + 1, "n2", st[0:n, 4:5], st[0:n, 5:6])
                yield
                for k in range(2):
                    b = see(act, i, f"x2T{k}")
                    has_read(i, f"x2T{k}", fn(xT[:, 4 * k:4 * k + 4, 0:n], b[:, 0:4 * n].rearrange("p (k t) -> p k t", k=4), ACT.Copy))
                for h in range(H):
                    b = see(act, i, f"q{h}")
                    qd = xm[:, (h % 2) * 256:(h % 2) * 256 + 256].rearrange("p (c t) -> p c t", c=2)
                    has_read(i, f"q{h}", fn(qd[:, :, 0:n], b[:, 0:2 * P].rearrange("p (c t) -> p c t", c=2)[:, :, 0:n], ACT.Copy))
                    if h:
                        evac(i, f"sc{h - 1}", sc_all[0:n, (h - 1) * 256:h * 256], 256, n)
                    if h in (2, 4):
                        yield
                evac(i, f"sc{H - 1}", sc_all[0:n, (H - 1) * 256:H * 256], 256, n)
                act.wait_ge(sig("cv_ready"), i + 1)
                fn(gate[0:n, :], cv[0:n, :], ACT.Exp).then_inc(sig("cv_exp"), 1)
                restart()
                yield

            def tail(i):
                j = i - 2
                n = NS if isinstance(i, int) and j == NB else P
                b = see(act, i, "t_pT")
                has_read(i, "t_pT", fn(loraT[:, 0:2, 0:n], b[:, 0:2 * P].rearrange("p (k t) -> p k t", k=2)[:, :, 0:n], ACT.Copy))
                evac(i, "ple0", uv[0:n, 0:512], 512, n)
                evac(i, "ple1", uv[0:n, 512:1024], 512, n)
                act.wait_ge(sig("x2_ready"), j + 1)
                fn(z[0:n, :], x[0:n, :], ACT.Square, accum_out=st[0:n, 6:7]).then_inc(sig("n3_ss"), 1)
                sqrt_of(j + 1, "n3", st[0:n, 7:8], st[0:n, 8:9])
                yield
                for c in range(4):
                    if c == 0:
                        act.wait_ge(sig("t_xn_ready"), j + 1)
                    evac(i, f"gate{c}", xn_gate(c)[0:n, :], WC, n, ACT.Sigmoid)
                yield
                act.wait_ge(sig("x3_ready"), j + 1)
                fn(z[0:n, :], x[0:n, :], ACT.Square, accum_out=st[0:n, 9:10]).then_inc(sig("n4_ss"), 1)
                sqrt_of(j + 1, "n4", st[0:n, 10:11], st[0:n, 11:12])
                yield

            def pair(i, m):
                for u in range(2):
                    c = (i - 1) * (HK // UNIT) + 2 * m + u
                    act.wait_ge(sig("dots_ready"), c + 1)
                    fn(pg[:, u, :], ph[:, u, :], ACT.Gelu).then_inc(sig("gelu_ready"), 1)

            def peer_sample():
                act.wait_ge(sig("dots_ready"), NB * (HK // UNIT) + 1)
                fn(pg[:, :, :].rearrange("p a b -> p (a b)"), ph[:, :, :].rearrange("p a b -> p (a b)"), ACT.Gelu).then_inc(sig("gelu_ready"), 1)

            drive(act, front, tail, pair, lambda i: None, peer_sample)
            act.wait_ge(sig("wkv_turned"), 1)
            fn(ms[0:64, 0, :], bank[1][0:64, :], ACT.Copy).then_inc(sig("wkv_rows"), 1)

        @block.vector
        def _(ve):
            eng_name[id(ve)] = "ve"
            steps = [0]
            v = nc.vector

            def link(ins):
                steps[0] += 1
                ins.then_inc(sig("ve_step"), 1)
                ve.wait_ge(sig("ve_step"), steps[0])

            def restart():
                if steps[0]:
                    ve.wait_ge(sig("ve_step"), steps[0])
                    settle(ve)
                    ve.sem_clear(sig("ve_step"))
                steps[0] = 0

            tt = v.tensor_tensor
            stt = v.scalar_tensor_tensor

            ve.wait_ge(sig("consts_ready"), 1)
            link(v.tensor_copy(iota16[:, :], iota_i[:, :]))
            b = see(ve, 0, "s_sk")
            has_read(0, "s_sk", v.tensor_copy(skT[:, :, :].rearrange("p c n -> p (c n)"), b[:, 0:2 * NK]))
            for k in range(2):
                b = see(ve, 0, f"s_ws{k}")
                has_read(0, f"s_ws{k}", tt(wsT[:, 4 * k:4 * k + 4, :], b[:, :].rearrange("p (g t) -> p g t", g=4), bc(m_causal[:, :], [P, 4, P], 1), ALU.mult))
            b = see(ve, 0, "s_vec")
            has_read(0, "s_vec", v.tensor_copy(vecs[:, :, :].rearrange("p a k -> p (a k)"), b[:, 0:3 * KT]))
            ve.wait_ge(sig("bank3_read"), 1)
            ve.wait_ge(sig("bank2_read"), 1)
            link(v.memset(ST[:, :, :], 0.0))
            ve.sem_inc(sig("ST_ready"), 1)
            link(v.memset(sm[:, 2:4, :], 0.0))
            restart()

            def finish_norm(name, i, n, col, scale, eps):
                ve.wait_ge(sig(name + "_ss"), i)
                v.tensor_scalar(st[0:n, col + 1:col + 2], st[0:n, col:col + 1], scale, eps, ALU.mult, ALU.add).then_inc(sig(name + "_var"), 1)
                ve.wait_ge(sig(name + "_root"), i)
                link(v.reciprocal(st[0:n, col + 2:col + 3], st[0:n, col + 2:col + 3]))
                return st[0:n, col + 2:col + 3]

            def group_norm(name, i, n, src, dst, g, b, eps):
                s3 = lambda ap: ap.rearrange("p (h d) -> p h d", h=H)
                link(v.tensor_reduce(st[0:n, 48:56], s3(src), AX.X, ALU.add))
                link(v.tensor_scalar(st[0:n, 48:56], st[0:n, 48:56], 1.0 / HD, None, ALU.mult))
                link(tt(s3(dst), s3(src), bc(st[0:n, 48:56], [n, H, HD], 2), ALU.subtract))
                link(tt(scr(0)[0:n, :], dst, dst, ALU.mult))
                link(v.tensor_reduce(st[0:n, 16:24], s3(scr(0)[0:n, :]), AX.X, ALU.add))
                v.tensor_scalar(st[0:n, 16:24], st[0:n, 16:24], 1.0 / HD, eps, ALU.mult, ALU.add).then_inc(sig(name + "_var"), 1)
                ve.wait_ge(sig(name + "_root"), i)
                link(v.reciprocal(st[0:n, 24:32], st[0:n, 24:32]))
                link(tt(s3(dst), s3(dst), bc(st[0:n, 24:32], [n, H, HD], 2), ALU.mult))
                link(tt(dst, dst, par[g][0:n, :], ALU.mult))
                return tt(dst, dst, par[b][0:n, :], ALU.add)

            def front(i):
                n = NS if rows(i) == "s" else P
                prompt = rows(i) == "p"
                f = lambda k: feat[0:n, k, :]
                r, k_, v_ = (xm[0:n, c * DA:(c + 1) * DA] for c in range(3))
                s3 = lambda ap: ap.rearrange("p (h d) -> p h d", h=H)
                rs = finish_norm("n1", i + 1, n, 0, 1.0 / D, RMS_EPS)
                v.tensor_scalar(z[0:n, :], x[0:n, :], rs, None, ALU.mult).then_inc(sig("xn_ready"), 1)
                for k in range(2):
                    b = see(ve, i, f"xT{k}")
                    has_read(i, f"xT{k}", tt(xT[:, 4 * k:4 * k + 4, 0:n], b[:, 0:4 * n].rearrange("p (k t) -> p k t", k=4),
                                             bc(vecs[:, KM, 4 * k:4 * k + 4], [P, 4, n], 2), ALU.mult))
                yield
                yield
                yield
                ve.wait_ge(sig("uv_ready"), i + 1)
                group_norm("ln", i + 1, n, uv[0:n, DA:D], uv[0:n, DA:D], "cmlp_ln_g", "cmlp_ln_b", LN_EPS).then_inc(sig("vn_ready"), 1)
                ve.wait_ge(sig("prev_loaded"), 16 * i + 16)
                ve.wait_ge(sig("mu_loaded"), 16 * i + 16)
                ve.wait_ge(sig("proj_ready"), i + 1)
                link(tt(xm[0:n, :], xm[0:n, :], pa[0:n, :], ALU.subtract))
                link(tt(xm[0:n, :], xm[0:n, :], mu[0:n, :], ALU.mult))
                tt(xm[0:n, :], xm[0:n, :], pa[0:n, :], ALU.add).then_inc(sig("xm_ready"), 1)
                yield
                if prompt:
                    b = see(ve, i, "spatial")
                    has_read(i, "spatial", tt(s3(scr(1)), s3(b[:, :]), bc(vecs[:, KO, :], [P, H, HD], 2), ALU.add))
                    after_read(ve, i, "spatial")
                else:
                    ve.wait_ge(sig("vn_ready"), i + 1)
                    link(tt(s3(scr(1)[0:n, :]), s3(uv[0:n, DA:D]), bc(ws00[:, :], [n, H, HD], 2), ALU.mult))
                    link(tt(s3(scr(1)[0:n, :]), s3(scr(1)[0:n, :]), bc(bs00[:, :], [n, H, HD], 2), ALU.add))
                link(tt(z[0:n, DA:D], uv[0:n, 0:DA], scr(1)[0:n, :], ALU.mult))
                ve.wait_ge(sig("xm_ready"), i + 1)
                link(tt(f(F_KK), k_, par["rwkv_k_k"][0:n, :], ALU.mult))
                link(tt(scr(0)[0:n, :], f(F_KK), f(F_KK), ALU.mult))
                v.tensor_reduce(st[0:n, 32:40], s3(scr(0)[0:n, :]), AX.X, ALU.add).then_inc(sig("kk_var"), 1)
                b = see(ve, i, "w_lora")
                has_read(i, "w_lora", tt(f(F_LW), b[0:n, :], par["rwkv_w0"][0:n, :], ALU.add))
                after_read(ve, i, "w_lora")
                ve.sem_inc(sig("wz_ready"), 1)
                b = see(ve, i, "a_lora")
                has_read(i, "a_lora", tt(f(F_A), b[0:n, :], par["rwkv_a0"][0:n, :], ALU.add))
                after_read(ve, i, "a_lora")
                ve.sem_inc(sig("az_ready"), 1)
                ve.wait_ge(sig("w_sig"), i + 1)
                v.tensor_scalar(f(F_LW), f(F_LW), -math.exp(-0.5), None, ALU.mult).then_inc(sig("lw_ready"), 1)
                ve.wait_ge(sig("a_sig"), i + 1)
                link(stt(scr(0)[0:n, :], f(F_A), -1.0, par["rwkv_k_a"][0:n, :], ALU.add, ALU.mult))
                link(stt(f(F_KH), scr(0)[0:n, :], 1.0, k_, ALU.add, ALU.mult))
                link(tt(scr(0)[0:n, :], r, f(F_KH), ALU.mult))
                link(tt(scr(0)[0:n, :], scr(0)[0:n, :], par["rwkv_r_k"][0:n, :], ALU.mult))
                link(v.tensor_reduce(st[0:n, 56:64], s3(scr(0)[0:n, :]), AX.X, ALU.add))
                ve.wait_ge(sig("kk_root"), i + 1)
                link(v.tensor_scalar(st[0:n, 40:48], st[0:n, 40:48], 1e-12, None, ALU.max))
                link(v.reciprocal(st[0:n, 40:48], st[0:n, 40:48]))
                link(tt(s3(f(F_KK)), s3(f(F_KK)), bc(st[0:n, 40:48], [n, H, HD], 2), ALU.mult))
                link(tt(f(F_A), f(F_A), f(F_KK), ALU.mult))
                yield
                if prompt:
                    ve.wait_ge(sig("lw_ready"), i + 1)
                    b = see(ve, i, "cum")
                    tt(f(F_PX), b[:, :], f(F_LW), ALU.subtract).then_inc(sig("cex_ready"), 1)
                    ve.wait_ge(sig("exps_ready"), i + 1)
                    tt(f(F_A), f(F_A), f(F_PI), ALU.mult)
                    tt(f(F_PC), f(F_PC), r, ALU.mult)
                    link(stt(f(F_PX), f(F_KK), -1.0, f(F_PX), ALU.mult, ALU.mult))
                    tt(f(F_PI), f(F_PI), f(F_KH), ALU.mult).then_inc(sig("hats_ready"), 1)
                    ve.wait_ge(sig("hats_ready"), i + 1)
                    v.memset(feat[64:128, V0, :], 0.0)
                    v.memset(feat[0:64, V1, :], 0.0)
                    v.tensor_copy(feat[0:64, V0, :], xm[0:64, 2 * DA:3 * DA])
                    v.tensor_copy(feat[64:128, V1, :], xm[64:128, 2 * DA:3 * DA]).then_inc(sig("v01_ready"), 1)
                else:
                    ve.wait_ge(sig("exps_ready"), i + 1)
                    ve.sem_inc(sig("sfeat_ready"), 1)
                    sample_step()
                for g in range(2):
                    if prompt:
                        half(i, g)
                    yield
                if not prompt:
                    ve.wait_ge(sig("sy_loaded"), 16)
                link(group_norm("gn", i + 1, n, yv[0:n, :], yv[0:n, :], "rwkv_ln_g", "rwkv_ln_b", GN_EPS))
                link(tt(s3(scr(0)[0:n, :]), s3(v_), bc(st[0:n, 56:64], [n, H, HD], 2), ALU.mult))
                link(tt(yv[0:n, :], yv[0:n, :], scr(0)[0:n, :], ALU.add))
                after_read(ve, i, "g_lora")
                tt(z[0:n, 0:DA], yv[0:n, :], f(F_G), ALU.mult).then_inc(sig("z_ready"), 1)
                ve.sem_inc(sig("gain_free"), 1)
                yield
                for c in range(4):
                    b = see(ve, i, f"wout{c}")
                    has_read(i, f"wout{c}", tt(x[0:n, c * WC:(c + 1) * WC], b[0:n, 0:WC], x[0:n, c * WC:(c + 1) * WC], ALU.add))
                after_read(ve, i, "wout2")
                after_read(ve, i, "wout3")
                ve.sem_inc(sig("x1_ready"), 1)
                rs = finish_norm("n2", i + 1, n, 3, 1.0 / D, RMS_EPS)
                ve.wait_ge(sig("gain_loaded"), 16 * i + 16)
                stt(xn2[0:n, :], x[0:n, :], rs, gain[0:n, :], ALU.mult, ALU.mult).then_inc(sig("xn2_ready"), 1)
                ve.wait_ge(sig("xn2_ready"), i + 1)
                ve.sem_inc(sig("gain_used"), 1)
                ve.sem_inc(sig("x_norm_done"), 1)
                yield
                for h in range(H):
                    after_read(ve, i, f"sc{h}")
                    settle(ve)
                    for c in range(2):
                        s = sc_all[0:n, h * 256 + c * NK:h * 256 + (c + 1) * NK]
                        top16(s, tkv[0:n, 0:NK], sv[0:n, h, c, :], si[0:n, h, c, :])
                    if h in (1, 3):
                        yield
                cand = sc_all[0:n, :].rearrange("p (h a b) -> p h a b", h=H, a=TOPK)
                for h in range(H):
                    ins = tt(cand[:, h], bc(sv[0:n, h, 0, :], [n, TOPK, TOPK], 2), bc(sv[0:n, h, 1, :], [n, TOPK, TOPK], 1), ALU.add)
                link(ins)
                for h in range(H):
                    top16(sc_all[0:n, h * 256:(h + 1) * 256], tkv[0:n, :], cv[0:n, h * TOPK:(h + 1) * TOPK], ci[0:n, h * TOPK:(h + 1) * TOPK])
                c3 = lambda ap: ap.rearrange("p (h k) -> p h k", h=H)
                link(v.tensor_copy(st[0:n, 48:56], c3(cv[0:n, :])[:, :, 0]))
                tt(c3(cv[0:n, :]), c3(cv[0:n, :]), bc(st[0:n, 48:56], [n, H, TOPK], 2), ALU.subtract).then_inc(sig("cv_ready"), 1)
                link(v.tensor_copy(sif[0:n], si[0:n]))
                o4 = oneh[0:n, :].rearrange("p (h j k) -> p h j k", h=H, j=TOPK)
                for half_, dst in ((0, e1), (1, e2)):
                    op, arg = (ALU.logical_shift_right, 4) if half_ == 0 else (ALU.bitwise_and, TOPK - 1)
                    link(v.tensor_scalar(hi[0:n, :], ci[0:n, :], arg, None, op))
                    link(v.tensor_copy(dst[0:n, :], hi[0:n, :]))
                    link(tt(oneh[0:n, :].rearrange("p (j k) -> p j k", k=TOPK), bc(dst[0:n, :], [n, HK, TOPK], 2), bc(iota16[0:n, :], [n, HK, TOPK], 1), ALU.is_equal))
                    for h in range(H):
                        ins = tt(o4[:, h], o4[:, h], bc(sif[0:n, h, half_, :], [n, TOPK, TOPK], 1), ALU.mult)
                    link(ins)
                    link(v.tensor_reduce(dst[0:n, :], oneh[0:n, :].rearrange("p (j k) -> p j k", k=TOPK), AX.X, ALU.add))
                link(stt(e1[0:n, :], e1[0:n, :], float(NK), e2[0:n, :], ALU.mult, ALU.add))
                link(v.tensor_copy(eidx[0:n, :], e1[0:n, :]))
                ve.wait_ge(sig("cv_exp"), i + 1)
                link(v.tensor_reduce(st[0:n, 48:56], c3(gate[0:n, :]), AX.X, ALU.add))
                link(v.reciprocal(st[0:n, 48:56], st[0:n, 48:56]))
                link(tt(c3(gate[0:n, :]), c3(gate[0:n, :]), bc(st[0:n, 48:56], [n, H, TOPK], 2), ALU.mult))
                restart()
                ve.sem_inc(sig("topk_done"), 1)
                yield

            def top16(s, tmp, val, idx):
                link(v.max(val[:, 0:8], s))
                v.max_index(idx[:, 0:8], val[:, 0:8], s)
                link(v.match_replace(tmp, val[:, 0:8], s, NEG))
                link(v.max(val[:, 8:16], tmp))
                link(v.max_index(idx[:, 8:16], val[:, 8:16], tmp))

            def sample_step():
                ve.wait_ge(sig("sfeat_loaded"), 16)
                fr, fk, fv, fw, fkk, fb = (ms[0:64, 0, 64 * k:64 * k + 64] for k in range(6))
                S = ft[0:64, 0:2, :].rearrange("p a n -> p (a n)").rearrange("p (v k) -> p v k", v=16)
                tmp = ft[0:64, 2:4, :].rearrange("p a n -> p (a n)").rearrange("p (v k) -> p v k", v=16)
                sa = ms[0:64, 2, 0:16]
                over_v = lambda ap: bc(ap, [64, 16, HD], 1)
                over_k = lambda ap: bc(ap, [64, 16, HD], 2)
                for q in range(4):
                    vq = fv[:, 16 * q:16 * q + 16]
                    ve.wait_ge(sig("swkv_loaded"), 16 * q + 16)
                    link(tt(tmp, S, over_v(fkk), ALU.mult))
                    link(v.tensor_reduce(sa, tmp, AX.X, ALU.add))
                    link(tt(S, S, over_v(fw), ALU.mult))
                    link(tt(tmp, over_k(sa), over_v(fb), ALU.mult))
                    link(tt(S, S, tmp, ALU.subtract))
                    link(tt(tmp, over_k(vq), over_v(fk), ALU.mult))
                    link(tt(S, S, tmp, ALU.add))
                    link(tt(tmp, S, over_v(fr), ALU.mult))
                    v.tensor_reduce(ms[0:64, 1, 16 * q:16 * q + 16], tmp, AX.X, ALU.add).then_inc(sig("swkv_new"), 1)
                    ve.wait_ge(sig("swkv_new"), q + 1)

            def half(i, g):
                h4 = lambda ap: ap.rearrange("p (h t) -> p h t", h=4)
                mask = lambda m: bc(m, [P, 4, P], 1)
                link(v.tensor_copy(h4(TI), mask(ident[:, :])))
                link(v.tensor_copy(h4(TT), mask(ident[:, :])))
                for use, dst, m in (("MT", MT, m_strict), ("MakT", MakT, m_strict), ("MrbT", MrbT, m_incl), ("MrkT", MrkT, m_incl)):
                    b = see(ve, i, f"{use}{g}")
                    has_read(i, f"{use}{g}", tt(h4(dst), h4(b[:, :]), mask(m[:, :]), ALU.mult))
                after_read(ve, i, f"MT{g}")
                for m in range(LEVELS):
                    tt(h4(CT), h4(MT), mask(m_level[:, m, :]), ALU.mult).then_inc(sig("CT_ready"), 1)
                    if m < LEVELS - 1:
                        b = see(ve, i, f"TX{g}{m}")
                        after = see(ve, i, f"TXt{g}{m}")
                        has_read(i, f"TX{g}{m}", tt(TI, b[:, :], TI, ALU.add))
                    b = see(ve, i, f"TXt{g}{m}")
                    has_read(i, f"TXt{g}{m}", tt(TT, b[:, :], TT, ALU.add))
                    if m < LEVELS - 1:
                        after_read(ve, i, f"TX{g}{m}")
                    after_read(ve, i, f"TXt{g}{m}")
                STg = ST[:, 4 * g:4 * g + 4, :]
                for q in range(2):
                    p0, p1 = CH * q, CH * q + CH
                    if q == 0:
                        after_read(ve, i, f"U1{g}")
                    b = see(ve, i, f"SR{g}{q}")
                    tt(sm[p0:p1, 2 + q, :], b[p0:p1, 0:256], sm[p0:p1, 1, :], ALU.add)
                    has_read(i, f"SR{g}{q}", v.tensor_copy(sm[p0:p1, 4, :], b[p0:p1, 256:512]))
                    b = see(ve, i, f"dS{g}{q}")
                    has_read(i, f"dS{g}{q}", tt(STg, b[0:64, 0:256].rearrange("p (h v) -> p h v", h=4), STg, ALU.add))
                    after_read(ve, i, f"dS{g}{q}")
                    tt(STg, STg, bc(PL[:, 4 * g:4 * g + 4, q], [64, 4, HD], 2), ALU.mult).then_inc(sig("ST_ready"), 1)
                b = see(ve, i, f"Y{g}")
                after_read(ve, i, f"SR{g}1")
                has_read(i, f"Y{g}", tt(yv[:, 256 * g:256 * g + 256], b[:, 0:256], sm[:, 4, :], ALU.add))
                after_read(ve, i, f"Y{g}")

            def handoff(i):
                n = P
                if not isinstance(i, int) or i >= 2:
                    j = i - 2
                    m = NS if isinstance(i, int) and j == NB else P
                    last = NB * HK + NS if isinstance(i, int) and j == NB else (i - 1) * HK
                    ve.wait_ge(sig("x1_loaded"), 16 * j + 16)
                    ve.wait_ge(sig("v_used"), last)
                    for c in range(2):
                        ins = tt(x[0:m, c * 512:(c + 1) * 512], acc[c][0:m, :], x[0:m, c * 512:(c + 1) * 512], ALU.add)
                    link(ins)
                    restart()
                    ve.sem_inc(sig("x2_ready"), 1)
                    ve.sem_inc(sig("acc_read"), 1)
                if isinstance(i, int) and i == 0 or isinstance(i, int) and i > NB + 1:
                    return
                if isinstance(i, int) and i == NB + 1:
                    b = see(ve, NB, "eT")
                    v.tensor_copy(pidx[:, 0:NS], b[:, 0:NS])
                    has_read(NB, "eT", v.tensor_copy(pgate[:, 0:NS], b[:, NS:2 * NS]))
                    after_read(ve, NB, "eT")
                    ve.sem_inc(sig("handed"), 1)
                    return
                v.tensor_copy(pidx[:, :], eidx[:, :])
                v.tensor_copy(pgate[:, :], gate[:, :])
                v.tensor_copy(px[:, :], xn2[:, :]).then_inc(sig("handed"), 1)
                ve.wait_ge(sig("handed"), i)

            def tail(i):
                j = i - 2
                n = NS if isinstance(i, int) and j == NB else P
                rs = finish_norm("n3", j + 1, n, 6, 1.0 / D, RMS_EPS)
                v.tensor_scalar(z[0:n, :], x[0:n, :], rs, None, ALU.mult).then_inc(sig("t_xn_ready"), 1)
                for k in range(2):
                    b = see(ve, i, f"t_xT{k}")
                    has_read(i, f"t_xT{k}", tt(xT[:, 4 * k:4 * k + 4, 0:n], b[:, 0:4 * n].rearrange("p (k t) -> p k t", k=4),
                                               bc(vecs[:, KN, 4 * k:4 * k + 4], [P, 4, n], 2), ALU.mult))
                yield
                after_read(ve, i, "ple1")
                for c in range(4):
                    after_read(ve, i, f"gate{c}")
                    link(tt(xn_gate(c)[0:n, :], xn_gate(c)[0:n, :], uv[0:n, c * WC:(c + 1) * WC], ALU.mult))
                    link(tt(x[0:n, c * WC:(c + 1) * WC], xn_gate(c)[0:n, :], x[0:n, c * WC:(c + 1) * WC], ALU.add))
                ve.sem_inc(sig("x3_ready"), 1)
                yield
                rs = finish_norm("n4", j + 1, n, 9, 1.0 / D, RMS_EPS)
                ve.wait_ge(sig("fgain_loaded"), 16 * j + 16)
                stt(x[0:n, :], x[0:n, :], rs, gain[0:n, :], ALU.mult, ALU.mult).then_inc(sig("y_ready"), 1)
                restart()
                yield

            def pair(i, m):
                for u in range(2):
                    k0 = (2 * m + u) * UNIT
                    c = (i - 1) * (HK // UNIT) + k0 // UNIT
                    for j in range(UNIT):
                        s = (k0 + j) % NU
                        ve.wait_ge(sig(f"u{s}_full"), 16 * ((i - 1) * (HK // NU) + (k0 + j) // NU + 1))
                        v.tensor_tensor_reduce(out=uring[:, s, :], in0=uring[:, s, :], in1=px[:, :], scale=1.0, scalar=0.0,
                                               op0=ALU.mult, op1=ALU.add, accum_out=ph[:, u, j:j + 1]).then_inc(sig("u_used"), 1)
                    ve.wait_ge(sig("u_used"), (i - 1) * HK + k0 + UNIT)
                    ve.sem_inc(sig("dots_ready"), 1)
                    ve.wait_ge(sig("gelu_ready"), c + 1)
                    tt(pact[:, u, :], pg[:, u, :], pgate[:, k0:k0 + UNIT], ALU.mult).then_inc(sig("act_ready"), 1)
                    ve.wait_ge(sig("act_ready"), c + 1)
                    wait_pos(ve, sig("v_used"), (i - 1) * HK + k0 - UNIT)
                    tt(dg[:, u, :, :], bc(ident[:, :], [P, UNIT, P], 1), bc(pact[:, u, :], [P, UNIT, P], 2), ALU.mult).then_inc(sig("diag_ready"), 1)

            def peer_sample():
                for t in range(NS):
                    ve.wait_ge(sig(f"u{t}_full"), 16 * (NB * (HK // NU) + 1))
                    ve.wait_ge(sig(f"sxt{t % NV}_loaded"), 16 * (t // NV + 1))
                    v.tensor_tensor_reduce(out=uring[:, t, :], in0=uring[:, t, :], in1=vring[:, t % NV, :], scale=1.0, scalar=0.0,
                                           op0=ALU.mult, op1=ALU.add, accum_out=ph[:, t // UNIT, t % UNIT:t % UNIT + 1]).then_inc(sig("sxt_used"), 1)
                ve.wait_ge(sig("sxt_used"), NS)
                ve.sem_inc(sig("dots_ready"), 1)
                c = NB * (HK // UNIT)
                ve.wait_ge(sig("gelu_ready"), c + 1)
                tt(pact[:, :, :].rearrange("p a b -> p (a b)"), pg[:, :, :].rearrange("p a b -> p (a b)"), pgate[:, 0:NS], ALU.mult).then_inc(sig("act_ready"), 1)
                ve.wait_ge(sig("act_ready"), c + 1)
                for u in range(2):
                    tt(dg[:, u, :, 0:NS], diag8[:, u * UNIT:(u + 1) * UNIT, :], bc(pact[:, u, :], [P, UNIT, NS], 2), ALU.mult).then_inc(sig("diag_ready"), 1)

            drive(ve, front, tail, pair, handoff, peer_sample)


_INS = ['x_prompt', 'x_sample', 'state_wkv', 'state_shift', 'p_prompt', 'p_sample', 'norm_mix_g', 'w_in', 'shift_mu', 'rwkv_w0',
        'rwkv_w2', 'rwkv_a0', 'rwkv_a2', 'rwkv_g2', 'rwkv_k_k', 'rwkv_k_a', 'rwkv_r_k', 'rwkv_ln_g', 'rwkv_ln_b', 'cmlp_ln_g',
        'cmlp_ln_b', 'cmlp_ws', 'cmlp_bs', 'w_out', 'norm_ffn_g', 'peer_wq', 'peer_subkeys', 'peer_u', 'peer_v', 'norm_ple_g',
        'ple_w', 'ple_gate_w', 'norm_final_g']
_OUTS = [((1, T_PROMPT, D), 'float32'), ((NS, 1, D), 'float32'), ((1, 1, H, HD, HD), 'float32'), ((1, 1, PA), 'float32'),
         ((1, NS, H, HD, HD), 'float32'), ((1, NS, PA), 'float32'), ((1, NS, 1, DA), 'float32')]


def kernel(**inputs):
    import numpy as _np
    import concourse.bacc as _bacc
    from concourse import mybir as _mybir
    from concourse.bass_utils import run_bass_kernel_spmd as _run

    nc = _bacc.Bacc("TRN2", target_bir_lowering=False, num_devices=1)
    arrays, args, outs = {}, {}, []
    for name in _INS:
        arr = _np.ascontiguousarray(inputs[name])
        arrays[f"in_{name}_dram"] = arr
        args[name] = nc.dram_tensor(f"in_{name}_dram", arr.shape, _mybir.dt.from_np(arr.dtype), kind="ExternalInput").ap()
    for i, (shape, dtype) in enumerate(_OUTS):
        outs.append(nc.dram_tensor(f"out_{i}_dram", shape, _mybir.dt.from_np(_np.dtype(dtype)), kind="ExternalOutput").ap())
    build(nc, args, outs)
    r = _run(nc, [arrays], core_ids=[0])
    return tuple(r.results[0][f"out_{i}_dram"] for i in range(len(_OUTS)))
```

```python
from contextlib import ExitStack
import math

import concourse.bass as bass
from concourse import mybir

F32 = mybir.dt.float32
U32 = mybir.dt.uint32
I32 = mybir.dt.int32
ALU = mybir.AluOpType
ACT = mybir.ActivationFunctionType
AX = mybir.AxisListType

P = 128
D = 1024
KT = D // P
T_PROMPT = 1024
NB = T_PROMPT // P
NS = 8
DA = 512
H = 8
HD = 64
PA = 1792
CH = 64
TOPK = 16
NK = 128
HK = H * TOPK
WC = 256
LEVELS = 6
NU, NV = 8, 8
NI = 4
UNIT = 4
UNITS = HK // UNIT
PE_EXPERTS = (0, 2)
VE_EXPERTS = (1, 3)
VPE, VVE = len(PE_EXPERTS), len(VE_EXPERTS)
SPREAD = 122
RMS_EPS, LN_EPS, GN_EPS = 1e-6, 1e-5, 64e-5
NEG = -3.0e38

TAIL_STAGES = ["t_sum", "t_norm", "t_turn", "t_xT"] + [f"gate{c}" for c in range(5)] + ["y_norm", "y"]
NORM = lambda name: [f"{name}_{part}" for part in ("mean", "var", "root", "scale")]
HALF_STAGES = lambda g: (
    [f"h{g}_{part}" for part in ("turn", "products", "TT", "TI")]
    + [f"h{g}_{part}{m}" for m in range(1, LEVELS) for part in ("merge", "update")]
    + [f"h{g}_{part}" for part in ("solve", "SR0", "dS0", "SR1", "dS1", "Y")]
)
FRONT_STAGES = (
    ["norm", "turn", "xT"] + [f"win{c}" for c in range(9)] + ["shift0", "win9", "shift1", "win10", "shift2"]
    + ["lora"] + NORM("ln") + ["lora_add", "kk", "gmlp", "key", "bonus", "kk_norm", "cum", "hats0", "hats1", "masked_v"]
    + HALF_STAGES(0) + HALF_STAGES(1)
    + NORM("gn") + ["gn_bonus", "gn_gate"] + [f"wout{c}" for c in range(5)] + ["norm2", "xn2", "x2T"]
    + [f"{part}{h}" for h in range(H + 2) for part in ("q", "top")]
    + ["cand"] + [f"ctop{h}" for h in range(H)] + ["soft"]
    + [f"digit{half}{part}" for half in range(2) for part in "abc"] + ["expert"]
)

HALF = lambda g: {
    0: [f"MT{g}"] + [f"TXt{g}{m}" for m in range(1, LEVELS)] + [f"Y{g}"],
    1: [f"MakT{g}", f"U0{g}"],
    2: [f"aT{g}", f"MrbT{g}", f"U1{g}"],
    3: [f"bT{g}", f"MrkT{g}", f"WT{g}"],
    4: [f"kT{g}", f"M{g}"] + [f"X{g}{m}" for m in range(1, LEVELS)] + [f"SR{g}{q}" for q in range(2)],
    5: [f"rT{g}"] + [f"TX{g}{m}" for m in range(1, LEVELS - 1)] + [f"dS{g}{q}" for q in range(2)],
}
SETUP_USES = {0: ["s_sk"], 1: ["s_ws0"], 2: ["s_ws1"], 3: ["s_vec"], 4: [], 5: []}
TAIL_USES = {
    0: ["t_xT0", "gate0", "gate2"], 1: ["t_xT1", "gate1", "gate3"], 2: ["ple0"], 3: ["ple1"], 4: ["t_pT"], 5: [],
}
_IN = {b: [f"xT{b}"] + [f"win{c}" for c in range(11) if c % 2 == b] for b in (0, 1)}
_OUT = {b: [f"zT{b}"] + [f"wout{c}" for c in range(4) if c % 2 == b] + [f"x2T{b}"] for b in (0, 1)}
_Q = {2 + b: [f"q{h}" for h in range(H) if h % 2 == b] for b in (0, 1)}
_Q |= {4 + b: [f"sc{h}" for h in range(H) if h % 2 == b] for b in (0, 1)}
FRONT_USES = {
    0: _IN[0] + HALF(0)[0] + HALF(1)[0] + _OUT[0],
    1: _IN[1] + HALF(0)[1] + HALF(1)[1] + _OUT[1],
    2: ["spatial"] + HALF(0)[2] + HALF(1)[2] + _Q[2],
    3: ["loraT", "g_lora"] + HALF(0)[3] + HALF(1)[3] + _Q[3],
    4: ["w_lora", "cum"] + HALF(0)[4] + HALF(1)[4] + _Q[4],
    5: ["a_lora", "pl"] + HALF(0)[5] + HALF(1)[5] + _Q[5],
}
SAMPLE_USES = {
    0: _IN[0] + _OUT[0], 1: _IN[1] + _OUT[1], 2: _Q[2], 3: ["loraT", "g_lora"] + _Q[3],
    4: ["w_lora"] + _Q[4], 5: ["a_lora"] + _Q[5] + ["eT"],
}
W_TAIL = ["ple"] + [f"gate{c}" for c in range(4)]
W_FRONT = [f"win{c}" for c in range(11)] + [f"wout{c}" for c in range(4)] + [f"wq{h}" for h in range(H)]


def uses_before(i, name, setup, tail, front, sample):
    if not isinstance(i, int):
        return (len(front) + len(tail)) * i + (len(setup) - 2 * len(tail) + (tail + front).index(name))
    here = (tail if i >= 2 else []) + (front if i < NB else sample if i == NB else [])
    before = len(setup) + len(front) * min(i, NB) + (len(sample) if i > NB else 0) + len(tail) * max(i - 2, 0)
    return before + here.index(name)


def build(nc, a, outs):
    y_prompt, y_sample, wkv_prompt, shift_prompt, wkv_sample, shift_sample, chunk_v = outs
    flat = lambda ap: ap.rearrange("a b d -> (a b) d")
    x_dram = {"p": flat(a["x_prompt"]), "s": flat(a["x_sample"])}
    ple_dram = {"p": a["p_prompt"][0, 0], "s": a["p_sample"][0].rearrange("b s d -> (b s) d")}
    y_dram = {"p": flat(y_prompt), "s": flat(y_sample)}
    peer_u, peer_v = a["peer_u"][0], a["peer_v"][0]
    scratch = lambda name, shape: nc.dram_tensor(name, shape, F32, kind="Internal").ap()
    proj_s = scratch("proj_s", (1 + T_PROMPT, PA))
    x1_s = scratch("x1_s", (T_PROMPT + NS, D))
    feat_s = scratch("feat_s", (6, NS, DA))
    ysamp_s = scratch("ysamp_s", (NS, DA))
    xn2_s = scratch("xn2_s", (NS, D))

    ctx = ExitStack()
    with ctx:
        sb = lambda name, shape, dt=F32: ctx.enter_context(nc.sbuf_tensor(name, shape, dt))
        sems = {}

        def sig(name):
            if name not in sems:
                sems[name] = ctx.enter_context(nc.semaphore(name))
            return sems[name]

        bank = [ctx.enter_context(nc.psum_tensor(f"bank{k}", [P, 512], F32)) for k in range(6)]
        acc = [ctx.enter_context(nc.psum_tensor(f"peer_acc{k}", [P, 512], F32)) for k in range(2)]

        ident = sb("ident", [P, P])
        m_incl = sb("m_incl", [P, P])
        m_strict = sb("m_strict", [P, P])
        m_causal = sb("m_causal", [P, P])
        m_pairT = sb("m_pairT", [P, P])
        m_level = sb("m_level", [P, LEVELS, P])
        chunk_of = sb("chunk_of", [P, 2])
        diag8 = sb("diag8", [P, NS, NS])
        iota_i = sb("iota_i", [P, TOPK], I32)
        iota16 = sb("iota16", [P, TOPK])
        bcast_names = ["rwkv_w0", "rwkv_a0", "rwkv_k_k", "rwkv_k_a", "rwkv_r_k", "rwkv_ln_g", "rwkv_ln_b", "cmlp_ln_g", "cmlp_ln_b"]
        par = {nm: sb("p_" + nm, [P, DA]) for nm in bcast_names}
        w2 = sb("w2", [64, DA])
        a2 = sb("a2", [64, DA])
        g2 = sb("g2", [P, DA])
        wsT = sb("wsT", [P, H, P])
        skT = sb("skT", [P, 2, NK])
        vecs = sb("vecs", [P, 3, KT])
        ws00 = sb("ws00", [NS, H])
        bs00 = sb("bs00", [NS, H])
        wbuf = sb("wbuf", [P, 2, KT * WC])
        uring = sb("uring", [P, NU, D])
        vring = sb("vring", [P, NV, D])
        idx_c = sb("idx_c", [P, NI, UNIT], U32)
        x = sb("x", [P, D])
        xT = sb("xT", [P, KT, P])
        z = sb("z", [P, D])
        uv = sb("uv", [P, D])
        xn2 = z
        pa = sb("pa", [P, PA])
        xm = sb("xm", [P, PA])
        feat = sb("feat", [P, 8, DA])
        ft = sb("ft", [P, 4, 512])
        ms = sb("ms", [P, 5, 512])
        wT = sb("wT", [64, 512])
        sm = sb("sm", [P, 5, 256])
        loraT = sb("loraT", [P, 3, P])
        ST = sb("ST", [64, H, HD])
        PL = sb("PL", [64, H, 2])
        st = sb("st", [P, 64])
        eps = sb("eps", [P, 3])
        sv = sb("sv", [P, H, 2, TOPK])
        si = sb("si", [P, H, 2, TOPK], U32)
        cv = sb("cv", [P, HK])
        ci = sb("ci", [P, HK], U32)
        hi = sb("hi", [P, HK], U32)
        e1 = sb("e1", [P, HK])
        e2 = sb("e2", [P, HK])
        gate = sb("gate", [P, HK])
        eidx = sb("eidx", [P, 2 * HK], U32)
        px = sb("px", [P, D])
        pgate = sb("pgate", [P, HK])
        sidx = sb("sidx", [P, NS], U32)
        accv = sb("accv", [P, D])
        ph = sb("ph", [P, 2, UNIT])
        pg = sb("pg", [P, 2, UNIT])
        pact = sb("pact", [P, 2, UNIT])
        sdg = sb("sdg", [P, NS, NS])
        dg = sb("dg", [P, 2, VPE, P])

        mu = feat[:, 0:4, :].rearrange("p a n -> p (a n)")[:, 0:PA]
        sc_all = feat[:, 0:4, :].rearrange("p a n -> p (a n)")
        oneh = feat[:, 4:8, :].rearrange("p a n -> p (a n)")
        F_LW, F_A, F_G, F_KK, F_KH, F_PC, F_PI, F_PX = range(8)
        yv = feat[:, F_LW, :]
        ptile = feat[:, 3, 0:2 * P]
        tkv = oneh[:, 0:256]
        sif = sv
        scr = lambda k: ft[:, k, :]
        MT, MakT, MrbT = (pa[:, 512 * k:512 * k + 512] for k in range(3))
        MrkT, TI, TT, XX, CT = (ms[:, k, :] for k in range(5))
        gain = pa[:, 0:D]
        KM, KN, KO = 0, 1, 2
        V0, V1 = F_KK, F_KH

        def settle(eng):
            eng.sem_inc(sig("settled_" + eng_name[id(eng)]), 1)

        eng_name = {}

        def seq(i, b, use):
            return uses_before(i, use, SETUP_USES[b], TAIL_USES[b], FRONT_USES[b], SAMPLE_USES[b])

        def bank_of(i, use):
            for table in (SETUP_USES, TAIL_USES, SAMPLE_USES if isinstance(i, int) and i >= NB else FRONT_USES):
                for b in table:
                    if use in table[b]:
                        return b
            raise KeyError(use)

        def wait_pos(eng, s, v):
            if not isinstance(v, int) or v > 0:
                eng.wait_ge(s, v)

        def count(i, use):
            b = bank_of(i, use)
            return b, (0 if use.startswith("s_") else seq(i, b, use))

        def take(pe, i, use):
            b, n = count(i, use)
            wait_pos(pe, sig(f"bank{b}_read"), n)
            return bank[b]

        def filled(i, use, ins):
            ins.then_inc(sig(f"bank{count(i, use)[0]}_filled"), 1)

        def see(eng, i, use):
            b, n = count(i, use)
            eng.wait_ge(sig(f"bank{b}_filled"), n + 1)
            return bank[b]

        def has_read(i, use, ins):
            ins.then_inc(sig(f"bank{count(i, use)[0]}_read"), 1)

        def after_read(eng, i, use):
            b, n = count(i, use)
            eng.wait_ge(sig(f"bank{b}_read"), n + 1)

        def wseq(i, name):
            if not isinstance(i, int):
                at = (W_TAIL + W_FRONT).index(name) - 2 * len(W_TAIL)
                per = len(W_TAIL) + len(W_FRONT)
                assert per % 2 == 0
                return at % 2, (per // 2) * i + at // 2
            n = uses_before(i, name, [], W_TAIL, W_FRONT, W_FRONT)
            return n % 2, n // 2

        def wchunk(pe, i, name):
            b, n = wseq(i, name)
            pe.wait_ge(sig(f"w{b}_loaded"), 16 * n + 16)
            return wbuf[:, b, :], sig(f"w{b}_used")

        def load_w(sp, i, name):
            b, n = wseq(i, name)
            wait_pos(sp, sig(f"w{b}_used"), n)
            if not isinstance(n, int):
                settle(sp)
            if name == "ple":
                src, dst = a["ple_w"][0].rearrange("(k p) n -> p k n", p=P), wbuf[:, b, :].rearrange("p (k n) -> p k n", k=2)
            else:
                c = int(name.lstrip("abcdefghijklmnopqrstuvwxyz"))
                w = {"win": "w_in", "wout": "w_out", "wq": "peer_wq", "gate": "ple_gate_w"}[name.rstrip("0123456789")]
                src = a[w][0].rearrange("(k p) n -> p k n", p=P)[:, :, c * WC:(c + 1) * WC]
                dst = wbuf[:, b, :].rearrange("p (k n) -> p k n", k=KT)
            sp.dma_start(dst, src).then_inc(sig(f"w{b}_loaded"), 16)

        def rows(i):
            return "s" if isinstance(i, int) and i == NB else "p"

        def tok(i, ap):
            if rows(i) == "s":
                return ap[0:NS, :]
            return ap[i * P:(i + 1) * P, :] if isinstance(i, int) else ap[bass.ds(i * P, P), :]

        def bc(ap, shape, axis):
            return ap.unsqueeze(axis).to_broadcast(shape)

        def play(program, stages):
            at = next(program, None)
            for name in stages:
                while at == name:
                    at = next(program, None)
                yield
            assert at is None, at

        def drive(front, tail, expert, finish, handoff, peer_sample, eng):
            def iteration(i, has_tail, has_peer):
                handoff(i)
                stages = play(tail(i), TAIL_STAGES) if has_tail else iter(())
                both = (s for part in (stages, play(front(i), FRONT_STAGES)) for s in part)
                total = len(FRONT_STAGES) + (len(TAIL_STAGES) if has_tail else 0)
                done = 0
                if has_peer:
                    for k in range(HK):
                        expert(i, k // UNIT, k % UNIT)
                        while done * SPREAD < (k + 1) * total and done < total:
                            next(both)
                            done += 1
                for _ in both:
                    done += 1
                assert done == total
                if has_peer:
                    finish(i)
            iteration(0, False, False)
            iteration(1, False, True)
            with eng.Fori(2, NB) as i:
                iteration(i, True, True)
            iteration(NB, True, True)
            handoff(NB + 1)
            if eng is not nc.tensor:
                peer_sample()
            for _ in play(tail(NB + 1), TAIL_STAGES):
                pass
            if eng is nc.tensor:
                peer_sample()
            for _ in play(tail(NB + 2), TAIL_STAGES):
                pass

        def xn_gate(c):
            return feat[:, c // 2, (c % 2) * WC:(c % 2 + 1) * WC]

        def query(h):
            return xm[:, (h % 2) * 256:(h % 2) * 256 + 256].rearrange("p (c t) -> p c t", c=2)

        block = ctx.enter_context(nc.Block())

        @block.sync
        def _(sp):
            eng_name[id(sp)] = "sp"

            def hold(s, value):
                sp.wait_ge(s, value)
                if not isinstance(value, int):
                    settle(sp)

            s_par = sig("params_loaded")
            sp.dma_start(w2[:, :], a["rwkv_w2"][0]).then_inc(s_par, 16)
            sp.dma_start(a2[:, :], a["rwkv_a2"][0]).then_inc(s_par, 16)
            sp.dma_start(g2[:, :], a["rwkv_g2"][0]).then_inc(s_par, 16)
            sp.dma_start(ws00[:, :], a["cmlp_ws"][0, :, 0, 0:1].rearrange("g a -> a g").partition_broadcast(NS).rearrange("p a g -> p (a g)"),
                         allow_slow_non_contiguous=True).then_inc(s_par, 16)
            sp.dma_start(bs00[:, :], a["cmlp_bs"][0, :, 0:1].rearrange("g a -> a g").partition_broadcast(NS).rearrange("p a g -> p (a g)"),
                         allow_slow_non_contiguous=True).then_inc(s_par, 16)
            sp.dma_start(ft[:, 0:2, 0:P], a["peer_subkeys"][0].rearrange("c n d -> n c d")).then_inc(sig("raw_loaded"), 16)
            sp.dma_start(pa[:, 0:H * P].rearrange("p (g j) -> p g j", g=H), a["cmlp_ws"][0].rearrange("g i j -> i g j")).then_inc(sig("raw_loaded"), 16)
            sp.dma_start(uv[0:KT, 0:P], a["norm_mix_g"][0].rearrange("(k p) -> k p", p=P)).then_inc(sig("raw_loaded"), 16)
            sp.dma_start(uv[0:KT, P:2 * P], a["norm_ple_g"][0].rearrange("(k p) -> k p", p=P)).then_inc(sig("raw_loaded"), 16)
            sp.dma_start(uv[0:KT, 2 * P:3 * P], a["cmlp_bs"][0]).then_inc(sig("raw_loaded"), 16)
            for nm in bcast_names:
                src = a[nm][0].rearrange("h d -> (h d)") if nm == "rwkv_r_k" else a[nm][0]
                sp.dma_start(par[nm][:, :], src.partition_broadcast(P)).then_inc(s_par, 16)
            hold(sig("zero_row"), 1)
            sp.dma_start(proj_s[0:1, :], xm[0:1, :]).then_inc(sig("zero_stored"), 16)

            def front(i):
                n = NS if rows(i) == "s" else P
                if isinstance(i, int) and i < 2:
                    load_w(sp, i, "win0")
                    load_w(sp, i, "win1")
                sp.dma_start(x[0:n, :], tok(i, x_dram[rows(i)])).then_inc(sig("x_loaded"), 16)
                for c in range(2, 9):
                    load_w(sp, i, f"win{c}")
                wait_pos(sp, sig("topk_done"), i)
                sp.dma_start(mu, a["shift_mu"][0].partition_broadcast(P)).then_inc(sig("mu_loaded"), 16)
                hold(sig("proj_ready"), i + 1)
                if rows(i) == "p":
                    sp.dma_start(proj_s[1 + i * P:1 + (i + 1) * P, :] if isinstance(i, int) else proj_s[bass.ds(i * P + 1, P), :], pa[:, :]).then_inc(sig("proj_stored"), 16)
                    load_w(sp, i, "win9")
                    hold(sig("proj_stored"), 16 * i + 16)
                    if isinstance(i, int) and i == 0:
                        hold(sig("zero_stored"), 16)
                    sp.dma_start(xm[:, :], tok(i, proj_s)).then_inc(sig("prev_loaded"), 16)
                else:
                    sp.dma_start(shift_sample[0], pa[0:NS, :]).then_inc(sig("out_stored"), 16)
                    load_w(sp, i, "win9")
                    sp.dma_start(xm[0:NS, :], a["state_shift"][0]).then_inc(sig("prev_loaded"), 16)
                load_w(sp, i, "win10")
                load_w(sp, i, "wout0")
                load_w(sp, i, "wout1")
                if rows(i) == "s":
                    hold(sig("vn_ready"), i + 1)
                    sp.dma_start(chunk_v[0].rearrange("b s d -> (b s) d"), uv[0:NS, DA:D]).then_inc(sig("out_stored"), 16)
                if rows(i) == "s":
                    hold(sig("sfeat_ready"), 1)
                    for k, src in enumerate((xm[0:NS, 0:DA], feat[0:NS, F_KH, :], xm[0:NS, 2 * DA:3 * DA], feat[0:NS, F_PC, :], feat[0:NS, F_KK, :], feat[0:NS, F_A, :])):
                        sp.dma_start(feat_s[k], src).then_inc(sig("sfeat_stored"), 16)
                    hold(sig("sfeat_stored"), 96)
                    sp.dma_start(ms[0:64, 0, 0:384].rearrange("p (k d) -> p k d", k=6), feat_s.rearrange("k b (h d) -> (b h) k d", h=H)).then_inc(sig("sfeat_loaded"), 16)
                    for v4 in range(4):
                        if v4:
                            hold(sig("swkv_used"), v4)
                        sp.dma_start(ft[0:64, 0:2, :].rearrange("p a n -> p (a n)"), a["state_wkv"][0, :, :, 16 * v4:16 * v4 + 16, :].rearrange("b h v k -> (b h) (v k)")).then_inc(sig("swkv_loaded"), 16)
                        hold(sig("swkv_new"), v4 + 1)
                        sp.dma_start(wkv_sample[0, :, :, 16 * v4:16 * v4 + 16, :].rearrange("b h v k -> (b h) (v k)"), ft[0:64, 0:2, :].rearrange("p a n -> p (a n)")).then_inc(sig("swkv_stored"), 16)
                        hold(sig("swkv_stored"), 16 * v4 + 16)
                        sp.sem_inc(sig("swkv_used"), 1)
                    sp.dma_start(ysamp_s.rearrange("b (h d) -> (b h) d", h=H), ms[0:64, 1, 0:64]).then_inc(sig("sy_stored"), 16)
                    hold(sig("sy_stored"), 16)
                    sp.dma_start(yv[0:NS, :], ysamp_s).then_inc(sig("sy_loaded"), 16)
                load_w(sp, i, "wout2")
                load_w(sp, i, "wout3")
                load_w(sp, i, "wq0")
                load_w(sp, i, "wq1")
                hold(sig("gain_free"), i + 1)
                sp.dma_start(gain, a["norm_ffn_g"][0].partition_broadcast(P)).then_inc(sig("gain_loaded"), 16)
                hold(sig("x1_ready"), i + 1)
                sp.dma_start(x1_s[T_PROMPT:T_PROMPT + NS, :] if rows(i) == "s" else tok(i, x1_s), x[0:n, :]).then_inc(sig("x1_stored"), 16)
                for h in range(2, H):
                    load_w(sp, i, f"wq{h}")
                if rows(i) == "s":
                    hold(sig("xn2_ready"), i + 1)
                    sp.dma_start(xn2_s, xn2[0:NS, :]).then_inc(sig("sxn2_stored"), 16)
                hold(sig("x1_stored"), 16 * i + 16)
                hold(sig("x_norm_done"), i + 1)
                yield

            def tail(i):
                j = i - 2
                sample = isinstance(i, int) and j == NB
                n = NS if sample else P
                load_w(sp, i, "ple")
                load_w(sp, i, "gate0")
                src = x1_s[T_PROMPT:T_PROMPT + NS, :] if sample else tok(j, x1_s)
                sp.dma_start(x[0:n, :], src).then_inc(sig("x1_loaded"), 16)
                sp.dma_start(gain, a["norm_final_g"].partition_broadcast(P)).then_inc(sig("fgain_loaded"), 16)
                hold(sig("topk_done"), i if not isinstance(i, int) else min(i, NB + 1))
                sp.dma_start(ptile[0:n, :], tok(NB if sample else j, ple_dram["s" if sample else "p"])).then_inc(sig("p_loaded"), 16)
                load_w(sp, i, "gate1")
                load_w(sp, i, "gate2")
                load_w(sp, i, "gate3")
                if not isinstance(i, int) or i <= NB:
                    load_w(sp, i, "win0")
                    load_w(sp, i, "win1")
                hold(sig("y_ready"), j + 1)
                sp.dma_start(tok(NB if sample else j, y_dram["s" if sample else "p"]), x[0:n, :]).then_inc(sig("y_stored"), 16)
                hold(sig("y_stored"), 16 * j + 16)
                yield

            def peer_sample():
                hold(sig("sxn2_stored"), 16)
                hold(sig("vpe_used"), NB * UNITS * VPE)
                hold(sig("vve_used"), NB * UNITS * VVE)
                for t in range(NS):
                    sp.dma_start(vring[:, t, :], xn2_s[t].partition_broadcast(P)).then_inc(sig(f"sxt{t}_loaded"), 16)

            drive(front, tail, lambda i, n, j: None, lambda i: None, lambda i: None, peer_sample, sp)
            sp.dma_start(shift_prompt[0], proj_s[T_PROMPT:T_PROMPT + 1, :]).then_inc(sig("out_stored"), 16)
            hold(sig("wkv_rows"), 1)
            sp.dma_start(wkv_prompt[0, 0].rearrange("h v k -> v h k"), ms[0:64, 0, :].rearrange("v (h k) -> v h k", h=H)).then_inc(sig("out_stored"), 16)
            hold(sig("out_stored"), 16 * 4)

        @block.gpsimd
        def _(gp):
            eng_name[id(gp)] = "gp"
            steps = [0]

            def link(ins):
                steps[0] += 1
                ins.then_inc(sig("gp_step"), 1)
                gp.wait_ge(sig("gp_step"), steps[0])

            def select(out, pattern, base, mult, op=ALU.is_ge, fill=0.0):
                link(gp.affine_select(out=out, in_=out, compare_op=op, fill=fill, base=base, pattern=pattern, channel_multiplier=mult))

            link(gp.memset(xm[0:1, :], 0.0))
            gp.sem_inc(sig("zero_row"), 1)
            link(gp.memset(ident[:, :], 0.0))
            select(ident[:, :], [[-1, P]], 0, 1, ALU.not_equal, 1.0)
            link(gp.memset(diag8[:, :, :], 0.0))
            select(diag8[:, :, :], [[1, NS], [-1, NS]], 0, 0, ALU.not_equal, 1.0)
            for m, off in ((m_causal, 0), (m_incl, 0), (m_strict, -1)):
                link(gp.memset(m[:, :], 1.0))
                select(m[:, :], [[1, P]], off, -1)
                if m is not m_causal:
                    select(m[:, CH:P], [[0, CH]], -CH, 1)
            link(gp.memset(chunk_of[:, :], 1.0))
            select(chunk_of[:, 0:1], [[0, 1]], CH - 1, -1)
            select(chunk_of[:, 1:2], [[0, 1]], -CH, 1)
            link(gp.memset(m_level[:, :, :], 0.0))
            for m in range(LEVELS):
                w = 1 << m
                up = m_level[:, m, :].rearrange("p (b u w) -> p b u w", u=2, w=w)[:, :, 1, :]
                nb = P // (2 * w)
                link(gp.memset(up, 1.0))
                select(up, [[-2 * w, nb], [0, w]], 0, 1)
                select(up, [[2 * w, nb], [0, w]], w - 1, -1)
            link(gp.memset(m_pairT[:, :], 1.0))
            select(m_pairT[:, :].rearrange("p (b u) -> p b u", u=2)[:, :, 1], [[0, CH]], -1, 0)
            select(m_pairT[:, :], [[-1, P]], -1, 1, ALU.is_equal)
            link(gp.iota(iota_i[:, :], pattern=[[1, TOPK]], base=0, channel_multiplier=0))
            for k, value in enumerate((RMS_EPS, LN_EPS, GN_EPS)):
                link(gp.memset(eps[:, k:k + 1], value))
            gp.sem_inc(sig("consts_ready"), 1)

            def copy_idx(i, n):
                g = (i - 1) * UNITS + n
                if not isinstance(i, int) or i > 1 or n >= NI:
                    gp.wait_ge(sig("u_used"), (g - NI + 1) * UNIT)
                    gp.wait_ge(sig("vpe_used"), (g - NI + 1) * VPE)
                    settle(gp)
                    gp.wait_ge(sig("vve_used"), (g - NI + 1) * VVE)
                    settle(gp)
                at = ((i - 1) % 2) * HK + n * UNIT
                src = eidx[:, at:at + UNIT] if isinstance(i, int) else eidx[:, bass.ds(at, UNIT)]
                gp.tensor_copy(idx_c[:, n % NI, :], src).then_inc(sig("idx_copied"), 1)
                gp.wait_ge(sig("idx_copied"), g + 1)
                settle(gp)

            def gather_u(i, n, j):
                s = n % 2 * UNIT + j
                wait_pos(gp, sig("u_used"), (i - 1) * HK + n * UNIT + j - NU + 1)
                settle(gp)
                gp.indirect_dma_start(uring[:, s, :], None, peer_u, bass.IndirectOffsetOnAxis(ap=idx_c[:, n % NI, j:j + 1], axis=0)).then_inc(sig(f"u{s}_full"), 16)

            def gather_v(i, n, j):
                s = n % 2 * UNIT + j
                before = (i - 1) * UNITS + n - 2
                if j in PE_EXPERTS:
                    wait_pos(gp, sig("vpe_used"), before * VPE + PE_EXPERTS.index(j) + 1)
                else:
                    wait_pos(gp, sig("vve_used"), before * VVE + VE_EXPERTS.index(j) + 1)
                settle(gp)
                gp.indirect_dma_start(vring[:, s, :], None, peer_v, bass.IndirectOffsetOnAxis(ap=idx_c[:, n % NI, j:j + 1], axis=0)).then_inc(sig(f"v{s}_full"), 16)

            def expert(i, n, j):
                if n == 0 and j == 0:
                    gp.wait_ge(sig("topk_done"), i)
                    settle(gp)
                    copy_idx(i, 0)
                    for jj in range(UNIT):
                        gather_u(i, 0, jj)
                if n + 1 < UNITS:
                    if j == 0:
                        copy_idx(i, n + 1)
                    gather_u(i, n + 1, j)
                gather_v(i, n, j)

            def peer_sample():
                gp.wait_ge(sig("handed"), NB + 1)
                for t in range(NS):
                    gp.indirect_dma_start(uring[:, t, :], None, peer_u, bass.IndirectOffsetOnAxis(ap=sidx[:, t:t + 1], axis=0)).then_inc(sig(f"u{t}_full"), 16)
                for t in range(NS):
                    gp.wait_ge(sig("sxt_used"), t + 1)
                    gp.indirect_dma_start(vring[:, t, :], None, peer_v, bass.IndirectOffsetOnAxis(ap=sidx[:, t:t + 1], axis=0)).then_inc(sig(f"v{t}_full"), 16)

            def nothing(i):
                return
                yield

            drive(nothing, nothing, expert, lambda i: None, lambda i: None, peer_sample, gp)

        @block.tensor
        def _(pe):
            eng_name[id(pe)] = "pe"
            mm = nc.tensor.matmul

            def turn(out, in_):
                n = in_.shape[0]
                return nc.tensor.transpose(out, in_, ident[0:n, 0:n])

            pe.wait_ge(sig("consts_ready"), 1)
            pe.wait_ge(sig("raw_loaded"), 16 * 5)
            for c in range(2):
                last = turn(bank[0][:, c * P:(c + 1) * P], ft[:, c, 0:P])
            filled(0, "s_sk", last)
            for g in range(H):
                last = turn(bank[1 + g // 4][:, (g % 4) * P:(g % 4 + 1) * P], pa[:, g * P:(g + 1) * P])
                if g % 4 == 3:
                    filled(0, f"s_ws{g // 4}", last)
            for k in range(3):
                last = turn(bank[3][:, k * KT:(k + 1) * KT], uv[0:KT, k * P:(k + 1) * P])
            filled(0, "s_vec", last)
            pe.wait_ge(sig("params_loaded"), 16 * (5 + len(bcast_names)))

            def turn_rows(i, use, src, n):
                for half in range(2):
                    b = take(pe, i, f"{use}{half}")
                    settle(pe)
                    for k in range(4):
                        last = turn(b[:, k * n:(k + 1) * n], src[0:n, (4 * half + k) * P:(4 * half + k + 1) * P])
                    filled(i, f"{use}{half}", last)

            def stream(i, name, n):
                w, used = wchunk(pe, i, name)
                w = w.rearrange("p (k n) -> p k n", k=KT)
                b = take(pe, i, name)
                settle(pe)
                for k in range(KT):
                    last = mm(b[0:n, 0:WC], xT[:, k, 0:n], w[:, k, :], start=(k == 0), stop=(k == KT - 1))
                filled(i, name, last)
                pe.wait_ge(sig(f"bank{bank_of(i, name)}_filled"), count(i, name)[1] + 1)
                pe.sem_inc(used, 1)

            def heads4(i, use, fn, g):
                b = take(pe, i, use)
                settle(pe)
                for h in range(4):
                    last = fn(b, h, 4 * g + h)
                filled(i, use, last)

            def front(i):
                n = NS if rows(i) == "s" else P
                prompt = rows(i) == "p"
                yield "turn"
                pe.wait_ge(sig("xn_ready"), i + 1)
                turn_rows(i, "xT", z, n)
                for c in range(11):
                    yield f"win{c}"
                    if c == 0:
                        after_read(pe, i, "xT0")
                        after_read(pe, i, "xT1")
                    stream(i, f"win{c}", n)
                yield "lora"
                pe.wait_ge(sig("lora_in"), i + 1)
                b = take(pe, i, "loraT")
                settle(pe)
                turn(b[0:64, 0:n], xm[0:n, 3 * DA:3 * DA + 64])
                turn(b[0:64, P:P + n], xm[0:n, 3 * DA + 64:3 * DA + 128])
                last = turn(b[:, 2 * P:2 * P + n], xm[0:n, 3 * DA + 128:PA])
                filled(i, "loraT", last)
                after_read(pe, i, "loraT")
                for use, w, k, rank in (("w_lora", w2, 0, 64), ("a_lora", a2, 1, 64), ("g_lora", g2, 2, P)):
                    b = take(pe, i, use)
                    settle(pe)
                    filled(i, use, mm(b[0:n, :], loraT[0:rank, k, 0:n], w[:, :], start=True, stop=True))
                if prompt:
                    yield "kk"
                    pe.wait_ge(sig("vn_ready"), i + 1)
                    b = take(pe, i, "spatial")
                    settle(pe)
                    for g in range(H):
                        last = mm(b[:, g * HD:(g + 1) * HD], wsT[:, g, :], uv[:, DA + g * HD:DA + (g + 1) * HD], start=True, stop=True)
                    filled(i, "spatial", last)
                    yield "bonus"
                    pe.wait_ge(sig("lw_ready"), i + 1)
                    b = take(pe, i, "cum")
                    settle(pe)
                    filled(i, "cum", mm(b[:, :], m_incl[:, :], feat[:, F_LW, :], start=True, stop=True))
                    b = take(pe, i, "pl")
                    settle(pe)
                    for h in range(H):
                        last = mm(b[0:64, 2 * h:2 * h + 2], feat[:, F_LW, h * HD:(h + 1) * HD], chunk_of[:, :], start=True, stop=True)
                    filled(i, "pl", last)
                    for g in range(2):
                        yield from half(i, g)
                yield "gn_gate"
                pe.wait_ge(sig("z_ready"), i + 1)
                turn_rows(i, "zT", z, n)
                for c in range(4):
                    yield f"wout{c}"
                    if c == 0:
                        after_read(pe, i, "zT0")
                        after_read(pe, i, "zT1")
                    stream(i, f"wout{c}", n)
                yield "x2T"
                pe.wait_ge(sig("xn2_ready"), i + 1)
                turn_rows(i, "x2T", xn2, n)
                for h in range(H + 1):
                    yield f"q{h}"
                    if h == 0:
                        after_read(pe, i, "x2T0")
                        after_read(pe, i, "x2T1")
                    if h < H:
                        w, used = wchunk(pe, i, f"wq{h}")
                        w = w.rearrange("p (k n) -> p k n", k=KT)
                        b = take(pe, i, f"q{h}")
                        settle(pe)
                        for c in range(2):
                            for k in range(KT):
                                last = mm(b[:, c * P:c * P + n], w[:, k, c * P:(c + 1) * P], xT[:, k, 0:n], start=(k == 0), stop=(k == KT - 1))
                        filled(i, f"q{h}", last)
                        pe.wait_ge(sig(f"bank{bank_of(i, f'q{h}')}_filled"), count(i, f"q{h}")[1] + 1)
                        pe.sem_inc(used, 1)
                    if h:
                        keys(i, h - 1, n)
                if not prompt:
                    yield "expert"
                    pe.wait_ge(sig("topk_done"), i + 1)
                    b = take(pe, i, "eT")
                    turn(b[:, 0:NS], e1[0:NS, :])
                    filled(i, "eT", turn(b[:, NS:2 * NS], gate[0:NS, :]))

            def keys(i, h, n):
                after_read(pe, i, f"q{h}")
                b = take(pe, i, f"sc{h}")
                settle(pe)
                for c in range(2):
                    last = mm(b[0:n, c * NK:(c + 1) * NK], query(h)[:, c, 0:n], skT[:, c, :], start=True, stop=True)
                filled(i, f"sc{h}", last)

            def half(i, g):
                hd = lambda ap, h: ap[:, h * P:(h + 1) * P]
                hv = lambda ap, h: ap[:, h * HD:(h + 1) * HD]
                yield f"h{g}_turn"
                pe.wait_ge(sig("hats_ready"), i + 1)
                for kind, src in (("aT", F_PX), ("bT", F_A), ("kT", F_PI), ("rT", F_PC)):
                    heads4(i, f"{kind}{g}", lambda b, h, hh: turn(b[0:64, h * P:(h + 1) * P], hv(feat[:, src, :], hh)), g)
                A, B, K, R = (ft[0:64, k, :] for k in range(4))
                product = lambda use, l, r: heads4(i, f"{use}{g}", lambda b, h, hh: mm(hd(b, h), hd(l, h), hd(r, h), start=True, stop=True), g)
                yield f"h{g}_products"
                for nm in ("aT", "bT", "kT", "rT"):
                    after_read(pe, i, f"{nm}{g}")
                product("MT", B, A)
                product("M", A, B)
                yield f"h{g}_TT"
                product("MakT", K, A)
                product("MrbT", B, R)
                yield f"h{g}_TI"
                product("MrkT", K, R)
                v = xm[:, 2 * DA:3 * DA]
                for m in range(1, LEVELS):
                    yield f"h{g}_merge{m}"
                    pe.wait_ge(sig("CT_ready"), (2 * i + g) * (LEVELS - 1) + m)
                    heads4(i, f"X{g}{m}", lambda b, h, hh: mm(hd(b, h), hd(CT, h), hd(TI, h), start=True, stop=True), g)
                    if m == LEVELS - 2:
                        after_read(pe, i, f"MakT{g}")
                        heads4(i, f"U0{g}", lambda b, h, hh: mm(hv(b, h), hd(MakT, h), hv(v, hh), start=True, stop=True), g)
                    after_read(pe, i, f"X{g}{m}")
                    heads4(i, f"TXt{g}{m}", lambda b, h, hh: mm(hd(b, h), hd(XX, h), hd(TT, h), start=True, stop=True), g)
                    if m < LEVELS - 1:
                        heads4(i, f"TX{g}{m}", lambda b, h, hh: mm(hd(b, h), hd(TT, h), hd(XX, h), start=True, stop=True), g)
                yield f"h{g}_solve"
                after_read(pe, i, f"U0{g}")
                after_read(pe, i, f"TXt{g}{LEVELS - 1}")
                heads4(i, f"U1{g}", lambda b, h, hh: mm(hv(b, h), hd(TT, h), hv(sm[:, 0, :], h), start=True, stop=True), g)
                heads4(i, f"WT{g}", lambda b, h, hh: mm(hd(b, h)[0:64, :], hv(feat[:, F_PX, :], hh), hd(TT, h), start=True, stop=True), g)
                for q in range(2):
                    yield f"h{g}_SR{q}"
                    if q == 0:
                        after_read(pe, i, f"WT{g}")
                    pe.wait_ge(sig("ST_ready"), (2 * i + g) * 2 + q + 1)
                    b = take(pe, i, f"SR{g}{q}")
                    settle(pe)
                    for h in range(4):
                        mm(hv(b, h), hd(wT, h), ST[:, 4 * g + h, :], start=True, stop=True)
                    for h in range(4):
                        last = mm(hv(b, 4 + h), hd(R, h), ST[:, 4 * g + h, :], start=True, stop=True)
                    filled(i, f"SR{g}{q}", last)
                    yield f"h{g}_dS{q}"
                    pe.wait_ge(sig("v01_ready"), 2 * i + 2)
                    after_read(pe, i, f"SR{g}{q}")
                    b = take(pe, i, f"dS{g}{q}")
                    settle(pe)
                    for h in range(4):
                        hh = 4 * g + h
                        mm(hv(b, h)[0:64, :], hv(feat[:, F_A, :], hh), hv(sm[:, 2 + q, :], h), start=True, stop=False)
                        last = mm(hv(b, h)[0:64, :], hv(feat[:, F_PI, :], hh), hv(feat[:, V0 if q == 0 else V1, :], hh), start=False, stop=True)
                    filled(i, f"dS{g}{q}", last)
                after_read(pe, i, f"MrkT{g}")
                b = take(pe, i, f"Y{g}")
                settle(pe)
                for h in range(4):
                    hh = 4 * g + h
                    mm(hv(b, h), hd(MrbT, h), hv(sm[:, 2, :], h), start=True, stop=False)
                    mm(hv(b, h), hd(MrbT, h), hv(sm[:, 3, :], h), start=False, stop=False)
                    last = mm(hv(b, h), hd(MrkT, h), hv(v, hh), start=False, stop=True)
                filled(i, f"Y{g}", last)

            def tail(i):
                j = i - 2
                n = NS if isinstance(i, int) and j == NB else P
                yield "t_norm"
                pe.wait_ge(sig("p_loaded"), 16 * j + 16)
                b = take(pe, i, "t_pT")
                settle(pe)
                turn(b[:, 0:n], ptile[0:n, 0:P])
                filled(i, "t_pT", turn(b[:, P:P + n], ptile[0:n, P:2 * P]))
                after_read(pe, i, "t_pT")
                w, used = wchunk(pe, i, "ple")
                w = w.rearrange("p (k n) -> p k n", k=2)
                for c in range(2):
                    b = take(pe, i, f"ple{c}")
                    settle(pe)
                    for k in range(2):
                        last = mm(b[0:n, :], loraT[:, k, 0:n], w[:, k, c * 512:(c + 1) * 512], start=(k == 0), stop=(k == 1))
                    filled(i, f"ple{c}", last)
                pe.wait_ge(sig("bank3_filled"), count(i, "ple1")[1] + 1)
                pe.sem_inc(used, 1)
                yield "t_turn"
                pe.wait_ge(sig("t_xn_ready"), j + 1)
                turn_rows(i, "t_xT", z, n)
                for c in range(4):
                    yield f"gate{c}"
                    if c == 0:
                        after_read(pe, i, "t_xT0")
                        after_read(pe, i, "t_xT1")
                    stream(i, f"gate{c}", n)

            def sum_v(i, n, j):
                s = n % 2 * UNIT + j
                at = PE_EXPERTS.index(j)
                pe.wait_ge(sig("diag_ready"), (i - 1) * UNITS + n + 1)
                pe.wait_ge(sig(f"v{s}_full"), 16 * ((i - 1) * (UNITS // 2) + n // 2 + 1))
                for c in range(2):
                    last = mm(acc[c][:, :], dg[:, n % 2, at, :], vring[:, s, c * 512:(c + 1) * 512],
                              start=(n + at == 0), stop=(n == UNITS - 1 and at == VPE - 1))
                last.then_inc(sig("vpe_used"), 1)

            def expert(i, n, j):
                if n == 1 and j == 0:
                    wait_pos(pe, sig("acc_read"), i - 1)
                    settle(pe)
                if n and j - 1 in PE_EXPERTS:
                    sum_v(i, n - 1, j - 1)

            def finish(i):
                for j in PE_EXPERTS:
                    sum_v(i, UNITS - 1, j)

            def peer_sample():
                pe.wait_ge(sig("acc_read"), NB)
                pe.wait_ge(sig("diag_ready"), NB * UNITS + 1)
                for t in range(NS):
                    pe.wait_ge(sig(f"v{t}_full"), 16 * (NB * (UNITS // 2) + 1))
                    for c in range(2):
                        last = mm(acc[c][0:NS, :], sdg[:, t, :], vring[:, t, c * 512:(c + 1) * 512], start=(t == 0), stop=(t == NS - 1))
                last.then_inc(sig("sample_summed"), 1)

            drive(front, tail, expert, finish, lambda i: None, peer_sample, pe)
            pe.wait_ge(sig("ST_ready"), NB * 4 + 1)
            pe.wait_ge(sig("bank1_read"), count(NB + 2, "gate3")[1] + 1)
            for h in range(H):
                last = turn(bank[1][0:64, h * HD:(h + 1) * HD], ST[:, h, :])
            last.then_inc(sig("wkv_turned"), 1)

        @block.scalar
        def _(act):
            eng_name[id(act)] = "act"
            steps = [0]

            def fn(out, in_, f, **kw):
                return nc.scalar.activation(out, in_, f, **kw)

            def link(ins):
                steps[0] += 1
                ins.then_inc(sig("act_step"), 1)
                act.wait_ge(sig("act_step"), steps[0])

            def restart():
                if steps[0]:
                    act.wait_ge(sig("act_step"), steps[0])
                    settle(act)
                    act.sem_clear(sig("act_step"))
                steps[0] = 0

            def evac(i, use, dst, cols, parts=P, f=ACT.Copy, **kw):
                b = see(act, i, use)
                has_read(i, use, fn(dst, b[0:parts, 0:cols], f, **kw))

            act.wait_ge(sig("consts_ready"), 1)

            def sqrt_of(i, name, src, dst, **kw):
                act.wait_ge(sig(name + "_var"), i)
                fn(dst, src, ACT.Sqrt, **kw).then_inc(sig(name + "_root"), 1)

            def rms_root(name, n, col):
                link(fn(z[0:n, :], x[0:n, :], ACT.Square, accum_out=st[0:n, col:col + 1]))
                fn(st[0:n, col + 1:col + 2], st[0:n, col:col + 1], ACT.Sqrt, scale=1.0 / D, bias=eps[0:n, 0:1]).then_inc(sig(name + "_root"), 1)

            def front(i):
                n = NS if rows(i) == "s" else P
                prompt = rows(i) == "p"
                yield "norm"
                wait_pos(act, sig("handed"), i)
                act.wait_ge(sig("x_loaded"), 16 * i + 16)
                rms_root("n1", n, 0)
                yield "turn"
                act.wait_ge(sig("n1_rs"), i + 1)
                fn(z[0:n, :], x[0:n, :], ACT.Copy, scale=st[0:n, 2:3]).then_inc(sig("xn_ready"), 1)
                for c in range(11):
                    yield f"win{c}"
                    if c == 0:
                        wait_pos(act, sig("gain_used"), i)
                        if not isinstance(i, int) or i >= 2:
                            act.wait_ge(sig("y_ready"), i - 1)
                    if c < 7:
                        evac(i, f"win{c}", pa[0:n, c * WC:(c + 1) * WC], WC, n)
                    else:
                        evac(i, f"win{c}", uv[0:n, (c - 7) * WC:(c - 6) * WC], WC, n, ACT.Gelu)
                    if c == 6:
                        act.wait_ge(sig("bank0_read"), count(i, "win6")[1] + 1)
                        act.wait_ge(sig("bank1_read"), count(i, "win5")[1] + 1)
                        act.sem_inc(sig("proj_ready"), 1)
                act.wait_ge(sig("bank0_read"), count(i, "win10")[1] + 1)
                act.wait_ge(sig("bank1_read"), count(i, "win9")[1] + 1)
                act.sem_inc(sig("uv_ready"), 1)
                yield "lora"
                act.wait_ge(sig("xm_ready"), i + 1)
                link(fn(xm[0:n, 3 * DA:3 * DA + 64], xm[0:n, 3 * DA:3 * DA + 64], ACT.Tanh))
                fn(xm[0:n, 3 * DA + 128:PA], xm[0:n, 3 * DA + 128:PA], ACT.Sigmoid).then_inc(sig("lora_in"), 1)
                b = see(act, i, "loraT")
                link(fn(loraT[0:64, 0:2, 0:n], b[0:64, 0:2 * P].rearrange("p (k t) -> p k t", k=2)[:, :, 0:n], ACT.Copy))
                has_read(i, "loraT", fn(loraT[:, 2, 0:n], b[:, 2 * P:2 * P + n], ACT.Copy))
                yield "ln_root"
                sqrt_of(i + 1, "ln", st[0:n, 16:24], st[0:n, 24:32], scale=1.0 / HD, bias=eps[0:n, 1:2])
                yield "lora_add"
                act.wait_ge(sig("wz_ready"), i + 1)
                fn(feat[0:n, F_LW, :], feat[0:n, F_LW, :], ACT.Sigmoid).then_inc(sig("w_sig"), 1)
                act.wait_ge(sig("az_ready"), i + 1)
                fn(feat[0:n, F_A, :], feat[0:n, F_A, :], ACT.Sigmoid).then_inc(sig("a_sig"), 1)
                evac(i, "g_lora", feat[0:n, F_G, :], DA, n)
                yield "kk"
                sqrt_of(i + 1, "kk", st[0:n, 32:40], st[0:n, 40:48])
                yield "cum"
                if prompt:
                    act.wait_ge(sig("cex_ready"), i + 1)
                    b = see(act, i, "cum")
                    link(fn(feat[:, F_PC, :], b[:, :], ACT.Exp))
                    has_read(i, "cum", fn(feat[:, F_PI, :], b[:, :], ACT.Exp, scale=-1.0))
                    link(fn(feat[:, F_PX, :], feat[:, F_PX, :], ACT.Exp))
                    b = see(act, i, "pl")
                    has_read(i, "pl", fn(PL[:, :, :].rearrange("p h q -> p (h q)"), b[0:64, 0:2 * H], ACT.Exp))
                    act.wait_ge(sig("bank4_read"), count(i, "cum")[1] + 1)
                    act.sem_inc(sig("exps_ready"), 1)
                    yield "masked_v"
                    act.wait_ge(sig("hats_ready"), i + 1)
                    fn(feat[0:64, V0, :], xm[0:64, 2 * DA:3 * DA], ACT.Copy)
                    fn(feat[64:128, V1, :], xm[64:128, 2 * DA:3 * DA], ACT.Copy).then_inc(sig("v01_ready"), 1)
                    for g in range(2):
                        yield f"h{g}_turn"
                        for k, kind in enumerate(("aT", "bT", "kT", "rT")):
                            evac(i, f"{kind}{g}", ft[0:64, k, :], 512, 64)
                        for m in range(1, LEVELS):
                            yield f"h{g}_merge{m}"
                            evac(i, f"X{g}{m}", XX, 512)
                            if m == LEVELS - 2:
                                evac(i, f"U0{g}", sm[:, 0, :], 256)
                        yield f"h{g}_solve"
                        evac(i, f"U1{g}", sm[:, 1, :], 256)
                        evac(i, f"WT{g}", wT[:, :], 512, 64)
                else:
                    act.wait_ge(sig("lw_ready"), i + 1)
                    fn(feat[0:n, F_PC, :], feat[0:n, F_LW, :], ACT.Exp).then_inc(sig("exps_ready"), 1)
                yield "gn_root"
                sqrt_of(i + 1, "gn", st[0:n, 16:24], st[0:n, 24:32], scale=1.0 / HD, bias=eps[0:n, 2:3])
                yield "gn_gate"
                for k in range(2):
                    b = see(act, i, f"zT{k}")
                    has_read(i, f"zT{k}", fn(xT[:, 4 * k:4 * k + 4, 0:n], b[:, 0:4 * n].rearrange("p (k t) -> p k t", k=4), ACT.Copy))
                yield "norm2"
                act.wait_ge(sig("x1_ready"), i + 1)
                rms_root("n2", n, 3)
                yield "x2T"
                for k in range(2):
                    b = see(act, i, f"x2T{k}")
                    has_read(i, f"x2T{k}", fn(xT[:, 4 * k:4 * k + 4, 0:n], b[:, 0:4 * n].rearrange("p (k t) -> p k t", k=4), ACT.Copy))
                for h in range(H + 1):
                    yield f"q{h}"
                    if h < H:
                        b = see(act, i, f"q{h}")
                        has_read(i, f"q{h}", fn(query(h)[:, :, 0:n], b[:, 0:2 * P].rearrange("p (c t) -> p c t", c=2)[:, :, 0:n], ACT.Copy))
                    if h:
                        evac(i, f"sc{h - 1}", sc_all[0:n, (h - 1) * 256:h * 256], 256, n)
                yield "soft"
                act.wait_ge(sig("cv_ready"), i + 1)
                fn(gate[0:n, :], cv[0:n, :], ACT.Exp).then_inc(sig("cv_exp"), 1)
                restart()

            def tail(i):
                j = i - 2
                n = NS if isinstance(i, int) and j == NB else P
                yield "t_norm"
                act.wait_ge(sig("x2_ready"), j + 1)
                rms_root("n3", n, 6)
                b = see(act, i, "t_pT")
                has_read(i, "t_pT", fn(loraT[:, 0:2, 0:n], b[:, 0:2 * P].rearrange("p (k t) -> p k t", k=2)[:, :, 0:n], ACT.Copy))
                evac(i, "ple0", uv[0:n, 0:512], 512, n)
                evac(i, "ple1", uv[0:n, 512:1024], 512, n)
                yield "t_turn"
                act.wait_ge(sig("n3_rs"), j + 1)
                fn(z[0:n, :], x[0:n, :], ACT.Copy, scale=st[0:n, 8:9]).then_inc(sig("t_xn_ready"), 1)
                for c in range(4):
                    yield f"gate{c}"
                    evac(i, f"gate{c}", xn_gate(c)[0:n, :], WC, n, ACT.Sigmoid)
                yield "y_norm"
                act.wait_ge(sig("x3_ready"), j + 1)
                rms_root("n4", n, 9)
                restart()

            def expert(i, n, j):
                if j == 0 and n:
                    diagonals(i, n - 1)
                if j == UNIT - 1:
                    act.wait_ge(sig("u_used"), (i - 1) * HK + (n + 1) * UNIT)
                    fn(pg[:, n % 2, :], ph[:, n % 2, :], ACT.Gelu).then_inc(sig("gelu_ready"), 1)

            def diagonals(i, n):
                act.wait_ge(sig("act_ready"), (i - 1) * UNITS + n + 1)
                wait_pos(act, sig("vpe_used"), ((i - 1) * UNITS + n - 1) * VPE)
                for at, j in enumerate(PE_EXPERTS):
                    last = fn(dg[:, n % 2, at, :], ident[:, :], ACT.Copy, scale=pact[:, n % 2, j:j + 1])
                last.then_inc(sig("diag_ready"), 1)

            def peer_sample():
                act.wait_ge(sig("sxt_used"), NS)
                fn(pg[:, :, :].rearrange("p a b -> p (a b)"), ph[:, :, :].rearrange("p a b -> p (a b)"), ACT.Gelu).then_inc(sig("gelu_ready"), 1)

            drive(front, tail, expert, lambda i: diagonals(i, UNITS - 1), lambda i: None, peer_sample, act)
            act.wait_ge(sig("wkv_turned"), 1)
            fn(ms[0:64, 0, :], bank[1][0:64, :], ACT.Copy).then_inc(sig("wkv_rows"), 1)

        @block.vector
        def _(ve):
            eng_name[id(ve)] = "ve"
            steps = [0]
            v = nc.vector

            def link(ins):
                steps[0] += 1
                ins.then_inc(sig("ve_step"), 1)
                ve.wait_ge(sig("ve_step"), steps[0])

            def restart():
                if steps[0]:
                    ve.wait_ge(sig("ve_step"), steps[0])
                    settle(ve)
                    ve.sem_clear(sig("ve_step"))
                steps[0] = 0

            tt = v.tensor_tensor
            stt = v.scalar_tensor_tensor

            ve.wait_ge(sig("consts_ready"), 1)
            link(v.tensor_copy(iota16[:, :], iota_i[:, :]))
            b = see(ve, 0, "s_sk")
            has_read(0, "s_sk", v.tensor_copy(skT[:, :, :].rearrange("p c n -> p (c n)"), b[:, 0:2 * NK]))
            for k in range(2):
                b = see(ve, 0, f"s_ws{k}")
                has_read(0, f"s_ws{k}", tt(wsT[:, 4 * k:4 * k + 4, :], b[:, :].rearrange("p (g t) -> p g t", g=4), bc(m_causal[:, :], [P, 4, P], 1), ALU.mult))
            b = see(ve, 0, "s_vec")
            has_read(0, "s_vec", v.tensor_copy(vecs[:, :, :].rearrange("p a k -> p (a k)"), b[:, 0:3 * KT]))
            ve.wait_ge(sig("bank3_read"), 1)
            ve.wait_ge(sig("bank2_read"), 1)
            link(v.memset(ST[:, :, :], 0.0))
            ve.sem_inc(sig("ST_ready"), 1)
            link(v.memset(sm[:, 2:4, :], 0.0))
            restart()

            def root_to_scale(name, i, n, col):
                ve.wait_ge(sig(name + "_root"), i)
                return v.reciprocal(st[0:n, col + 2:col + 3], st[0:n, col + 1:col + 2])

            def group_norm(name, i, n, src, dst, g, b):
                s3 = lambda ap: ap.rearrange("p (h d) -> p h d", h=H)
                yield f"{name}_mean"
                if name == "ln":
                    ve.wait_ge(sig("uv_ready"), i)
                elif isinstance(i, int) and i == NB + 1:
                    ve.wait_ge(sig("sy_loaded"), 16)
                link(v.tensor_reduce(st[0:n, 48:56], s3(src), AX.X, ALU.add))
                link(v.tensor_scalar(st[0:n, 48:56], st[0:n, 48:56], 1.0 / HD, None, ALU.mult))
                link(tt(s3(dst), s3(src), bc(st[0:n, 48:56], [n, H, HD], 2), ALU.subtract))
                yield f"{name}_var"
                link(tt(scr(0)[0:n, :], dst, dst, ALU.mult))
                v.tensor_reduce(st[0:n, 16:24], s3(scr(0)[0:n, :]), AX.X, ALU.add).then_inc(sig(name + "_var"), 1)
                yield f"{name}_scale"
                ve.wait_ge(sig(name + "_root"), i)
                link(v.reciprocal(st[0:n, 24:32], st[0:n, 24:32]))
                link(tt(s3(dst), s3(dst), bc(st[0:n, 24:32], [n, H, HD], 2), ALU.mult))
                link(tt(dst, dst, par[g][0:n, :], ALU.mult))
                link(tt(dst, dst, par[b][0:n, :], ALU.add))

            def front(i):
                n = NS if rows(i) == "s" else P
                prompt = rows(i) == "p"
                f = lambda k: feat[0:n, k, :]
                r, k_, v_ = (xm[0:n, c * DA:(c + 1) * DA] for c in range(3))
                s3 = lambda ap: ap.rearrange("p (h d) -> p h d", h=H)
                yield "turn"
                root_to_scale("n1", i + 1, n, 0).then_inc(sig("n1_rs"), 1)
                yield "xT"
                for k in range(2):
                    b = see(ve, i, f"xT{k}")
                    has_read(i, f"xT{k}", tt(xT[:, 4 * k:4 * k + 4, 0:n], b[:, 0:4 * n].rearrange("p (k t) -> p k t", k=4),
                                             bc(vecs[:, KM, 4 * k:4 * k + 4], [P, 4, n], 2), ALU.mult))
                yield "shift0"
                ve.wait_ge(sig("prev_loaded"), 16 * i + 16)
                ve.wait_ge(sig("proj_ready"), i + 1)
                link(tt(xm[0:n, :], xm[0:n, :], pa[0:n, :], ALU.subtract))
                yield "shift1"
                ve.wait_ge(sig("mu_loaded"), 16 * i + 16)
                link(tt(xm[0:n, :], xm[0:n, :], mu[0:n, :], ALU.mult))
                yield "shift2"
                tt(xm[0:n, :], xm[0:n, :], pa[0:n, :], ALU.add).then_inc(sig("xm_ready"), 1)
                yield from group_norm("ln", i + 1, n, uv[0:n, DA:D], uv[0:n, DA:D], "cmlp_ln_g", "cmlp_ln_b")
                ve.sem_inc(sig("vn_ready"), 1)
                yield "lora_add"
                ve.wait_ge(sig("xm_ready"), i + 1)
                b = see(ve, i, "w_lora")
                has_read(i, "w_lora", tt(f(F_LW), b[0:n, :], par["rwkv_w0"][0:n, :], ALU.add))
                after_read(ve, i, "w_lora")
                ve.sem_inc(sig("wz_ready"), 1)
                b = see(ve, i, "a_lora")
                has_read(i, "a_lora", tt(f(F_A), b[0:n, :], par["rwkv_a0"][0:n, :], ALU.add))
                after_read(ve, i, "a_lora")
                ve.sem_inc(sig("az_ready"), 1)
                yield "kk"
                link(tt(f(F_KK), k_, par["rwkv_k_k"][0:n, :], ALU.mult))
                link(tt(scr(0)[0:n, :], f(F_KK), f(F_KK), ALU.mult))
                v.tensor_reduce(st[0:n, 32:40], s3(scr(0)[0:n, :]), AX.X, ALU.add).then_inc(sig("kk_var"), 1)
                yield "gmlp"
                ve.wait_ge(sig("w_sig"), i + 1)
                v.tensor_scalar(f(F_LW), f(F_LW), -math.exp(-0.5), None, ALU.mult).then_inc(sig("lw_ready"), 1)
                if prompt:
                    b = see(ve, i, "spatial")
                    has_read(i, "spatial", tt(s3(scr(1)), s3(b[:, :]), bc(vecs[:, KO, :], [P, H, HD], 2), ALU.add))
                    after_read(ve, i, "spatial")
                else:
                    link(tt(s3(scr(1)[0:n, :]), s3(uv[0:n, DA:D]), bc(ws00[:, :], [n, H, HD], 2), ALU.mult))
                    link(tt(s3(scr(1)[0:n, :]), s3(scr(1)[0:n, :]), bc(bs00[:, :], [n, H, HD], 2), ALU.add))
                link(tt(z[0:n, DA:D], uv[0:n, 0:DA], scr(1)[0:n, :], ALU.mult))
                yield "key"
                ve.wait_ge(sig("a_sig"), i + 1)
                ve.wait_ge(sig("kk_var"), i + 1)
                link(stt(scr(0)[0:n, :], f(F_A), -1.0, par["rwkv_k_a"][0:n, :], ALU.add, ALU.mult))
                link(stt(f(F_KH), scr(0)[0:n, :], 1.0, k_, ALU.add, ALU.mult))
                yield "bonus"
                link(tt(scr(0)[0:n, :], r, f(F_KH), ALU.mult))
                link(tt(scr(0)[0:n, :], scr(0)[0:n, :], par["rwkv_r_k"][0:n, :], ALU.mult))
                link(v.tensor_reduce(st[0:n, 56:64], s3(scr(0)[0:n, :]), AX.X, ALU.add))
                yield "kk_norm"
                ve.wait_ge(sig("kk_root"), i + 1)
                link(v.tensor_scalar(st[0:n, 40:48], st[0:n, 40:48], 1e-12, None, ALU.max))
                link(v.reciprocal(st[0:n, 40:48], st[0:n, 40:48]))
                link(tt(s3(f(F_KK)), s3(f(F_KK)), bc(st[0:n, 40:48], [n, H, HD], 2), ALU.mult))
                link(tt(f(F_A), f(F_A), f(F_KK), ALU.mult))
                yield "cum"
                ve.wait_ge(sig("lw_ready"), i + 1)
                if prompt:
                    b = see(ve, i, "cum")
                    tt(f(F_PX), b[:, :], f(F_LW), ALU.subtract).then_inc(sig("cex_ready"), 1)
                    yield "hats0"
                    ve.wait_ge(sig("exps_ready"), i + 1)
                    tt(f(F_A), f(F_A), f(F_PI), ALU.mult)
                    tt(f(F_PC), f(F_PC), r, ALU.mult)
                    yield "hats1"
                    link(stt(f(F_PX), f(F_KK), -1.0, f(F_PX), ALU.mult, ALU.mult))
                    tt(f(F_PI), f(F_PI), f(F_KH), ALU.mult).then_inc(sig("hats_ready"), 1)
                    yield "masked_v"
                    ve.wait_ge(sig("hats_ready"), i + 1)
                    v.memset(feat[64:128, V0, :], 0.0)
                    v.memset(feat[0:64, V1, :], 0.0).then_inc(sig("v01_ready"), 1)
                    for g in range(2):
                        yield from half(i, g)
                else:
                    ve.wait_ge(sig("exps_ready"), i + 1)
                    ve.sem_inc(sig("sfeat_ready"), 1)
                    yield from sample_step()
                yield from group_norm("gn", i + 1, n, yv[0:n, :], yv[0:n, :], "rwkv_ln_g", "rwkv_ln_b")
                yield "gn_bonus"
                link(tt(s3(scr(0)[0:n, :]), s3(v_), bc(st[0:n, 56:64], [n, H, HD], 2), ALU.mult))
                link(tt(yv[0:n, :], yv[0:n, :], scr(0)[0:n, :], ALU.add))
                yield "gn_gate"
                after_read(ve, i, "g_lora")
                tt(z[0:n, 0:DA], yv[0:n, :], f(F_G), ALU.mult).then_inc(sig("z_ready"), 1)
                ve.sem_inc(sig("gain_free"), 1)
                for c in range(4):
                    yield f"wout{c + 1}"
                    b = see(ve, i, f"wout{c}")
                    has_read(i, f"wout{c}", tt(x[0:n, c * WC:(c + 1) * WC], b[0:n, 0:WC], x[0:n, c * WC:(c + 1) * WC], ALU.add))
                after_read(ve, i, "wout2")
                after_read(ve, i, "wout3")
                ve.sem_inc(sig("x1_ready"), 1)
                yield "xn2"
                link(root_to_scale("n2", i + 1, n, 3))
                ve.wait_ge(sig("gain_loaded"), 16 * i + 16)
                stt(xn2[0:n, :], x[0:n, :], st[0:n, 5:6], gain[0:n, :], ALU.mult, ALU.mult).then_inc(sig("xn2_ready"), 1)
                ve.wait_ge(sig("xn2_ready"), i + 1)
                ve.sem_inc(sig("gain_used"), 1)
                ve.sem_inc(sig("x_norm_done"), 1)
                for h in range(H):
                    for c in range(2):
                        yield f"top{h + 1}" if c == 0 else f"q{h + 2}"
                        if c == 0:
                            after_read(ve, i, f"sc{h}")
                            settle(ve)
                        s = sc_all[0:n, h * 256 + c * NK:h * 256 + (c + 1) * NK]
                        top16(s, tkv[0:n, 0:NK], sv[0:n, h, c, :], si[0:n, h, c, :])
                yield "cand"
                cand = sc_all[0:n, :].rearrange("p (h a b) -> p h a b", h=H, a=TOPK)
                for h in range(H):
                    ins = tt(cand[:, h], bc(sv[0:n, h, 0, :], [n, TOPK, TOPK], 2), bc(sv[0:n, h, 1, :], [n, TOPK, TOPK], 1), ALU.add)
                link(ins)
                for h in range(H):
                    yield f"ctop{h}"
                    top16(sc_all[0:n, h * 256:(h + 1) * 256], tkv[0:n, :], cv[0:n, h * TOPK:(h + 1) * TOPK], ci[0:n, h * TOPK:(h + 1) * TOPK])
                yield "soft"
                c3 = lambda ap: ap.rearrange("p (h k) -> p h k", h=H)
                link(v.tensor_copy(st[0:n, 48:56], c3(cv[0:n, :])[:, :, 0]))
                tt(c3(cv[0:n, :]), c3(cv[0:n, :]), bc(st[0:n, 48:56], [n, H, TOPK], 2), ALU.subtract).then_inc(sig("cv_ready"), 1)
                link(v.tensor_copy(sif[0:n], si[0:n]))
                o4 = oneh[0:n, :].rearrange("p (h j k) -> p h j k", h=H, j=TOPK)
                for half_, dst in ((0, e1), (1, e2)):
                    yield f"digit{half_}a"
                    op, arg = (ALU.logical_shift_right, 4) if half_ == 0 else (ALU.bitwise_and, TOPK - 1)
                    link(v.tensor_scalar(hi[0:n, :], ci[0:n, :], arg, None, op))
                    link(v.tensor_copy(dst[0:n, :], hi[0:n, :]))
                    link(tt(oneh[0:n, :].rearrange("p (j k) -> p j k", k=TOPK), bc(dst[0:n, :], [n, HK, TOPK], 2), bc(iota16[0:n, :], [n, HK, TOPK], 1), ALU.is_equal))
                    yield f"digit{half_}b"
                    for h in range(H):
                        ins = tt(o4[:, h], o4[:, h], bc(sif[0:n, h, half_, :], [n, TOPK, TOPK], 1), ALU.mult)
                    link(ins)
                    yield f"digit{half_}c"
                    link(v.tensor_reduce(dst[0:n, :], oneh[0:n, :].rearrange("p (j k) -> p j k", k=TOPK), AX.X, ALU.add))
                yield "expert"
                link(stt(e1[0:n, :], e1[0:n, :], float(NK), e2[0:n, :], ALU.mult, ALU.add))
                at = (i % 2) * HK
                link(v.tensor_copy(eidx[0:n, at:at + HK] if isinstance(i, int) else eidx[:, bass.ds(at, HK)], e1[0:n, :]))
                ve.wait_ge(sig("cv_exp"), i + 1)
                link(v.tensor_reduce(st[0:n, 48:56], c3(gate[0:n, :]), AX.X, ALU.add))
                link(v.reciprocal(st[0:n, 48:56], st[0:n, 48:56]))
                link(tt(c3(gate[0:n, :]), c3(gate[0:n, :]), bc(st[0:n, 48:56], [n, H, TOPK], 2), ALU.mult))
                restart()
                ve.sem_inc(sig("topk_done"), 1)

            def top16(s, tmp, val, idx):
                link(v.max(val[:, 0:8], s))
                v.max_index(idx[:, 0:8], val[:, 0:8], s)
                link(v.match_replace(tmp, val[:, 0:8], s, NEG))
                link(v.max(val[:, 8:16], tmp))
                link(v.max_index(idx[:, 8:16], val[:, 8:16], tmp))

            def sample_step():
                fr, fk, fv, fw, fkk, fb = (ms[0:64, 0, 64 * k:64 * k + 64] for k in range(6))
                S = ft[0:64, 0:2, :].rearrange("p a n -> p (a n)").rearrange("p (v k) -> p v k", v=16)
                tmp = ft[0:64, 2:4, :].rearrange("p a n -> p (a n)").rearrange("p (v k) -> p v k", v=16)
                sa = ms[0:64, 2, 0:16]
                over_v = lambda ap: bc(ap, [64, 16, HD], 1)
                over_k = lambda ap: bc(ap, [64, 16, HD], 2)
                for q in range(4):
                    vq = fv[:, 16 * q:16 * q + 16]
                    yield f"h0_update{q + 1}"
                    if q == 0:
                        ve.wait_ge(sig("sfeat_loaded"), 16)
                    ve.wait_ge(sig("swkv_loaded"), 16 * q + 16)
                    link(tt(tmp, S, over_v(fkk), ALU.mult))
                    link(v.tensor_reduce(sa, tmp, AX.X, ALU.add))
                    link(tt(S, S, over_v(fw), ALU.mult))
                    link(tt(tmp, over_k(sa), over_v(fb), ALU.mult))
                    link(tt(S, S, tmp, ALU.subtract))
                    link(tt(tmp, over_k(vq), over_v(fk), ALU.mult))
                    link(tt(S, S, tmp, ALU.add))
                    link(tt(tmp, S, over_v(fr), ALU.mult))
                    v.tensor_reduce(ms[0:64, 1, 16 * q:16 * q + 16], tmp, AX.X, ALU.add).then_inc(sig("swkv_new"), 1)
                    ve.wait_ge(sig("swkv_new"), q + 1)

            def half(i, g):
                h4 = lambda ap: ap.rearrange("p (h t) -> p h t", h=4)
                mask = lambda m: bc(m, [P, 4, P], 1)
                masked = {"MT": (MT, m_strict), "MakT": (MakT, m_strict), "MrbT": (MrbT, m_incl), "MrkT": (MrkT, m_incl)}

                def keep(use):
                    dst, m = masked[use]
                    b = see(ve, i, f"{use}{g}")
                    has_read(i, f"{use}{g}", tt(h4(dst), h4(b[:, :]), mask(m[:, :]), ALU.mult))

                yield f"h{g}_TT"
                keep("MT")
                after_read(ve, i, f"MT{g}")
                link(tt(h4(TT), h4(MT), mask(m_level[:, 0, :]), ALU.mult))
                link(tt(h4(TT), h4(TT), mask(ident[:, :]), ALU.add))
                yield f"h{g}_TI"
                b = see(ve, i, f"M{g}")
                has_read(i, f"M{g}", tt(h4(TI), h4(b[:, :]), mask(m_pairT[:, :]), ALU.mult))
                after_read(ve, i, f"M{g}")
                link(tt(h4(TI), h4(TI), mask(ident[:, :]), ALU.add))
                tt(h4(CT), h4(MT), mask(m_level[:, 1, :]), ALU.mult).then_inc(sig("CT_ready"), 1)
                for m in range(1, LEVELS):
                    yield f"h{g}_merge{m}"
                    if m <= 3:
                        keep(("MakT", "MrbT", "MrkT")[m - 1])
                    yield f"h{g}_update{m}"
                    if m < LEVELS - 1:
                        b = see(ve, i, f"TX{g}{m}")
                        has_read(i, f"TX{g}{m}", tt(TI, b[:, :], TI, ALU.add))
                    b = see(ve, i, f"TXt{g}{m}")
                    has_read(i, f"TXt{g}{m}", tt(TT, b[:, :], TT, ALU.add))
                    if m < LEVELS - 1:
                        after_read(ve, i, f"TX{g}{m}")
                        after_read(ve, i, f"TXt{g}{m}")
                        tt(h4(CT), h4(MT), mask(m_level[:, m + 1, :]), ALU.mult).then_inc(sig("CT_ready"), 1)
                STg = ST[:, 4 * g:4 * g + 4, :]
                for q in range(2):
                    p0, p1 = CH * q, CH * q + CH
                    yield f"h{g}_dS{q}"
                    if q == 0:
                        after_read(ve, i, f"U1{g}")
                    b = see(ve, i, f"SR{g}{q}")
                    tt(sm[p0:p1, 2 + q, :], b[p0:p1, 0:256], sm[p0:p1, 1, :], ALU.add)
                    has_read(i, f"SR{g}{q}", v.tensor_copy(sm[p0:p1, 4, :], b[p0:p1, 256:512]))
                    yield f"h{g}_SR1" if q == 0 else f"h{g}_Y"
                    b = see(ve, i, f"dS{g}{q}")
                    has_read(i, f"dS{g}{q}", tt(STg, b[0:64, 0:256].rearrange("p (h v) -> p h v", h=4), STg, ALU.add))
                    after_read(ve, i, f"dS{g}{q}")
                    tt(STg, STg, bc(PL[:, 4 * g:4 * g + 4, q], [64, 4, HD], 2), ALU.mult).then_inc(sig("ST_ready"), 1)
                b = see(ve, i, f"Y{g}")
                after_read(ve, i, f"SR{g}1")
                has_read(i, f"Y{g}", tt(yv[:, 256 * g:256 * g + 256], b[:, 0:256], sm[:, 4, :], ALU.add))
                after_read(ve, i, f"Y{g}")

            def handoff(i):
                if not isinstance(i, int) or 0 < i <= NB:
                    v.tensor_copy(pgate[:, :], gate[:, :])
                    v.tensor_copy(px[:, :], xn2[:, :]).then_inc(sig("handed"), 1)
                    ve.wait_ge(sig("handed"), i)
                elif i == NB + 1:
                    b = see(ve, NB, "eT")
                    v.tensor_copy(sidx[:, :], b[:, 0:NS])
                    has_read(NB, "eT", v.tensor_copy(pgate[:, 0:NS], b[:, NS:2 * NS]))
                    after_read(ve, NB, "eT")
                    ve.sem_inc(sig("handed"), 1)

            def take_sums(i):
                j = i - 2
                sample = isinstance(i, int) and j == NB
                m = NS if sample else P
                ve.wait_ge(sig("x1_loaded"), 16 * j + 16)
                if sample:
                    ve.wait_ge(sig("sample_summed"), 1)
                else:
                    link(tt(x[:, :], x[:, :], accv[:, :], ALU.add))
                    ve.wait_ge(sig("vpe_used"), (i - 1) * UNITS * VPE)
                for c in range(2):
                    ins = tt(x[0:m, c * 512:(c + 1) * 512], acc[c][0:m, :], x[0:m, c * 512:(c + 1) * 512], ALU.add)
                link(ins)
                restart()
                ve.sem_inc(sig("x2_ready"), 1)
                ve.sem_inc(sig("acc_read"), 1)

            def tail(i):
                j = i - 2
                n = NS if isinstance(i, int) and j == NB else P
                yield "t_sum"
                take_sums(i)
                yield "t_turn"
                root_to_scale("n3", j + 1, n, 6).then_inc(sig("n3_rs"), 1)
                yield "t_xT"
                for k in range(2):
                    b = see(ve, i, f"t_xT{k}")
                    has_read(i, f"t_xT{k}", tt(xT[:, 4 * k:4 * k + 4, 0:n], b[:, 0:4 * n].rearrange("p (k t) -> p k t", k=4),
                                               bc(vecs[:, KN, 4 * k:4 * k + 4], [P, 4, n], 2), ALU.mult))
                for c in range(4):
                    yield f"gate{c + 1}"
                    if c == 0:
                        after_read(ve, i, "ple1")
                    after_read(ve, i, f"gate{c}")
                    link(tt(xn_gate(c)[0:n, :], xn_gate(c)[0:n, :], uv[0:n, c * WC:(c + 1) * WC], ALU.mult))
                    link(tt(x[0:n, c * WC:(c + 1) * WC], xn_gate(c)[0:n, :], x[0:n, c * WC:(c + 1) * WC], ALU.add))
                ve.sem_inc(sig("x3_ready"), 1)
                yield "y"
                link(root_to_scale("n4", j + 1, n, 9))
                ve.wait_ge(sig("fgain_loaded"), 16 * j + 16)
                stt(x[0:n, :], x[0:n, :], st[0:n, 11:12], gain[0:n, :], ALU.mult, ALU.mult).then_inc(sig("y_ready"), 1)
                restart()

            def weigh(i, n):
                ve.wait_ge(sig("gelu_ready"), (i - 1) * UNITS + n + 1)
                tt(pact[:, n % 2, :], pg[:, n % 2, :], pgate[:, n * UNIT:(n + 1) * UNIT], ALU.mult).then_inc(sig("act_ready"), 1)

            def sum_v(i, n, j):
                s = n % 2 * UNIT + j
                act_j = pact[:, n % 2, j:j + 1]
                ve.wait_ge(sig("act_ready"), (i - 1) * UNITS + n + 1)
                ve.wait_ge(sig(f"v{s}_full"), 16 * ((i - 1) * (UNITS // 2) + n // 2 + 1))
                wait_pos(ve, sig("vve_used"), ((i - 1) * UNITS + n) * VVE + VE_EXPERTS.index(j))
                if n == 0 and j == VE_EXPERTS[0]:
                    ins = v.tensor_scalar(accv[:, :], vring[:, s, :], act_j, None, ALU.mult)
                else:
                    ins = stt(accv[:, :], vring[:, s, :], act_j, accv[:, :], ALU.mult, ALU.add)
                ins.then_inc(sig("vve_used"), 1)

            def expert(i, n, j):
                s = n % 2 * UNIT + j
                ve.wait_ge(sig(f"u{s}_full"), 16 * ((i - 1) * (UNITS // 2) + n // 2 + 1))
                v.tensor_tensor_reduce(out=uring[:, s, :], in0=uring[:, s, :], in1=px[:, :], scale=1.0, scalar=0.0,
                                       op0=ALU.mult, op1=ALU.add, accum_out=ph[:, n % 2, j:j + 1]).then_inc(sig("u_used"), 1)
                if n and j == 0:
                    weigh(i, n - 1)
                if n and j in VE_EXPERTS:
                    sum_v(i, n - 1, j)

            def finish(i):
                weigh(i, UNITS - 1)
                for j in VE_EXPERTS:
                    sum_v(i, UNITS - 1, j)
                ve.wait_ge(sig("vve_used"), i * UNITS * VVE)

            def peer_sample():
                for t in range(NS):
                    ve.wait_ge(sig(f"u{t}_full"), 16 * (NB * (UNITS // 2) + 1))
                    ve.wait_ge(sig(f"sxt{t}_loaded"), 16)
                    v.tensor_tensor_reduce(out=uring[:, t, :], in0=uring[:, t, :], in1=vring[:, t, :], scale=1.0, scalar=0.0,
                                           op0=ALU.mult, op1=ALU.add, accum_out=ph[:, t // UNIT, t % UNIT:t % UNIT + 1]).then_inc(sig("sxt_used"), 1)
                c = NB * UNITS
                ve.wait_ge(sig("gelu_ready"), c + 1)
                tt(pact[:, :, :].rearrange("p a b -> p (a b)"), pg[:, :, :].rearrange("p a b -> p (a b)"), pgate[:, 0:NS], ALU.mult).then_inc(sig("act_ready"), 1)
                ve.wait_ge(sig("act_ready"), c + 1)
                tt(sdg[:, :, :], diag8[:, :, :], bc(pact[:, :, :].rearrange("p a b -> p (a b)"), [P, NS, NS], 2), ALU.mult).then_inc(sig("diag_ready"), 1)

            drive(front, tail, expert, finish, handoff, peer_sample, ve)


_INS = ['x_prompt', 'x_sample', 'state_wkv', 'state_shift', 'p_prompt', 'p_sample', 'norm_mix_g', 'w_in', 'shift_mu', 'rwkv_w0',
        'rwkv_w2', 'rwkv_a0', 'rwkv_a2', 'rwkv_g2', 'rwkv_k_k', 'rwkv_k_a', 'rwkv_r_k', 'rwkv_ln_g', 'rwkv_ln_b', 'cmlp_ln_g',
        'cmlp_ln_b', 'cmlp_ws', 'cmlp_bs', 'w_out', 'norm_ffn_g', 'peer_wq', 'peer_subkeys', 'peer_u', 'peer_v', 'norm_ple_g',
        'ple_w', 'ple_gate_w', 'norm_final_g']
_OUTS = [((1, T_PROMPT, D), 'float32'), ((NS, 1, D), 'float32'), ((1, 1, H, HD, HD), 'float32'), ((1, 1, PA), 'float32'),
         ((1, NS, H, HD, HD), 'float32'), ((1, NS, PA), 'float32'), ((1, NS, 1, DA), 'float32')]


def kernel(**inputs):
    import numpy as _np
    import concourse.bacc as _bacc
    from concourse import mybir as _mybir
    from concourse.bass_utils import run_bass_kernel_spmd as _run

    nc = _bacc.Bacc("TRN2", target_bir_lowering=False, num_devices=1)
    arrays, args, outs = {}, {}, []
    for name in _INS:
        arr = _np.ascontiguousarray(inputs[name])
        arrays[f"in_{name}_dram"] = arr
        args[name] = nc.dram_tensor(f"in_{name}_dram", arr.shape, _mybir.dt.from_np(arr.dtype), kind="ExternalInput").ap()
    for i, (shape, dtype) in enumerate(_OUTS):
        outs.append(nc.dram_tensor(f"out_{i}_dram", shape, _mybir.dt.from_np(_np.dtype(dtype)), kind="ExternalOutput").ap())
    build(nc, args, outs)
    r = _run(nc, [arrays], core_ids=[0])
    return tuple(r.results[0][f"out_{i}_dram"] for i in range(len(_OUTS)))
```

```python
from contextlib import ExitStack
import math

import concourse.bass as bass
from concourse import mybir

F32 = mybir.dt.float32
U32 = mybir.dt.uint32
I32 = mybir.dt.int32
ALU = mybir.AluOpType
ACT = mybir.ActivationFunctionType
AX = mybir.AxisListType

P = 128
D = 1024
KT = D // P
T_PROMPT = 1024
NB = T_PROMPT // P
NS = 8
DA = 512
H = 8
HD = 64
PA = 1792
CH = 64
TOPK = 16
NK = 128
HK = H * TOPK
WC = 256
LEVELS = 6
NU, NV = 8, 8
NI = 4
UNIT = 4
UNITS = HK // UNIT
SPREAD = 123
PE_SHARE = {0: 2, 3: 1, 9: 3, 13: 2, 26: 4}
MOST_PE = max(PE_SHARE.values())
RMS_EPS, LN_EPS, GN_EPS = 1e-6, 1e-5, 64e-5
NEG = -3.0e38


def pe_experts(n):
    share = PE_SHARE[max(start for start in PE_SHARE if start <= n)]
    return {1: (2,), 2: (0, 2), 3: (0, 1, 2), 4: (0, 1, 2, 3)}[share]


def ve_experts(n):
    return tuple(j for j in range(UNIT) if j not in pe_experts(n))


PER_BLOCK = {who: sum(len(who(n)) for n in range(UNITS)) for who in (pe_experts, ve_experts)}


def summed(who, i, n, j=UNIT - 1):
    if n < 0:
        i, n = i - 1, n + UNITS
    return (i - 1) * PER_BLOCK[who] + sum(len(who(m)) for m in range(n)) + sum(e <= j for e in who(n))


TAIL_STAGES = ["t_sum", "t_norm", "t_turn", "t_xT"] + [f"gate{c}" for c in range(5)] + ["y_norm", "y"]
NORM = lambda name: [f"{name}_{part}" for part in ("mean", "var", "root", "scale")]
HALF_STAGES = lambda g: (
    [f"h{g}_{part}" for part in ("turn", "products", "TT", "TI")]
    + [f"h{g}_{part}{m}" for m in range(1, LEVELS) for part in ("merge", "update")]
    + [f"h{g}_{part}" for part in ("solve", "SR0", "dS0", "SR1", "dS1", "Y")]
)
FRONT_STAGES = (
    ["norm", "turn", "xT"] + [f"win{c}" for c in range(11)] + ["shift0", "shift1", "shift2", "lora"] + NORM("ln") + ["lora_add", "kk", "gmlp", "key", "bonus", "kk_norm", "cum", "hats0", "hats1", "masked_v"]
    + [stage for both in zip(HALF_STAGES(0), HALF_STAGES(1)) for stage in both]
    + NORM("gn") + ["gn_bonus", "gn_gate"] + [f"wout{c}" for c in range(5)] + ["norm2", "xn2", "x2T"]
    + [stage for h in range(H + 2) for stage in [f"q{h}"] + ([f"ctop{h - 2}"] if h > 1 else []) + [f"top{h}"]] + ["soft"]
    + [f"digit{half}{part}" for half in range(2) for part in "abc"] + ["expert"]
)

HALF = lambda g: {
    3 * g: [f"aT{g}", f"rT{g}", f"MakT{g}"] + [f"TXt{g}{m}" for m in range(1, LEVELS)] + [f"SR{g}0", f"dS{g}1"],
    3 * g + 1: [f"bT{g}", f"MT{g}", f"MrbT{g}"] + [f"TX{g}{m}" for m in range(1, LEVELS - 1)] + [f"U1{g}", f"dS{g}0", f"Y{g}"],
    3 * g + 2: [f"kT{g}", f"M{g}", f"X{g}1", f"X{g}2", f"MrkT{g}", f"X{g}3", f"X{g}4", f"U0{g}", f"X{g}5", f"WT{g}", f"SR{g}1"],
}
SETUP_USES = {0: ["s_sk"], 1: ["s_ws0"], 2: ["s_ws1"], 3: ["s_vec"], 4: [], 5: []}
TAIL_USES = {
    0: ["t_xT0", "gate0", "gate2"], 1: ["t_xT1", "gate1", "gate3"], 2: ["ple0"], 3: ["ple1"], 4: ["t_pT"], 5: [],
}
_IN = {b: [f"xT{b}"] + [f"win{c}" for c in range(11) if c % 2 == b] for b in (0, 1)}
_OUT = {b: [f"zT{b}"] + [f"wout{c}" for c in range(4) if c % 2 == b] + [f"x2T{b}"] for b in (0, 1)}
_Q = {2 + b: [f"q{h}" for h in range(H) if h % 2 == b] for b in (0, 1)}
_Q |= {4 + b: [f"sc{h}" for h in range(H) if h % 2 == b] for b in (0, 1)}
FRONT_USES = {
    0: _IN[0] + HALF(0)[0] + _OUT[0],
    1: _IN[1] + HALF(0)[1] + _OUT[1],
    2: ["spatial"] + HALF(0)[2] + _Q[2],
    3: ["loraT", "g_lora"] + HALF(1)[3] + _Q[3],
    4: ["w_lora", "cum"] + HALF(1)[4] + _Q[4],
    5: ["a_lora", "pl"] + HALF(1)[5] + _Q[5],
}
SAMPLE_USES = {
    0: _IN[0] + _OUT[0], 1: _IN[1] + _OUT[1], 2: _Q[2], 3: ["loraT", "g_lora"] + _Q[3],
    4: ["w_lora"] + _Q[4], 5: ["a_lora"] + _Q[5] + ["eT"],
}
W_TAIL = ["ple"] + [f"gate{c}" for c in range(4)]
W_FRONT = [f"win{c}" for c in range(11)] + [f"wout{c}" for c in range(4)] + [f"wq{h}" for h in range(H)]


BOTH_STAGES = (TAIL_STAGES[:TAIL_STAGES.index("gate2")] + ["norm"] + ["gate2", "gate3", "turn", "gate4", "xT", "y_norm", "y"]
               + FRONT_STAGES[FRONT_STAGES.index("win0"):])
STAGE_WEIGHTS = {
    "t_sum": 33, "t_norm": 25, "t_turn": 15, "t_xT": 13, "gate4": 10, "gate": 48, "y_norm": 10, "y": 14, "norm": 12, "norm2": 12,
    "turn": 15, "xT": 14, "win": 55, "ln_mean": 26, "ln_var": 20, "ln_root": 5, "ln_scale": 30, "shift": 32, "lora": 55,
    "lora_add": 22, "kk": 34, "gmlp": 36, "key": 26, "bonus": 38, "kk_norm": 30, "cum": 18, "hats": 26, "masked_v": 28,
    "h_turn": 42, "h_products": 32, "h_TT": 38, "h_TI": 42, "h_merge": 48, "h_update": 18, "h_update5": 8, "h_solve": 28,
    "h_SR": 14, "h_dS": 14, "h_Y": 14, "gn_mean": 20, "gn_var": 16, "gn_root": 5, "gn_scale": 24, "gn_bonus": 18, "gn_gate": 20,
    "wout4": 8, "wout": 50, "xn2": 16, "x2T": 18, "q": 40, "top": 18, "q8": 22, "q9": 20, "top9": 1, "ctop": 24, "soft": 14,
    "digita": 48, "digitb": 46, "digitc": 38, "expert": 20,
}


def stage_weight(name):
    if name[0] == "h" and name[1].isdigit():
        name = "h" + name[2:]
    if name.startswith("digit"):
        name = "digit" + name[-1]
    return STAGE_WEIGHTS[name] if name in STAGE_WEIGHTS else STAGE_WEIGHTS[name.rstrip("0123456789")]


def uses_before(i, name, setup, tail, front, sample):
    if not isinstance(i, int):
        return (len(front) + len(tail)) * i + (len(setup) - 2 * len(tail) + (tail + front).index(name))
    here = (tail if i >= 2 else []) + (front if i < NB else sample if i == NB else [])
    before = len(setup) + len(front) * min(i, NB) + (len(sample) if i > NB else 0) + len(tail) * max(i - 2, 0)
    return before + here.index(name)


def build(nc, a, outs):
    y_prompt, y_sample, wkv_prompt, shift_prompt, wkv_sample, shift_sample, chunk_v = outs
    flat = lambda ap: ap.rearrange("a b d -> (a b) d")
    x_dram = {"p": flat(a["x_prompt"]), "s": flat(a["x_sample"])}
    ple_dram = {"p": a["p_prompt"][0, 0], "s": a["p_sample"][0].rearrange("b s d -> (b s) d")}
    y_dram = {"p": flat(y_prompt), "s": flat(y_sample)}
    peer_u, peer_v = a["peer_u"][0], a["peer_v"][0]
    scratch = lambda name, shape: nc.dram_tensor(name, shape, F32, kind="Internal").ap()
    proj_s = scratch("proj_s", (1 + NB, PA))
    x1_s = scratch("x1_s", (T_PROMPT + NS, D))
    feat_s = scratch("feat_s", (6, NS, DA))
    ysamp_s = scratch("ysamp_s", (NS, DA))
    xn2_s = scratch("xn2_s", (NS, D))

    ctx = ExitStack()
    with ctx:
        sb = lambda name, shape, dt=F32: ctx.enter_context(nc.sbuf_tensor(name, shape, dt))
        sems = {}

        def sig(name):
            if name not in sems:
                sems[name] = ctx.enter_context(nc.semaphore(name))
            return sems[name]

        bank = [ctx.enter_context(nc.psum_tensor(f"bank{k}", [P, 512], F32)) for k in range(6)]
        acc = [ctx.enter_context(nc.psum_tensor(f"peer_acc{k}", [P, 512], F32)) for k in range(2)]

        ident = sb("ident", [P, P])
        m_incl = sb("m_incl", [P, P])
        m_strict = sb("m_strict", [P, P])
        m_causal = sb("m_causal", [P, P])
        m_pairT = sb("m_pairT", [P, P])
        m_level = sb("m_level", [P, LEVELS, P])
        chunk_of = sb("chunk_of", [P, 2])
        diag8 = sb("diag8", [P, NS, NS])
        iota_i = sb("iota_i", [P, TOPK], I32)
        iota16 = sb("iota16", [P, TOPK])
        bcast_names = ["rwkv_w0", "rwkv_a0", "rwkv_k_k", "rwkv_k_a", "rwkv_r_k", "rwkv_ln_g", "rwkv_ln_b", "cmlp_ln_g", "cmlp_ln_b"]
        par = {nm: sb("p_" + nm, [P, DA]) for nm in bcast_names}
        w2 = sb("w2", [64, DA])
        a2 = sb("a2", [64, DA])
        g2 = sb("g2", [P, DA])
        wsT = sb("wsT", [P, H, P])
        skT = sb("skT", [P, 2, NK])
        vecs = sb("vecs", [P, 3, KT])
        ws00 = sb("ws00", [NS, H])
        bs00 = sb("bs00", [NS, H])
        wbuf = sb("wbuf", [P, 2, KT * WC])
        uring = sb("uring", [P, NU, D])
        vring = sb("vring", [P, NV, D])
        idx_c = sb("idx_c", [P, NI, UNIT], U32)
        x = sb("x", [P, D])
        xT = sb("xT", [P, KT, P])
        z = sb("z", [P, D])
        uv = sb("uv", [P, D])
        xn2 = z
        pa = sb("pa", [P, PA])
        xm = sb("xm", [P, PA])
        feat = sb("feat", [P, 8, DA])
        ft = sb("ft", [P, 4, 512])
        ms = sb("ms", [P, 5, 512])
        sm = sb("sm", [P, 5, 256])
        loraT = sb("loraT", [P, 3, P])
        ST = sb("ST", [64, H, HD])
        PL = sb("PL", [64, H, 2])
        st = sb("st", [P, 64])
        eps = sb("eps", [P, 3])
        sv = sb("sv", [P, H, 2, TOPK])
        si = sb("si", [P, H, 2, TOPK], U32)
        cv = sb("cv", [P, HK])
        ci = sb("ci", [P, HK], U32)
        hi = sb("hi", [P, HK], U32)
        e1 = sb("e1", [P, HK])
        e2 = sb("e2", [P, HK])
        gate = sb("gate", [P, HK])
        eidx = sb("eidx", [P, 2 * HK], U32)
        px = sb("px", [P, D])
        pgate = sb("pgate", [P, HK])
        sidx = sb("sidx", [P, NS], U32)
        accv = sb("accv", [P, D])
        ph = sb("ph", [P, 2, UNIT])
        pg = sb("pg", [P, 2, UNIT])
        pact = sb("pact", [P, 2, UNIT])
        sdg = sb("sdg", [P, NS, NS])
        dg = sb("dg", [P, 2, MOST_PE, P])

        mu = feat[:, 0:4, :].rearrange("p a n -> p (a n)")[:, 0:PA]
        sc_all = feat[:, 0:4, :].rearrange("p a n -> p (a n)")
        oneh = feat[:, 4:8, :].rearrange("p a n -> p (a n)")
        F_LW, F_A, F_G, F_KK, F_KH, F_PC, F_PI, F_PX = range(8)
        yv = feat[:, F_LW, :]
        ptile = feat[:, 3, 0:2 * P]
        tkv = oneh[:, 0:256]
        sif = sv
        scr = lambda k: ft[:, k, :]
        col = lambda ap, k: ap[:, 512 * k:512 * k + 512]
        xT_flat = xT[:, :, :].rearrange("p k t -> p (k t)")
        wb = [wbuf[:, b, :] for b in range(2)]
        hatsT = [[ft[0:64, k, :] for k in range(4)], [col(uv, 0)[0:64], col(uv, 1)[0:64], col(x, 0)[0:64], col(x, 1)[0:64]]]
        MT, MakT, MrbT = ([col(pa, 0), col(xm, 0)], [col(pa, 1), col(xm, 1)], [col(pa, 2), col(z, 0)])
        MrkT, TI, TT, XX, CT = ([ms[:, 0, :], col(wb[1], 0)], [ms[:, 1, :], col(xT_flat, 0)], [ms[:, 2, :], col(xT_flat, 1)],
                                [ms[:, 3, :], col(wb[1], 1)], [ms[:, 4, :], col(wb[1], 2)])
        wTs = [wb[0][0:64, 5 * 256:5 * 256 + 512], col(wb[1], 3)[0:64]]
        sms = [sm[:, :, :], wb[0][:, 0:5 * 256].rearrange("p (k n) -> p k n", k=5)]
        gain = pa[:, 0:D]
        KM, KN, KO = 0, 1, 2
        V0, V1 = F_KK, F_KH

        def settle(eng):
            eng.sem_inc(sig("settled_" + eng_name[id(eng)]), 1)

        eng_name = {}

        def seq(i, b, use):
            return uses_before(i, use, SETUP_USES[b], TAIL_USES[b], FRONT_USES[b], SAMPLE_USES[b])

        def bank_of(i, use):
            for table in (SETUP_USES, TAIL_USES, SAMPLE_USES if isinstance(i, int) and i >= NB else FRONT_USES):
                for b in table:
                    if use in table[b]:
                        return b
            raise KeyError(use)

        def wait_pos(eng, s, v):
            if not isinstance(v, int) or v > 0:
                eng.wait_ge(s, v)

        def count(i, use):
            b = bank_of(i, use)
            return b, (0 if use.startswith("s_") else seq(i, b, use))

        def take(pe, i, use):
            b, n = count(i, use)
            wait_pos(pe, sig(f"bank{b}_read"), n)
            return bank[b]

        def filled(i, use, ins):
            ins.then_inc(sig(f"bank{count(i, use)[0]}_filled"), 1)

        def see(eng, i, use):
            b, n = count(i, use)
            eng.wait_ge(sig(f"bank{b}_filled"), n + 1)
            return bank[b]

        def has_read(i, use, ins):
            ins.then_inc(sig(f"bank{count(i, use)[0]}_read"), 1)

        def after_read(eng, i, use):
            b, n = count(i, use)
            eng.wait_ge(sig(f"bank{b}_read"), n + 1)

        def wseq(i, name):
            if not isinstance(i, int):
                at = (W_TAIL + W_FRONT).index(name) - 2 * len(W_TAIL)
                per = len(W_TAIL) + len(W_FRONT)
                assert per % 2 == 0
                return at % 2, (per // 2) * i + at // 2
            n = uses_before(i, name, [], W_TAIL, W_FRONT, W_FRONT)
            return n % 2, n // 2

        def wchunk(pe, i, name, half):
            b, n = wseq(i, name)
            pe.wait_ge(sig(f"w{b}{half}_loaded"), 16 * n + 16)
            return wbuf[:, b, :], sig(f"w{b}{half}_used")

        def load_w(sp, i, name):
            b, n = wseq(i, name)
            for half in range(2):
                wait_pos(sp, sig(f"w{b}{half}_used"), n)
                if not isinstance(n, int):
                    settle(sp)
                if name == "ple":
                    src, dst = a["ple_w"][0].rearrange("(k p) n -> p k n", p=P), wbuf[:, b, :].rearrange("p (k n) -> p k n", k=2)
                    src, dst = src[:, half, :], dst[:, half, :]
                else:
                    c = int(name.lstrip("abcdefghijklmnopqrstuvwxyz"))
                    w = {"win": "w_in", "wout": "w_out", "wq": "peer_wq", "gate": "ple_gate_w"}[name.rstrip("0123456789")]
                    src = a[w][0].rearrange("(k p) n -> p k n", p=P)[:, :, c * WC:(c + 1) * WC]
                    dst = wbuf[:, b, :].rearrange("p (k n) -> p k n", k=KT)
                    if name.startswith("wq"):
                        dst = wbuf[:, b, :].rearrange("p (c k n) -> p c k n", c=2, k=KT)
                        src, dst = src[:, :, half * P:(half + 1) * P], dst[:, half]
                    else:
                        src, dst = src[:, half * KT // 2:(half + 1) * KT // 2, :], dst[:, half * KT // 2:(half + 1) * KT // 2, :]
                sp.dma_start(dst, src).then_inc(sig(f"w{b}{half}_loaded"), 16)

        def rows(i):
            return "s" if isinstance(i, int) and i == NB else "p"

        def tok(i, ap):
            if rows(i) == "s":
                return ap[0:NS, :]
            return ap[i * P:(i + 1) * P, :] if isinstance(i, int) else ap[bass.ds(i * P, P), :]

        def bc(ap, shape, axis):
            return ap.unsqueeze(axis).to_broadcast(shape)

        def by_turns(first, second):
            programs = [first, second]
            names = [next(program, None) for program in programs]
            while any(names):
                k = min((BOTH_STAGES.index(name), k) for k, name in enumerate(names) if name)[1]
                yield names[k]
                names[k] = next(programs[k], None)

        def play(program, stages):
            at = next(program, None)
            for name in stages:
                while at == name:
                    at = next(program, None)
                yield
            assert at is None, at

        def drive(front, tail, expert, finish, handoff, peer_sample, eng):
            def iteration(i, has_tail, has_peer):
                handoff(i)
                if has_tail:
                    names = BOTH_STAGES
                    run = play(by_turns(tail(i), front(i)), names)
                else:
                    names = FRONT_STAGES
                    run = play(front(i), names)
                before = [sum(stage_weight(name) for name in names[:k]) for k in range(len(names))]
                span = before[-1] + stage_weight(names[-1])
                total, done = len(names), 0
                if has_peer:
                    for k in range(HK):
                        expert(i, k // UNIT, k % UNIT)
                        while done < total and before[done] * SPREAD < (k + 1) * span:
                            next(run)
                            done += 1
                for _ in run:
                    done += 1
                assert done == total
                if has_peer:
                    finish(i)
            iteration(0, False, False)
            iteration(1, False, True)
            with eng.Fori(2, NB) as i:
                iteration(i, True, True)
            iteration(NB, True, True)
            handoff(NB + 1)
            run = play(tail(NB + 1), TAIL_STAGES)
            for name in TAIL_STAGES:
                if name == "gate0" and eng is not nc.tensor:
                    peer_sample()
                next(run)
            if eng is nc.tensor:
                peer_sample()
            for _ in play(tail(NB + 2), TAIL_STAGES):
                pass

        def xn_gate(c):
            return feat[:, c // 2, (c % 2) * WC:(c % 2 + 1) * WC]

        def query(h):
            return xm[:, (h % 2) * 256:(h % 2) * 256 + 256].rearrange("p (c t) -> p c t", c=2)

        block = ctx.enter_context(nc.Block())

        @block.sync
        def _(sp):
            eng_name[id(sp)] = "sp"

            def hold(s, value):
                sp.wait_ge(s, value)
                if not isinstance(value, int):
                    settle(sp)

            sp.dma_start(vring[:, 1:3, 0:P], a["peer_subkeys"][0].rearrange("c n d -> n c d")).then_inc(sig("raw_loaded"), 16)
            sp.dma_start(pa[:, 0:H * P].rearrange("p (g j) -> p g j", g=H), a["cmlp_ws"][0].rearrange("g i j -> i g j")).then_inc(sig("raw_loaded"), 16)
            sp.dma_start(vring[0:KT, 0, 0:P], a["norm_mix_g"][0].rearrange("(k p) -> k p", p=P)).then_inc(sig("raw_loaded"), 16)
            sp.dma_start(vring[0:KT, 0, P:2 * P], a["norm_ple_g"][0].rearrange("(k p) -> k p", p=P)).then_inc(sig("raw_loaded"), 16)
            sp.dma_start(vring[0:KT, 0, 2 * P:3 * P], a["cmlp_bs"][0]).then_inc(sig("raw_loaded"), 16)
            def load_params():
                s_par = sig("params_loaded")
                sp.dma_start(w2[:, :], a["rwkv_w2"][0]).then_inc(s_par, 16)
                sp.dma_start(a2[:, :], a["rwkv_a2"][0]).then_inc(s_par, 16)
                sp.dma_start(g2[:, :], a["rwkv_g2"][0]).then_inc(s_par, 16)
                sp.dma_start(ws00[:, :], a["cmlp_ws"][0, :, 0, 0:1].rearrange("g a -> a g").partition_broadcast(NS).rearrange("p a g -> p (a g)"),
                             allow_slow_non_contiguous=True).then_inc(s_par, 16)
                sp.dma_start(bs00[:, :], a["cmlp_bs"][0, :, 0:1].rearrange("g a -> a g").partition_broadcast(NS).rearrange("p a g -> p (a g)"),
                             allow_slow_non_contiguous=True).then_inc(s_par, 16)
                for nm in bcast_names:
                    src = a[nm][0].rearrange("h d -> (h d)") if nm == "rwkv_r_k" else a[nm][0]
                    sp.dma_start(par[nm][:, :], src.partition_broadcast(P)).then_inc(s_par, 16)

            hold(sig("zero_row"), 1)
            sp.dma_start(proj_s[0:1, :], xm[0:1, :]).then_inc(sig("zero_stored"), 16)

            def load_x(i):
                n = NS if rows(i) == "s" else P
                sp.dma_start(z[0:n, :], tok(i, x_dram[rows(i)])).then_inc(sig("x_loaded"), 16)

            def front(i):
                n = NS if rows(i) == "s" else P
                if isinstance(i, int) and i < 2:
                    load_w(sp, i, "win0")
                    load_w(sp, i, "win1")
                    if i:
                        hold(sig("handed"), i)
                    load_x(i)
                    if i == 0:
                        load_params()
                for c in range(2, 9):
                    load_w(sp, i, f"win{c}")
                if not isinstance(i, int) or i >= 2:
                    hold(sig("y_stored"), 16 * (i - 1))
                wait_pos(sp, sig("topk_done"), i)
                sp.dma_start(mu, a["shift_mu"][0].partition_broadcast(P)).then_inc(sig("mu_loaded"), 16)
                hold(sig("proj_ready"), i + 1)
                if rows(i) == "p":
                    at = lambda k: proj_s[k:k + 1, :] if isinstance(i, int) else proj_s[bass.ds(k, 1), :]
                    sp.dma_start(xm[1:P, :], pa[0:P - 1, :]).then_inc(sig("prev_loaded"), 16)
                    sp.dma_start(at(i + 1), pa[P - 1:P, :]).then_inc(sig("proj_stored"), 16)
                    if isinstance(i, int) and i == 0:
                        hold(sig("zero_stored"), 16)
                    else:
                        hold(sig("proj_stored"), 16 * i)
                    sp.dma_start(xm[0:1, :], at(i)).then_inc(sig("prev_loaded"), 16)
                    load_w(sp, i, "win9")
                else:
                    sp.dma_start(shift_sample[0], pa[0:NS, :]).then_inc(sig("out_stored"), 16)
                    load_w(sp, i, "win9")
                    sp.dma_start(xm[0:NS, :], a["state_shift"][0]).then_inc(sig("prev_loaded"), 16)
                load_w(sp, i, "win10")
                if rows(i) == "s":
                    hold(sig("vn_ready"), i + 1)
                    sp.dma_start(chunk_v[0].rearrange("b s d -> (b s) d"), uv[0:NS, DA:D]).then_inc(sig("out_stored"), 16)
                if rows(i) == "s":
                    hold(sig("sfeat_ready"), 1)
                    for k, src in enumerate((xm[0:NS, 0:DA], feat[0:NS, F_KH, :], xm[0:NS, 2 * DA:3 * DA], feat[0:NS, F_PC, :], feat[0:NS, F_KK, :], feat[0:NS, F_A, :])):
                        sp.dma_start(feat_s[k], src).then_inc(sig("sfeat_stored"), 16)
                    hold(sig("sfeat_stored"), 96)
                    sp.dma_start(ms[0:64, 0, 0:384].rearrange("p (k d) -> p k d", k=6), feat_s.rearrange("k b (h d) -> (b h) k d", h=H)).then_inc(sig("sfeat_loaded"), 16)
                    for v4 in range(4):
                        if v4:
                            hold(sig("swkv_used"), v4)
                        sp.dma_start(ft[0:64, 0:2, :].rearrange("p a n -> p (a n)"), a["state_wkv"][0, :, :, 16 * v4:16 * v4 + 16, :].rearrange("b h v k -> (b h) (v k)")).then_inc(sig("swkv_loaded"), 16)
                        hold(sig("swkv_new"), v4 + 1)
                        sp.dma_start(wkv_sample[0, :, :, 16 * v4:16 * v4 + 16, :].rearrange("b h v k -> (b h) (v k)"), ft[0:64, 0:2, :].rearrange("p a n -> p (a n)")).then_inc(sig("swkv_stored"), 16)
                        hold(sig("swkv_stored"), 16 * v4 + 16)
                        sp.sem_inc(sig("swkv_used"), 1)
                    sp.dma_start(ysamp_s.rearrange("b (h d) -> (b h) d", h=H), ms[0:64, 1, 0:64]).then_inc(sig("sy_stored"), 16)
                    hold(sig("sy_stored"), 16)
                    sp.dma_start(yv[0:NS, :], ysamp_s).then_inc(sig("sy_loaded"), 16)
                hold(sig("wkv_done"), i + 1)
                load_w(sp, i, "wout0")
                load_w(sp, i, "wout1")
                sp.dma_start(x[0:n, :], tok(i, x_dram[rows(i)])).then_inc(sig("xres_loaded"), 16)
                load_w(sp, i, "wout2")
                load_w(sp, i, "wout3")
                load_w(sp, i, "wq0")
                load_w(sp, i, "wq1")
                hold(sig("gain_free"), i + 1)
                sp.dma_start(gain, a["norm_ffn_g"][0].partition_broadcast(P)).then_inc(sig("gain_loaded"), 16)
                hold(sig("x1_ready"), i + 1)
                sp.dma_start(x1_s[T_PROMPT:T_PROMPT + NS, :] if rows(i) == "s" else tok(i, x1_s), x[0:n, :]).then_inc(sig("x1_stored"), 16)
                for h in range(2, H):
                    load_w(sp, i, f"wq{h}")
                if rows(i) == "s":
                    hold(sig("xn2_ready"), i + 1)
                    sp.dma_start(xn2_s, xn2[0:NS, :]).then_inc(sig("sxn2_stored"), 16)
                hold(sig("x1_stored"), 16 * i + 16)
                hold(sig("x_norm_done"), i + 1)
                yield

            def tail(i):
                j = i - 2
                sample = isinstance(i, int) and j == NB
                n = NS if sample else P
                load_w(sp, i, "ple")
                load_w(sp, i, "gate0")
                src = x1_s[T_PROMPT:T_PROMPT + NS, :] if sample else tok(j, x1_s)
                sp.dma_start(x[0:n, :], src).then_inc(sig("x1_loaded"), 16)
                sp.dma_start(gain, a["norm_final_g"].partition_broadcast(P)).then_inc(sig("fgain_loaded"), 16)
                hold(sig("topk_done"), i if not isinstance(i, int) else min(i, NB + 1))
                sp.dma_start(ptile[0:n, :], tok(NB if sample else j, ple_dram["s" if sample else "p"])).then_inc(sig("p_loaded"), 16)
                load_w(sp, i, "gate1")
                if isinstance(i, int) and i == NB + 1:
                    yield "gate0"
                if not isinstance(i, int) or i <= NB:
                    hold(sig("bank1_filled"), count(i, "t_xT1")[1] + 1)
                    load_x(i)
                load_w(sp, i, "gate2")
                load_w(sp, i, "gate3")
                if not isinstance(i, int) or i <= NB:
                    load_w(sp, i, "win0")
                    load_w(sp, i, "win1")
                hold(sig("y_ready"), j + 1)
                sp.dma_start(tok(NB if sample else j, y_dram["s" if sample else "p"]), x[0:n, :]).then_inc(sig("y_stored"), 16)
                if isinstance(i, int) and i > NB:
                    hold(sig("y_stored"), 16 * j + 16)
                yield

            def peer_sample():
                hold(sig("sxn2_stored"), 16)
                hold(sig("vpe_used"), NB * PER_BLOCK[pe_experts])
                hold(sig("vve_used"), NB * PER_BLOCK[ve_experts])
                for t in range(NS):
                    sp.dma_start(vring[:, t, :], xn2_s[t].partition_broadcast(P)).then_inc(sig(f"sxt{t}_loaded"), 16)

            drive(front, tail, lambda i, n, j: None, lambda i: None, lambda i: None, peer_sample, sp)
            hold(sig("proj_stored"), 16 * NB)
            sp.dma_start(shift_prompt[0], proj_s[NB:NB + 1, :]).then_inc(sig("out_stored"), 16)
            hold(sig("wkv_rows"), 1)
            sp.dma_start(wkv_prompt[0, 0].rearrange("h v k -> v h k"), ms[0:64, 0, :].rearrange("v (h k) -> v h k", h=H)).then_inc(sig("out_stored"), 16)
            hold(sig("out_stored"), 16 * 4)

        @block.gpsimd
        def _(gp):
            eng_name[id(gp)] = "gp"
            steps = [0]

            def link(ins):
                steps[0] += 1
                ins.then_inc(sig("gp_step"), 1)
                gp.wait_ge(sig("gp_step"), steps[0])

            def select(out, pattern, base, mult, op=ALU.is_ge, fill=0.0):
                link(gp.affine_select(out=out, in_=out, compare_op=op, fill=fill, base=base, pattern=pattern, channel_multiplier=mult))

            link(gp.memset(xm[0:1, :], 0.0))
            gp.sem_inc(sig("zero_row"), 1)
            link(gp.memset(ident[:, :], 0.0))
            select(ident[:, :], [[-1, P]], 0, 1, ALU.not_equal, 1.0)
            link(gp.memset(diag8[:, :, :], 0.0))
            select(diag8[:, :, :], [[1, NS], [-1, NS]], 0, 0, ALU.not_equal, 1.0)
            for m, off in ((m_causal, 0), (m_incl, 0), (m_strict, -1)):
                link(gp.memset(m[:, :], 1.0))
                select(m[:, :], [[1, P]], off, -1)
                if m is not m_causal:
                    select(m[:, CH:P], [[0, CH]], -CH, 1)
            link(gp.memset(chunk_of[:, :], 1.0))
            select(chunk_of[:, 0:1], [[0, 1]], CH - 1, -1)
            select(chunk_of[:, 1:2], [[0, 1]], -CH, 1)
            link(gp.memset(m_level[:, :, :], 0.0))
            for m in range(LEVELS):
                w = 1 << m
                up = m_level[:, m, :].rearrange("p (b u w) -> p b u w", u=2, w=w)[:, :, 1, :]
                nb = P // (2 * w)
                link(gp.memset(up, 1.0))
                select(up, [[-2 * w, nb], [0, w]], 0, 1)
                select(up, [[2 * w, nb], [0, w]], w - 1, -1)
            link(gp.memset(m_pairT[:, :], 1.0))
            select(m_pairT[:, :].rearrange("p (b u) -> p b u", u=2)[:, :, 1], [[0, CH]], -1, 0)
            select(m_pairT[:, :], [[-1, P]], -1, 1, ALU.is_equal)
            link(gp.iota(iota_i[:, :], pattern=[[1, TOPK]], base=0, channel_multiplier=0))
            for k, value in enumerate((RMS_EPS, LN_EPS, GN_EPS)):
                link(gp.memset(eps[:, k:k + 1], value))
            gp.sem_inc(sig("consts_ready"), 1)

            def copy_idx(i, n):
                g = (i - 1) * UNITS + n
                if not isinstance(i, int) or i > 1 or n >= NI:
                    gp.wait_ge(sig("u_used"), (g - NI + 1) * UNIT)
                    gp.wait_ge(sig("vpe_used"), summed(pe_experts, i, n - NI))
                    settle(gp)
                    gp.wait_ge(sig("vve_used"), summed(ve_experts, i, n - NI))
                    settle(gp)
                at = ((i - 1) % 2) * HK + n * UNIT
                src = eidx[:, at:at + UNIT] if isinstance(i, int) else eidx[:, bass.ds(at, UNIT)]
                gp.tensor_copy(idx_c[:, n % NI, :], src).then_inc(sig("idx_copied"), 1)
                gp.wait_ge(sig("idx_copied"), g + 1)
                settle(gp)

            def gather_u(i, n, j):
                s = n % 2 * UNIT + j
                wait_pos(gp, sig("u_used"), (i - 1) * HK + n * UNIT + j - NU + 1)
                settle(gp)
                gp.indirect_dma_start(uring[:, s, :], None, peer_u, bass.IndirectOffsetOnAxis(ap=idx_c[:, n % NI, j:j + 1], axis=0)).then_inc(sig(f"u{s}_full"), 16)

            def gather_v(i, n, j):
                s = n % 2 * UNIT + j
                if not isinstance(i, int) or i > 1 or n >= 2:
                    if j in pe_experts((n - 2) % UNITS):
                        gp.wait_ge(sig("vpe_used"), summed(pe_experts, i, n - 2, j))
                    else:
                        gp.wait_ge(sig("vve_used"), summed(ve_experts, i, n - 2, j))
                    settle(gp)
                gp.indirect_dma_start(vring[:, s, :], None, peer_v, bass.IndirectOffsetOnAxis(ap=idx_c[:, n % NI, j:j + 1], axis=0)).then_inc(sig(f"v{s}_full"), 16)

            def expert(i, n, j):
                if n == 0 and j == 0:
                    gp.wait_ge(sig("topk_done"), i)
                    settle(gp)
                    copy_idx(i, 0)
                    for jj in range(UNIT):
                        gather_u(i, 0, jj)
                if n + 1 < UNITS:
                    if j == 0:
                        copy_idx(i, n + 1)
                    gather_u(i, n + 1, j)
                gather_v(i, n, j)

            def peer_sample():
                gp.wait_ge(sig("handed"), NB + 1)
                for t in range(NS):
                    gp.indirect_dma_start(uring[:, t, :], None, peer_u, bass.IndirectOffsetOnAxis(ap=sidx[:, t:t + 1], axis=0)).then_inc(sig(f"u{t}_full"), 16)
                for t in range(NS):
                    gp.wait_ge(sig("sxt_used"), t + 1)
                    gp.indirect_dma_start(vring[:, t, :], None, peer_v, bass.IndirectOffsetOnAxis(ap=sidx[:, t:t + 1], axis=0)).then_inc(sig(f"v{t}_full"), 16)

            def nothing(i):
                return
                yield

            drive(nothing, nothing, expert, lambda i: None, lambda i: None, peer_sample, gp)

        @block.tensor
        def _(pe):
            eng_name[id(pe)] = "pe"
            mm = nc.tensor.matmul

            def turn(out, in_):
                n = in_.shape[0]
                return nc.tensor.transpose(out, in_, ident[0:n, 0:n])

            pe.wait_ge(sig("consts_ready"), 1)
            pe.wait_ge(sig("raw_loaded"), 16 * 5)
            for c in range(2):
                last = turn(bank[0][:, c * P:(c + 1) * P], vring[:, 1 + c, 0:P])
            filled(0, "s_sk", last)
            for g in range(H):
                last = turn(bank[1 + g // 4][:, (g % 4) * P:(g % 4 + 1) * P], pa[:, g * P:(g + 1) * P])
                if g % 4 == 3:
                    filled(0, f"s_ws{g // 4}", last)
            for k in range(3):
                last = turn(bank[3][:, k * KT:(k + 1) * KT], vring[0:KT, 0, k * P:(k + 1) * P])
            filled(0, "s_vec", last)

            def turn_rows(i, use, src, n):
                for half in range(2):
                    b = take(pe, i, f"{use}{half}")
                    settle(pe)
                    for k in range(4):
                        last = turn(b[:, k * n:(k + 1) * n], src[0:n, (4 * half + k) * P:(4 * half + k + 1) * P])
                    filled(i, f"{use}{half}", last)

            def stream(i, name, n):
                b = take(pe, i, name)
                settle(pe)
                for half in range(2):
                    w, used = wchunk(pe, i, name, half)
                    w = w.rearrange("p (k n) -> p k n", k=KT)
                    for k in range(half * KT // 2, (half + 1) * KT // 2):
                        last = mm(b[0:n, 0:WC], xT[:, k, 0:n], w[:, k, :], start=(k == 0), stop=(k == KT - 1))
                    if half == 0:
                        last.then_inc(used, 1)
                filled(i, name, last)
                pe.wait_ge(sig(f"bank{bank_of(i, name)}_filled"), count(i, name)[1] + 1)
                pe.sem_inc(used, 1)

            def heads4(i, use, fn, g):
                b = take(pe, i, use)
                settle(pe)
                for h in range(4):
                    last = fn(b, h, 4 * g + h)
                filled(i, use, last)

            def front(i):
                n = NS if rows(i) == "s" else P
                prompt = rows(i) == "p"
                yield "turn"
                pe.wait_ge(sig("xn_ready"), i + 1)
                turn_rows(i, "xT", z, n)
                for c in range(11):
                    yield f"win{c}"
                    if c == 0:
                        after_read(pe, i, "xT0")
                        after_read(pe, i, "xT1")
                    stream(i, f"win{c}", n)
                yield "lora"
                if isinstance(i, int) and i == 0:
                    pe.wait_ge(sig("params_loaded"), 16 * (5 + len(bcast_names)))
                pe.wait_ge(sig("lora_in"), i + 1)
                b = take(pe, i, "loraT")
                settle(pe)
                turn(b[0:64, 0:n], xm[0:n, 3 * DA:3 * DA + 64])
                turn(b[0:64, P:P + n], xm[0:n, 3 * DA + 64:3 * DA + 128])
                last = turn(b[:, 2 * P:2 * P + n], xm[0:n, 3 * DA + 128:PA])
                filled(i, "loraT", last)
                after_read(pe, i, "loraT")
                for use, w, k, rank in (("w_lora", w2, 0, 64), ("a_lora", a2, 1, 64), ("g_lora", g2, 2, P)):
                    b = take(pe, i, use)
                    settle(pe)
                    filled(i, use, mm(b[0:n, :], loraT[0:rank, k, 0:n], w[:, :], start=True, stop=True))
                if prompt:
                    yield "kk"
                    pe.wait_ge(sig("vn_ready"), i + 1)
                    b = take(pe, i, "spatial")
                    settle(pe)
                    for g in range(H):
                        last = mm(b[:, g * HD:(g + 1) * HD], wsT[:, g, :], uv[:, DA + g * HD:DA + (g + 1) * HD], start=True, stop=True)
                    filled(i, "spatial", last)
                    yield "bonus"
                    pe.wait_ge(sig("lw_ready"), i + 1)
                    b = take(pe, i, "cum")
                    settle(pe)
                    filled(i, "cum", mm(b[:, :], m_incl[:, :], feat[:, F_LW, :], start=True, stop=True))
                    b = take(pe, i, "pl")
                    settle(pe)
                    for h in range(H):
                        last = mm(b[0:64, 2 * h:2 * h + 2], feat[:, F_LW, h * HD:(h + 1) * HD], chunk_of[:, :], start=True, stop=True)
                    filled(i, "pl", last)
                    yield from by_turns(half(i, 0), half(i, 1))
                yield "gn_gate"
                pe.wait_ge(sig("z_ready"), i + 1)
                turn_rows(i, "zT", z, n)
                for c in range(4):
                    yield f"wout{c}"
                    if c == 0:
                        after_read(pe, i, "zT0")
                        after_read(pe, i, "zT1")
                    stream(i, f"wout{c}", n)
                yield "x2T"
                pe.wait_ge(sig("xn2_ready"), i + 1)
                turn_rows(i, "x2T", xn2, n)
                for h in range(H + 1):
                    yield f"q{h}"
                    if h == 0:
                        after_read(pe, i, "x2T0")
                        after_read(pe, i, "x2T1")
                    if h < H:
                        b = take(pe, i, f"q{h}")
                        settle(pe)
                        for c in range(2):
                            w, used = wchunk(pe, i, f"wq{h}", c)
                            w = w.rearrange("p (c k n) -> p c k n", c=2, k=KT)
                            for k in range(KT):
                                last = mm(b[:, c * P:c * P + n], w[:, c, k, :], xT[:, k, 0:n], start=(k == 0), stop=(k == KT - 1))
                            if c == 0:
                                last.then_inc(used, 1)
                        filled(i, f"q{h}", last)
                        pe.wait_ge(sig(f"bank{bank_of(i, f'q{h}')}_filled"), count(i, f"q{h}")[1] + 1)
                        pe.sem_inc(used, 1)
                    if h:
                        keys(i, h - 1, n)
                if not prompt:
                    yield "expert"
                    pe.wait_ge(sig("topk_done"), i + 1)
                    b = take(pe, i, "eT")
                    turn(b[:, 0:NS], e1[0:NS, :])
                    filled(i, "eT", turn(b[:, NS:2 * NS], gate[0:NS, :]))

            def keys(i, h, n):
                after_read(pe, i, f"q{h}")
                b = take(pe, i, f"sc{h}")
                settle(pe)
                for c in range(2):
                    last = mm(b[0:n, c * NK:(c + 1) * NK], query(h)[:, c, 0:n], skT[:, c, :], start=True, stop=True)
                filled(i, f"sc{h}", last)

            def half(i, g):
                hd = lambda ap, h: ap[:, h * P:(h + 1) * P]
                hv = lambda ap, h: ap[:, h * HD:(h + 1) * HD]
                yield f"h{g}_turn"
                pe.wait_ge(sig("hats_ready"), i + 1)
                for kind, src in (("aT", F_PX), ("bT", F_A), ("kT", F_PI), ("rT", F_PC)):
                    heads4(i, f"{kind}{g}", lambda b, h, hh: turn(b[0:64, h * P:(h + 1) * P], hv(feat[:, src, :], hh)), g)
                A, B, K, R = hatsT[g]
                TTg, TIg, XXg = TT[g], TI[g], XX[g]
                SMg = sms[g]
                product = lambda use, l, r: heads4(i, f"{use}{g}", lambda b, h, hh: mm(hd(b, h), hd(l, h), hd(r, h), start=True, stop=True), g)
                yield f"h{g}_products"
                for nm in ("aT", "bT", "kT", "rT"):
                    after_read(pe, i, f"{nm}{g}")
                product("MT", B, A)
                product("M", A, B)
                yield f"h{g}_TT"
                product("MakT", K, A)
                yield f"h{g}_TI"
                product("MrbT", B, R)
                v = xm[:, 2 * DA:3 * DA]
                for m in range(1, LEVELS):
                    yield f"h{g}_merge{m}"
                    pe.wait_ge(sig(f"CT{g}_ready"), (LEVELS - 1) * i + m)
                    heads4(i, f"X{g}{m}", lambda b, h, hh: mm(hd(b, h), hd(CT[g], h), hd(TIg, h), start=True, stop=True), g)
                    after_read(pe, i, f"X{g}{m}")
                    heads4(i, f"TXt{g}{m}", lambda b, h, hh: mm(hd(b, h), hd(XXg, h), hd(TTg, h), start=True, stop=True), g)
                    if m < LEVELS - 1:
                        heads4(i, f"TX{g}{m}", lambda b, h, hh: mm(hd(b, h), hd(TTg, h), hd(XXg, h), start=True, stop=True), g)
                    if m == 2:
                        product("MrkT", K, R)
                    if m == 4:
                        after_read(pe, i, f"MakT{g}")
                        heads4(i, f"U0{g}", lambda b, h, hh: mm(hv(b, h), hd(MakT[g], h), hv(v, hh), start=True, stop=True), g)
                yield f"h{g}_solve"
                after_read(pe, i, f"U0{g}")
                after_read(pe, i, f"TXt{g}{LEVELS - 1}")
                heads4(i, f"U1{g}", lambda b, h, hh: mm(hv(b, h), hd(TTg, h), hv(SMg[:, 0, :], h), start=True, stop=True), g)
                heads4(i, f"WT{g}", lambda b, h, hh: mm(hd(b, h)[0:64, :], hv(feat[:, F_PX, :], hh), hd(TTg, h), start=True, stop=True), g)
                for q in range(2):
                    yield f"h{g}_SR{q}"
                    if q == 0:
                        after_read(pe, i, f"WT{g}")
                    pe.wait_ge(sig(f"ST{g}_ready"), 2 * i + q + 1)
                    b = take(pe, i, f"SR{g}{q}")
                    settle(pe)
                    for h in range(4):
                        mm(hv(b, h), hd(wTs[g], h), ST[:, 4 * g + h, :], start=True, stop=True)
                    for h in range(4):
                        last = mm(hv(b, 4 + h), hd(R, h), ST[:, 4 * g + h, :], start=True, stop=True)
                    filled(i, f"SR{g}{q}", last)
                    yield f"h{g}_dS{q}"
                    pe.wait_ge(sig("v01_ready"), 2 * i + 2)
                    after_read(pe, i, f"SR{g}{q}")
                    b = take(pe, i, f"dS{g}{q}")
                    settle(pe)
                    for h in range(4):
                        hh = 4 * g + h
                        mm(hv(b, h)[0:64, :], hv(feat[:, F_A, :], hh), hv(SMg[:, 2 + q, :], h), start=True, stop=False)
                        last = mm(hv(b, h)[0:64, :], hv(feat[:, F_PI, :], hh), hv(feat[:, V0 if q == 0 else V1, :], hh), start=False, stop=True)
                    filled(i, f"dS{g}{q}", last)
                after_read(pe, i, f"MrkT{g}")
                b = take(pe, i, f"Y{g}")
                settle(pe)
                for h in range(4):
                    hh = 4 * g + h
                    mm(hv(b, h), hd(MrbT[g], h), hv(SMg[:, 2, :], h), start=True, stop=False)
                    mm(hv(b, h), hd(MrbT[g], h), hv(SMg[:, 3, :], h), start=False, stop=False)
                    last = mm(hv(b, h), hd(MrkT[g], h), hv(v, hh), start=False, stop=True)
                filled(i, f"Y{g}", last)

            def tail(i):
                j = i - 2
                n = NS if isinstance(i, int) and j == NB else P
                yield "t_norm"
                pe.wait_ge(sig("p_loaded"), 16 * j + 16)
                b = take(pe, i, "t_pT")
                settle(pe)
                turn(b[:, 0:n], ptile[0:n, 0:P])
                filled(i, "t_pT", turn(b[:, P:P + n], ptile[0:n, P:2 * P]))
                after_read(pe, i, "t_pT")
                w, used0 = wchunk(pe, i, "ple", 0)
                w, used1 = wchunk(pe, i, "ple", 1)
                w = w.rearrange("p (k n) -> p k n", k=2)
                for c in range(2):
                    b = take(pe, i, f"ple{c}")
                    settle(pe)
                    for k in range(2):
                        last = mm(b[0:n, :], loraT[:, k, 0:n], w[:, k, c * 512:(c + 1) * 512], start=(k == 0), stop=(k == 1))
                    filled(i, f"ple{c}", last)
                pe.wait_ge(sig("bank3_filled"), count(i, "ple1")[1] + 1)
                pe.sem_inc(used0, 1)
                pe.sem_inc(used1, 1)
                yield "t_turn"
                pe.wait_ge(sig("t_xn_ready"), j + 1)
                turn_rows(i, "t_xT", z, n)
                for c in range(4):
                    yield f"gate{c}"
                    if c == 0:
                        after_read(pe, i, "t_xT0")
                        after_read(pe, i, "t_xT1")
                    stream(i, f"gate{c}", n)

            def sum_v(i, n, j):
                s = n % 2 * UNIT + j
                at = pe_experts(n).index(j)
                pe.wait_ge(sig("diag_ready"), (i - 1) * UNITS + n + 1)
                pe.wait_ge(sig(f"v{s}_full"), 16 * ((i - 1) * (UNITS // 2) + n // 2 + 1))
                for c in range(2):
                    last = mm(acc[c][:, :], dg[:, n % 2, at, :], vring[:, s, c * 512:(c + 1) * 512],
                              start=(n + at == 0), stop=(n == UNITS - 1 and j == pe_experts(n)[-1]))
                last.then_inc(sig("vpe_used"), 1)

            def expert(i, n, j):
                if n == 1 and j == 0:
                    wait_pos(pe, sig("acc_read"), i - 1)
                    settle(pe)
                if n and j - 1 in pe_experts(n - 1):
                    sum_v(i, n - 1, j - 1)
                if n and j == UNIT - 1 and j in pe_experts(n - 1):
                    sum_v(i, n - 1, j)

            def finish(i):
                for j in pe_experts(UNITS - 1):
                    sum_v(i, UNITS - 1, j)

            def peer_sample():
                pe.wait_ge(sig("acc_read"), NB)
                pe.wait_ge(sig("diag_ready"), NB * UNITS + 1)
                for t in range(NS):
                    pe.wait_ge(sig(f"v{t}_full"), 16 * (NB * (UNITS // 2) + 1))
                    for c in range(2):
                        last = mm(acc[c][0:NS, :], sdg[:, t, :], vring[:, t, c * 512:(c + 1) * 512], start=(t == 0), stop=(t == NS - 1))
                last.then_inc(sig("sample_summed"), 1)

            drive(front, tail, expert, finish, lambda i: None, peer_sample, pe)
            pe.wait_ge(sig("ST0_ready"), NB * 2 + 1)
            pe.wait_ge(sig("ST1_ready"), NB * 2 + 1)
            pe.wait_ge(sig("bank1_read"), count(NB + 2, "gate3")[1] + 1)
            for h in range(H):
                last = turn(bank[1][0:64, h * HD:(h + 1) * HD], ST[:, h, :])
            last.then_inc(sig("wkv_turned"), 1)

        @block.scalar
        def _(act):
            eng_name[id(act)] = "act"
            steps = [0]

            def fn(out, in_, f, **kw):
                return nc.scalar.activation(out, in_, f, **kw)

            def link(ins):
                steps[0] += 1
                ins.then_inc(sig("act_step"), 1)
                act.wait_ge(sig("act_step"), steps[0])

            def restart():
                if steps[0]:
                    act.wait_ge(sig("act_step"), steps[0])
                    settle(act)
                    act.sem_clear(sig("act_step"))
                steps[0] = 0

            def evac(i, use, dst, cols, parts=P, f=ACT.Copy, **kw):
                b = see(act, i, use)
                has_read(i, use, fn(dst, b[0:parts, 0:cols], f, **kw))

            act.wait_ge(sig("consts_ready"), 1)

            def sqrt_of(i, name, src, dst, **kw):
                act.wait_ge(sig(name + "_var"), i)
                fn(dst, src, ACT.Sqrt, **kw).then_inc(sig(name + "_root"), 1)

            def rms_root(name, n, col, x=x):
                link(fn(ft[0:n, 0:2, :].rearrange("p a n -> p (a n)"), x[0:n, :], ACT.Square, accum_out=st[0:n, col:col + 1]))
                fn(st[0:n, col + 1:col + 2], st[0:n, col:col + 1], ACT.Sqrt, scale=1.0 / D, bias=eps[0:n, 0:1]).then_inc(sig(name + "_root"), 1)

            def front(i):
                n = NS if rows(i) == "s" else P
                prompt = rows(i) == "p"
                yield "norm"
                wait_pos(act, sig("handed"), i)
                act.wait_ge(sig("x_loaded"), 16 * i + 16)
                rms_root("n1", n, 0, z)
                yield "turn"
                act.wait_ge(sig("n1_rs"), i + 1)
                fn(z[0:n, :], z[0:n, :], ACT.Copy, scale=st[0:n, 2:3]).then_inc(sig("xn_ready"), 1)
                for c in range(11):
                    yield f"win{c}"
                    if c == 0:
                        wait_pos(act, sig("gain_used"), i)
                        if not isinstance(i, int) or i >= 2:
                            act.wait_ge(sig("y_ready"), i - 1)
                    if c < 7:
                        evac(i, f"win{c}", pa[0:n, c * WC:(c + 1) * WC], WC, n)
                    else:
                        evac(i, f"win{c}", uv[0:n, (c - 7) * WC:(c - 6) * WC], WC, n, ACT.Gelu)
                    if c == 6:
                        act.wait_ge(sig("bank0_read"), count(i, "win6")[1] + 1)
                        act.wait_ge(sig("bank1_read"), count(i, "win5")[1] + 1)
                        act.sem_inc(sig("proj_ready"), 1)
                act.wait_ge(sig("bank0_read"), count(i, "win10")[1] + 1)
                act.wait_ge(sig("bank1_read"), count(i, "win9")[1] + 1)
                act.sem_inc(sig("uv_ready"), 1)
                yield "lora"
                act.wait_ge(sig("xm_ready"), i + 1)
                link(fn(xm[0:n, 3 * DA:3 * DA + 64], xm[0:n, 3 * DA:3 * DA + 64], ACT.Tanh))
                fn(xm[0:n, 3 * DA + 128:PA], xm[0:n, 3 * DA + 128:PA], ACT.Sigmoid).then_inc(sig("lora_in"), 1)
                b = see(act, i, "loraT")
                link(fn(loraT[0:64, 0:2, 0:n], b[0:64, 0:2 * P].rearrange("p (k t) -> p k t", k=2)[:, :, 0:n], ACT.Copy))
                has_read(i, "loraT", fn(loraT[:, 2, 0:n], b[:, 2 * P:2 * P + n], ACT.Copy))
                yield "ln_root"
                sqrt_of(i + 1, "ln", st[0:n, 16:24], st[0:n, 24:32], scale=1.0 / HD, bias=eps[0:n, 1:2])
                yield "lora_add"
                act.wait_ge(sig("wz_ready"), i + 1)
                fn(feat[0:n, F_LW, :], feat[0:n, F_LW, :], ACT.Sigmoid).then_inc(sig("w_sig"), 1)
                act.wait_ge(sig("az_ready"), i + 1)
                fn(feat[0:n, F_A, :], feat[0:n, F_A, :], ACT.Sigmoid).then_inc(sig("a_sig"), 1)
                evac(i, "g_lora", feat[0:n, F_G, :], DA, n)
                yield "kk"
                sqrt_of(i + 1, "kk", st[0:n, 32:40], st[0:n, 40:48])
                yield "cum"
                if prompt:
                    act.wait_ge(sig("cex_ready"), i + 1)
                    b = see(act, i, "cum")
                    link(fn(feat[:, F_PC, :], b[:, :], ACT.Exp))
                    has_read(i, "cum", fn(feat[:, F_PI, :], b[:, :], ACT.Exp, scale=-1.0))
                    link(fn(feat[:, F_PX, :], feat[:, F_PX, :], ACT.Exp))
                    b = see(act, i, "pl")
                    has_read(i, "pl", fn(PL[:, :, :].rearrange("p h q -> p (h q)"), b[0:64, 0:2 * H], ACT.Exp))
                    act.wait_ge(sig("bank4_read"), count(i, "cum")[1] + 1)
                    act.sem_inc(sig("exps_ready"), 1)
                    yield "masked_v"
                    act.wait_ge(sig("hats_ready"), i + 1)
                    fn(feat[0:64, V0, :], xm[0:64, 2 * DA:3 * DA], ACT.Copy)
                    fn(feat[64:128, V1, :], xm[64:128, 2 * DA:3 * DA], ACT.Copy).then_inc(sig("v01_ready"), 1)
                    yield from by_turns(half(i, 0), half(i, 1))
                else:
                    act.wait_ge(sig("lw_ready"), i + 1)
                    fn(feat[0:n, F_PC, :], feat[0:n, F_LW, :], ACT.Exp).then_inc(sig("exps_ready"), 1)
                yield "gn_root"
                sqrt_of(i + 1, "gn", st[0:n, 16:24], st[0:n, 24:32], scale=1.0 / HD, bias=eps[0:n, 2:3])
                yield "gn_gate"
                for k in range(2):
                    b = see(act, i, f"zT{k}")
                    has_read(i, f"zT{k}", fn(xT[:, 4 * k:4 * k + 4, 0:n], b[:, 0:4 * n].rearrange("p (k t) -> p k t", k=4), ACT.Copy))
                yield "norm2"
                act.wait_ge(sig("x1_ready"), i + 1)
                rms_root("n2", n, 3)
                yield "x2T"
                for k in range(2):
                    b = see(act, i, f"x2T{k}")
                    has_read(i, f"x2T{k}", fn(xT[:, 4 * k:4 * k + 4, 0:n], b[:, 0:4 * n].rearrange("p (k t) -> p k t", k=4), ACT.Copy))
                for h in range(H + 1):
                    yield f"q{h}"
                    if h < H:
                        b = see(act, i, f"q{h}")
                        has_read(i, f"q{h}", fn(query(h)[:, :, 0:n], b[:, 0:2 * P].rearrange("p (c t) -> p c t", c=2)[:, :, 0:n], ACT.Copy))
                    if h:
                        evac(i, f"sc{h - 1}", sc_all[0:n, (h - 1) * 256:h * 256], 256, n)
                yield "soft"
                act.wait_ge(sig("cv_ready"), i + 1)
                fn(gate[0:n, :], cv[0:n, :], ACT.Exp).then_inc(sig("cv_exp"), 1)
                restart()

            def half(i, g):
                yield f"h{g}_turn"
                for k, kind in enumerate(("aT", "bT", "kT", "rT")):
                    evac(i, f"{kind}{g}", hatsT[g][k], 512, 64)
                for m in range(1, LEVELS):
                    yield f"h{g}_merge{m}"
                    evac(i, f"X{g}{m}", XX[g], 512)
                    if m == 4:
                        evac(i, f"U0{g}", sms[g][:, 0, :], 256)
                yield f"h{g}_solve"
                evac(i, f"U1{g}", sms[g][:, 1, :], 256)
                evac(i, f"WT{g}", wTs[g], 512, 64)

            def tail(i):
                j = i - 2
                n = NS if isinstance(i, int) and j == NB else P
                yield "t_norm"
                act.wait_ge(sig("x2_ready"), j + 1)
                rms_root("n3", n, 6)
                b = see(act, i, "t_pT")
                has_read(i, "t_pT", fn(loraT[:, 0:2, 0:n], b[:, 0:2 * P].rearrange("p (k t) -> p k t", k=2)[:, :, 0:n], ACT.Copy))
                evac(i, "ple0", uv[0:n, 0:512], 512, n)
                evac(i, "ple1", uv[0:n, 512:1024], 512, n)
                yield "t_turn"
                act.wait_ge(sig("n3_rs"), j + 1)
                fn(z[0:n, :], x[0:n, :], ACT.Copy, scale=st[0:n, 8:9]).then_inc(sig("t_xn_ready"), 1)
                for c in range(4):
                    yield f"gate{c}"
                    evac(i, f"gate{c}", xn_gate(c)[0:n, :], WC, n, ACT.Sigmoid)
                yield "y_norm"
                act.wait_ge(sig("x3_ready"), j + 1)
                rms_root("n4", n, 9)
                restart()

            def expert(i, n, j):
                if j == 0 and n:
                    diagonals(i, n - 1)
                if j == UNIT - 1:
                    act.wait_ge(sig("u_used"), (i - 1) * HK + (n + 1) * UNIT)
                    fn(pg[:, n % 2, :], ph[:, n % 2, :], ACT.Gelu).then_inc(sig("gelu_ready"), 1)

            def diagonals(i, n):
                act.wait_ge(sig("act_ready"), (i - 1) * UNITS + n + 1)
                if not isinstance(i, int) or i > 1 or n >= 2:
                    act.wait_ge(sig("vpe_used"), summed(pe_experts, i, n - 2))
                for at, j in enumerate(pe_experts(n)):
                    last = fn(dg[:, n % 2, at, :], ident[:, :], ACT.Copy, scale=pact[:, n % 2, j:j + 1])
                last.then_inc(sig("diag_ready"), 1)

            def peer_sample():
                act.wait_ge(sig("sxt_used"), NS)
                fn(pg[:, :, :].rearrange("p a b -> p (a b)"), ph[:, :, :].rearrange("p a b -> p (a b)"), ACT.Gelu).then_inc(sig("gelu_ready"), 1)

            drive(front, tail, expert, lambda i: diagonals(i, UNITS - 1), lambda i: None, peer_sample, act)
            act.wait_ge(sig("wkv_turned"), 1)
            fn(ms[0:64, 0, :], bank[1][0:64, :], ACT.Copy).then_inc(sig("wkv_rows"), 1)

        @block.vector
        def _(ve):
            eng_name[id(ve)] = "ve"
            steps = [0]
            v = nc.vector

            def link(ins):
                steps[0] += 1
                ins.then_inc(sig("ve_step"), 1)
                ve.wait_ge(sig("ve_step"), steps[0])

            def restart():
                if steps[0]:
                    ve.wait_ge(sig("ve_step"), steps[0])
                    settle(ve)
                    ve.sem_clear(sig("ve_step"))
                steps[0] = 0

            tt = v.tensor_tensor
            stt = v.scalar_tensor_tensor

            ve.wait_ge(sig("consts_ready"), 1)
            link(v.tensor_copy(iota16[:, :], iota_i[:, :]))
            b = see(ve, 0, "s_sk")
            has_read(0, "s_sk", v.tensor_copy(skT[:, :, :].rearrange("p c n -> p (c n)"), b[:, 0:2 * NK]))
            for k in range(2):
                b = see(ve, 0, f"s_ws{k}")
                has_read(0, f"s_ws{k}", tt(wsT[:, 4 * k:4 * k + 4, :], b[:, :].rearrange("p (g t) -> p g t", g=4), bc(m_causal[:, :], [P, 4, P], 1), ALU.mult))
            b = see(ve, 0, "s_vec")
            has_read(0, "s_vec", v.tensor_copy(vecs[:, :, :].rearrange("p a k -> p (a k)"), b[:, 0:3 * KT]))
            ve.wait_ge(sig("bank3_read"), 1)
            ve.wait_ge(sig("bank2_read"), 1)
            link(v.memset(ST[:, :, :], 0.0))
            ve.sem_inc(sig("ST0_ready"), 1)
            ve.sem_inc(sig("ST1_ready"), 1)
            link(v.memset(sm[:, 2:4, :], 0.0))
            restart()

            def root_to_scale(name, i, n, col):
                ve.wait_ge(sig(name + "_root"), i)
                return v.reciprocal(st[0:n, col + 2:col + 3], st[0:n, col + 1:col + 2])

            def group_norm(name, i, n, src, dst, g, b):
                s3 = lambda ap: ap.rearrange("p (h d) -> p h d", h=H)
                yield f"{name}_mean"
                if name == "ln":
                    ve.wait_ge(sig("uv_ready"), i)
                elif isinstance(i, int) and i == NB + 1:
                    ve.wait_ge(sig("sy_loaded"), 16)
                link(v.tensor_reduce(st[0:n, 48:56], s3(src), AX.X, ALU.add))
                link(v.tensor_scalar(st[0:n, 48:56], st[0:n, 48:56], 1.0 / HD, None, ALU.mult))
                link(tt(s3(dst), s3(src), bc(st[0:n, 48:56], [n, H, HD], 2), ALU.subtract))
                yield f"{name}_var"
                link(tt(scr(0)[0:n, :], dst, dst, ALU.mult))
                v.tensor_reduce(st[0:n, 16:24], s3(scr(0)[0:n, :]), AX.X, ALU.add).then_inc(sig(name + "_var"), 1)
                yield f"{name}_scale"
                ve.wait_ge(sig(name + "_root"), i)
                link(v.reciprocal(st[0:n, 24:32], st[0:n, 24:32]))
                link(tt(s3(dst), s3(dst), bc(st[0:n, 24:32], [n, H, HD], 2), ALU.mult))
                link(tt(dst, dst, par[g][0:n, :], ALU.mult))
                link(tt(dst, dst, par[b][0:n, :], ALU.add))

            def front(i):
                n = NS if rows(i) == "s" else P
                prompt = rows(i) == "p"
                f = lambda k: feat[0:n, k, :]
                r, k_, v_ = (xm[0:n, c * DA:(c + 1) * DA] for c in range(3))
                s3 = lambda ap: ap.rearrange("p (h d) -> p h d", h=H)
                yield "turn"
                root_to_scale("n1", i + 1, n, 0).then_inc(sig("n1_rs"), 1)
                yield "xT"
                for k in range(2):
                    b = see(ve, i, f"xT{k}")
                    has_read(i, f"xT{k}", tt(xT[:, 4 * k:4 * k + 4, 0:n], b[:, 0:4 * n].rearrange("p (k t) -> p k t", k=4),
                                             bc(vecs[:, KM, 4 * k:4 * k + 4], [P, 4, n], 2), ALU.mult))
                yield "shift0"
                ve.wait_ge(sig("prev_loaded"), 32 * i + (32 if prompt else 16))
                if prompt:
                    ve.wait_ge(sig("proj_stored"), 16 * i + 16)
                ve.wait_ge(sig("proj_ready"), i + 1)
                link(tt(xm[0:n, :], xm[0:n, :], pa[0:n, :], ALU.subtract))
                yield "shift1"
                ve.wait_ge(sig("mu_loaded"), 16 * i + 16)
                link(tt(xm[0:n, :], xm[0:n, :], mu[0:n, :], ALU.mult))
                yield "shift2"
                tt(xm[0:n, :], xm[0:n, :], pa[0:n, :], ALU.add).then_inc(sig("xm_ready"), 1)
                yield from group_norm("ln", i + 1, n, uv[0:n, DA:D], uv[0:n, DA:D], "cmlp_ln_g", "cmlp_ln_b")
                ve.sem_inc(sig("vn_ready"), 1)
                yield "lora_add"
                ve.wait_ge(sig("xm_ready"), i + 1)
                b = see(ve, i, "w_lora")
                has_read(i, "w_lora", tt(f(F_LW), b[0:n, :], par["rwkv_w0"][0:n, :], ALU.add))
                after_read(ve, i, "w_lora")
                ve.sem_inc(sig("wz_ready"), 1)
                b = see(ve, i, "a_lora")
                has_read(i, "a_lora", tt(f(F_A), b[0:n, :], par["rwkv_a0"][0:n, :], ALU.add))
                after_read(ve, i, "a_lora")
                ve.sem_inc(sig("az_ready"), 1)
                yield "kk"
                link(tt(f(F_KK), k_, par["rwkv_k_k"][0:n, :], ALU.mult))
                link(tt(scr(0)[0:n, :], f(F_KK), f(F_KK), ALU.mult))
                v.tensor_reduce(st[0:n, 32:40], s3(scr(0)[0:n, :]), AX.X, ALU.add).then_inc(sig("kk_var"), 1)
                yield "gmlp"
                ve.wait_ge(sig("w_sig"), i + 1)
                v.tensor_scalar(f(F_LW), f(F_LW), -math.exp(-0.5), None, ALU.mult).then_inc(sig("lw_ready"), 1)
                if prompt:
                    b = see(ve, i, "spatial")
                    has_read(i, "spatial", tt(s3(scr(1)), s3(b[:, :]), bc(vecs[:, KO, :], [P, H, HD], 2), ALU.add))
                    after_read(ve, i, "spatial")
                else:
                    link(tt(s3(scr(1)[0:n, :]), s3(uv[0:n, DA:D]), bc(ws00[:, :], [n, H, HD], 2), ALU.mult))
                    link(tt(s3(scr(1)[0:n, :]), s3(scr(1)[0:n, :]), bc(bs00[:, :], [n, H, HD], 2), ALU.add))
                link(tt(z[0:n, DA:D], uv[0:n, 0:DA], scr(1)[0:n, :], ALU.mult))
                yield "key"
                ve.wait_ge(sig("a_sig"), i + 1)
                ve.wait_ge(sig("kk_var"), i + 1)
                link(stt(scr(0)[0:n, :], f(F_A), -1.0, par["rwkv_k_a"][0:n, :], ALU.add, ALU.mult))
                link(stt(f(F_KH), scr(0)[0:n, :], 1.0, k_, ALU.add, ALU.mult))
                yield "bonus"
                link(tt(scr(0)[0:n, :], r, f(F_KH), ALU.mult))
                link(tt(scr(0)[0:n, :], scr(0)[0:n, :], par["rwkv_r_k"][0:n, :], ALU.mult))
                link(v.tensor_reduce(st[0:n, 56:64], s3(scr(0)[0:n, :]), AX.X, ALU.add))
                yield "kk_norm"
                ve.wait_ge(sig("kk_root"), i + 1)
                link(v.tensor_scalar(st[0:n, 40:48], st[0:n, 40:48], 1e-12, None, ALU.max))
                link(v.reciprocal(st[0:n, 40:48], st[0:n, 40:48]))
                link(tt(s3(f(F_KK)), s3(f(F_KK)), bc(st[0:n, 40:48], [n, H, HD], 2), ALU.mult))
                link(tt(f(F_A), f(F_A), f(F_KK), ALU.mult))
                yield "cum"
                ve.wait_ge(sig("lw_ready"), i + 1)
                if prompt:
                    b = see(ve, i, "cum")
                    tt(f(F_PX), b[:, :], f(F_LW), ALU.subtract).then_inc(sig("cex_ready"), 1)
                    yield "hats0"
                    ve.wait_ge(sig("exps_ready"), i + 1)
                    tt(f(F_A), f(F_A), f(F_PI), ALU.mult)
                    tt(f(F_PC), f(F_PC), r, ALU.mult)
                    yield "hats1"
                    link(stt(f(F_PX), f(F_KK), -1.0, f(F_PX), ALU.mult, ALU.mult))
                    tt(f(F_PI), f(F_PI), f(F_KH), ALU.mult).then_inc(sig("hats_ready"), 1)
                    yield "masked_v"
                    ve.wait_ge(sig("hats_ready"), i + 1)
                    v.memset(sms[1][:, 2:4, :], 0.0)
                    v.memset(feat[64:128, V0, :], 0.0)
                    v.memset(feat[0:64, V1, :], 0.0).then_inc(sig("v01_ready"), 1)
                    yield from by_turns(half(i, 0), half(i, 1))
                else:
                    ve.wait_ge(sig("exps_ready"), i + 1)
                    ve.sem_inc(sig("sfeat_ready"), 1)
                    yield from sample_step()
                ve.sem_inc(sig("wkv_done"), 1)
                yield from group_norm("gn", i + 1, n, yv[0:n, :], yv[0:n, :], "rwkv_ln_g", "rwkv_ln_b")
                yield "gn_bonus"
                link(tt(s3(scr(0)[0:n, :]), s3(v_), bc(st[0:n, 56:64], [n, H, HD], 2), ALU.mult))
                link(tt(yv[0:n, :], yv[0:n, :], scr(0)[0:n, :], ALU.add))
                yield "gn_gate"
                after_read(ve, i, "g_lora")
                tt(z[0:n, 0:DA], yv[0:n, :], f(F_G), ALU.mult).then_inc(sig("z_ready"), 1)
                ve.sem_inc(sig("gain_free"), 1)
                for c in range(4):
                    yield f"wout{c + 1}"
                    if c == 0:
                        ve.wait_ge(sig("xres_loaded"), 16 * i + 16)
                    b = see(ve, i, f"wout{c}")
                    has_read(i, f"wout{c}", tt(x[0:n, c * WC:(c + 1) * WC], b[0:n, 0:WC], x[0:n, c * WC:(c + 1) * WC], ALU.add))
                after_read(ve, i, "wout2")
                after_read(ve, i, "wout3")
                ve.sem_inc(sig("x1_ready"), 1)
                yield "xn2"
                link(root_to_scale("n2", i + 1, n, 3))
                ve.wait_ge(sig("gain_loaded"), 16 * i + 16)
                stt(xn2[0:n, :], x[0:n, :], st[0:n, 5:6], gain[0:n, :], ALU.mult, ALU.mult).then_inc(sig("xn2_ready"), 1)
                ve.wait_ge(sig("xn2_ready"), i + 1)
                ve.sem_inc(sig("gain_used"), 1)
                ve.sem_inc(sig("x_norm_done"), 1)
                cand = sc_all[0:n, :].rearrange("p (h a b) -> p h a b", h=H, a=TOPK)
                tops = lambda h, c: top16(sc_all[0:n, h * 256 + c * NK:h * 256 + (c + 1) * NK], tkv[0:n, 0:NK], sv[0:n, h, c, :], si[0:n, h, c, :])
                for h in range(1, H + 2):
                    if h > 1:
                        yield f"q{h}"
                        tops(h - 2, 1)
                        yield f"ctop{h - 2}"
                        done = slice((h - 2) * TOPK, (h - 1) * TOPK)
                        link(tt(cand[:, h - 2], bc(sv[0:n, h - 2, 0, :], [n, TOPK, TOPK], 2), bc(sv[0:n, h - 2, 1, :], [n, TOPK, TOPK], 1), ALU.add))
                        top16(sc_all[0:n, (h - 2) * 256:(h - 1) * 256], tkv[0:n, :], cv[0:n, done], ci[0:n, done])
                    if h <= H:
                        yield f"top{h}"
                        after_read(ve, i, f"sc{h - 1}")
                        settle(ve)
                        tops(h - 1, 0)
                yield "soft"
                c3 = lambda ap: ap.rearrange("p (h k) -> p h k", h=H)
                link(v.tensor_copy(st[0:n, 48:56], c3(cv[0:n, :])[:, :, 0]))
                tt(c3(cv[0:n, :]), c3(cv[0:n, :]), bc(st[0:n, 48:56], [n, H, TOPK], 2), ALU.subtract).then_inc(sig("cv_ready"), 1)
                link(v.tensor_copy(sif[0:n], si[0:n]))
                o4 = oneh[0:n, :].rearrange("p (h j k) -> p h j k", h=H, j=TOPK)
                for half_, dst in ((0, e1), (1, e2)):
                    yield f"digit{half_}a"
                    op, arg = (ALU.logical_shift_right, 4) if half_ == 0 else (ALU.bitwise_and, TOPK - 1)
                    link(v.tensor_scalar(hi[0:n, :], ci[0:n, :], arg, None, op))
                    link(v.tensor_copy(dst[0:n, :], hi[0:n, :]))
                    link(tt(oneh[0:n, :].rearrange("p (j k) -> p j k", k=TOPK), bc(dst[0:n, :], [n, HK, TOPK], 2), bc(iota16[0:n, :], [n, HK, TOPK], 1), ALU.is_equal))
                    yield f"digit{half_}b"
                    for h in range(H):
                        ins = tt(o4[:, h], o4[:, h], bc(sif[0:n, h, half_, :], [n, TOPK, TOPK], 1), ALU.mult)
                    link(ins)
                    yield f"digit{half_}c"
                    link(v.tensor_reduce(dst[0:n, :], oneh[0:n, :].rearrange("p (j k) -> p j k", k=TOPK), AX.X, ALU.add))
                yield "expert"
                link(stt(e1[0:n, :], e1[0:n, :], float(NK), e2[0:n, :], ALU.mult, ALU.add))
                at = (i % 2) * HK
                link(v.tensor_copy(eidx[0:n, at:at + HK] if isinstance(i, int) else eidx[:, bass.ds(at, HK)], e1[0:n, :]))
                ve.wait_ge(sig("cv_exp"), i + 1)
                link(v.tensor_reduce(st[0:n, 48:56], c3(gate[0:n, :]), AX.X, ALU.add))
                link(v.reciprocal(st[0:n, 48:56], st[0:n, 48:56]))
                link(tt(c3(gate[0:n, :]), c3(gate[0:n, :]), bc(st[0:n, 48:56], [n, H, TOPK], 2), ALU.mult))
                restart()
                ve.sem_inc(sig("topk_done"), 1)

            def top16(s, tmp, val, idx):
                link(v.max(val[:, 0:8], s))
                v.max_index(idx[:, 0:8], val[:, 0:8], s)
                link(v.match_replace(tmp, val[:, 0:8], s, NEG))
                link(v.max(val[:, 8:16], tmp))
                link(v.max_index(idx[:, 8:16], val[:, 8:16], tmp))

            def sample_step():
                fr, fk, fv, fw, fkk, fb = (ms[0:64, 0, 64 * k:64 * k + 64] for k in range(6))
                S = ft[0:64, 0:2, :].rearrange("p a n -> p (a n)").rearrange("p (v k) -> p v k", v=16)
                tmp = ft[0:64, 2:4, :].rearrange("p a n -> p (a n)").rearrange("p (v k) -> p v k", v=16)
                sa = ms[0:64, 2, 0:16]
                over_v = lambda ap: bc(ap, [64, 16, HD], 1)
                over_k = lambda ap: bc(ap, [64, 16, HD], 2)
                for q in range(4):
                    vq = fv[:, 16 * q:16 * q + 16]
                    yield f"h0_update{q + 1}"
                    if q == 0:
                        ve.wait_ge(sig("sfeat_loaded"), 16)
                    ve.wait_ge(sig("swkv_loaded"), 16 * q + 16)
                    link(tt(tmp, S, over_v(fkk), ALU.mult))
                    link(v.tensor_reduce(sa, tmp, AX.X, ALU.add))
                    link(tt(S, S, over_v(fw), ALU.mult))
                    link(tt(tmp, over_k(sa), over_v(fb), ALU.mult))
                    link(tt(S, S, tmp, ALU.subtract))
                    link(tt(tmp, over_k(vq), over_v(fk), ALU.mult))
                    link(tt(S, S, tmp, ALU.add))
                    link(tt(tmp, S, over_v(fr), ALU.mult))
                    v.tensor_reduce(ms[0:64, 1, 16 * q:16 * q + 16], tmp, AX.X, ALU.add).then_inc(sig("swkv_new"), 1)
                    ve.wait_ge(sig("swkv_new"), q + 1)

            def half(i, g):
                h4 = lambda ap: ap.rearrange("p (h t) -> p h t", h=4)
                mask = lambda m: bc(m, [P, 4, P], 1)
                masked = {"MT": (MT[g], m_strict), "MakT": (MakT[g], m_strict), "MrbT": (MrbT[g], m_incl), "MrkT": (MrkT[g], m_incl)}
                TTg, TIg, CTg, SMg = TT[g], TI[g], CT[g], sms[g]

                def keep(use):
                    dst, m = masked[use]
                    b = see(ve, i, f"{use}{g}")
                    has_read(i, f"{use}{g}", tt(h4(dst), h4(b[:, :]), mask(m[:, :]), ALU.mult))

                yield f"h{g}_TT"
                keep("MT")
                after_read(ve, i, f"MT{g}")
                link(tt(h4(TTg), h4(MT[g]), mask(m_level[:, 0, :]), ALU.mult))
                link(tt(h4(TTg), h4(TTg), mask(ident[:, :]), ALU.add))
                yield f"h{g}_TI"
                b = see(ve, i, f"M{g}")
                has_read(i, f"M{g}", tt(h4(TIg), h4(b[:, :]), mask(m_pairT[:, :]), ALU.mult))
                after_read(ve, i, f"M{g}")
                link(tt(h4(TIg), h4(TIg), mask(ident[:, :]), ALU.add))
                tt(h4(CTg), h4(MT[g]), mask(m_level[:, 1, :]), ALU.mult).then_inc(sig(f"CT{g}_ready"), 1)
                keep("MakT")
                for m in range(1, LEVELS):
                    yield f"h{g}_merge{m}"
                    if m == 1:
                        keep("MrbT")
                    yield f"h{g}_update{m}"
                    if m < LEVELS - 1:
                        b = see(ve, i, f"TX{g}{m}")
                        has_read(i, f"TX{g}{m}", tt(TIg, b[:, :], TIg, ALU.add))
                    b = see(ve, i, f"TXt{g}{m}")
                    has_read(i, f"TXt{g}{m}", tt(TTg, b[:, :], TTg, ALU.add))
                    if m < LEVELS - 1:
                        after_read(ve, i, f"TX{g}{m}")
                        after_read(ve, i, f"TXt{g}{m}")
                        tt(h4(CTg), h4(MT[g]), mask(m_level[:, m + 1, :]), ALU.mult).then_inc(sig(f"CT{g}_ready"), 1)
                    if m == 2:
                        keep("MrkT")
                STg = ST[:, 4 * g:4 * g + 4, :]
                for q in range(2):
                    p0, p1 = CH * q, CH * q + CH
                    yield f"h{g}_dS{q}"
                    if q == 0:
                        after_read(ve, i, f"U1{g}")
                    b = see(ve, i, f"SR{g}{q}")
                    tt(SMg[p0:p1, 2 + q, :], b[p0:p1, 0:256], SMg[p0:p1, 1, :], ALU.add)
                    has_read(i, f"SR{g}{q}", v.tensor_copy(SMg[p0:p1, 4, :], b[p0:p1, 256:512]))
                    yield f"h{g}_SR1" if q == 0 else f"h{g}_Y"
                    b = see(ve, i, f"dS{g}{q}")
                    has_read(i, f"dS{g}{q}", tt(STg, b[0:64, 0:256].rearrange("p (h v) -> p h v", h=4), STg, ALU.add))
                    after_read(ve, i, f"dS{g}{q}")
                    tt(STg, STg, bc(PL[:, 4 * g:4 * g + 4, q], [64, 4, HD], 2), ALU.mult).then_inc(sig(f"ST{g}_ready"), 1)
                b = see(ve, i, f"Y{g}")
                after_read(ve, i, f"SR{g}1")
                has_read(i, f"Y{g}", tt(yv[:, 256 * g:256 * g + 256], b[:, 0:256], SMg[:, 4, :], ALU.add))
                after_read(ve, i, f"Y{g}")

            def handoff(i):
                if not isinstance(i, int) or 0 < i <= NB:
                    v.tensor_copy(pgate[:, :], gate[:, :])
                    v.tensor_copy(px[:, :], xn2[:, :]).then_inc(sig("handed"), 1)
                    ve.wait_ge(sig("handed"), i)
                elif i == NB + 1:
                    b = see(ve, NB, "eT")
                    v.tensor_copy(sidx[:, :], b[:, 0:NS])
                    has_read(NB, "eT", v.tensor_copy(pgate[:, 0:NS], b[:, NS:2 * NS]))
                    after_read(ve, NB, "eT")
                    ve.sem_inc(sig("handed"), 1)

            def take_sums(i):
                j = i - 2
                sample = isinstance(i, int) and j == NB
                m = NS if sample else P
                ve.wait_ge(sig("x1_loaded"), 16 * j + 16)
                if sample:
                    ve.wait_ge(sig("sample_summed"), 1)
                else:
                    link(tt(x[:, :], x[:, :], accv[:, :], ALU.add))
                    ve.wait_ge(sig("vpe_used"), summed(pe_experts, i - 1, UNITS - 1))
                for c in range(2):
                    ins = tt(x[0:m, c * 512:(c + 1) * 512], acc[c][0:m, :], x[0:m, c * 512:(c + 1) * 512], ALU.add)
                link(ins)
                restart()
                ve.sem_inc(sig("x2_ready"), 1)
                ve.sem_inc(sig("acc_read"), 1)

            def tail(i):
                j = i - 2
                n = NS if isinstance(i, int) and j == NB else P
                yield "t_sum"
                take_sums(i)
                yield "t_turn"
                root_to_scale("n3", j + 1, n, 6).then_inc(sig("n3_rs"), 1)
                yield "t_xT"
                for k in range(2):
                    b = see(ve, i, f"t_xT{k}")
                    has_read(i, f"t_xT{k}", tt(xT[:, 4 * k:4 * k + 4, 0:n], b[:, 0:4 * n].rearrange("p (k t) -> p k t", k=4),
                                               bc(vecs[:, KN, 4 * k:4 * k + 4], [P, 4, n], 2), ALU.mult))
                for c in range(4):
                    yield f"gate{c + 1}"
                    if c == 0:
                        after_read(ve, i, "ple1")
                    after_read(ve, i, f"gate{c}")
                    link(tt(xn_gate(c)[0:n, :], xn_gate(c)[0:n, :], uv[0:n, c * WC:(c + 1) * WC], ALU.mult))
                    link(tt(x[0:n, c * WC:(c + 1) * WC], xn_gate(c)[0:n, :], x[0:n, c * WC:(c + 1) * WC], ALU.add))
                ve.sem_inc(sig("x3_ready"), 1)
                yield "y"
                link(root_to_scale("n4", j + 1, n, 9))
                ve.wait_ge(sig("fgain_loaded"), 16 * j + 16)
                stt(x[0:n, :], x[0:n, :], st[0:n, 11:12], gain[0:n, :], ALU.mult, ALU.mult).then_inc(sig("y_ready"), 1)
                restart()

            def weigh(i, n):
                ve.wait_ge(sig("gelu_ready"), (i - 1) * UNITS + n + 1)
                tt(pact[:, n % 2, :], pg[:, n % 2, :], pgate[:, n * UNIT:(n + 1) * UNIT], ALU.mult).then_inc(sig("act_ready"), 1)

            def sum_v(i, n, j):
                s = n % 2 * UNIT + j
                act_j = pact[:, n % 2, j:j + 1]
                ve.wait_ge(sig("act_ready"), (i - 1) * UNITS + n + 1)
                ve.wait_ge(sig(f"v{s}_full"), 16 * ((i - 1) * (UNITS // 2) + n // 2 + 1))
                wait_pos(ve, sig("vve_used"), summed(ve_experts, i, n, j) - 1)
                if n == 0 and j == ve_experts(0)[0]:
                    ins = v.tensor_scalar(accv[:, :], vring[:, s, :], act_j, None, ALU.mult)
                else:
                    ins = stt(accv[:, :], vring[:, s, :], act_j, accv[:, :], ALU.mult, ALU.add)
                ins.then_inc(sig("vve_used"), 1)

            def expert(i, n, j):
                s = n % 2 * UNIT + j
                ve.wait_ge(sig(f"u{s}_full"), 16 * ((i - 1) * (UNITS // 2) + n // 2 + 1))
                v.tensor_tensor_reduce(out=uring[:, s, :], in0=uring[:, s, :], in1=px[:, :], scale=1.0, scalar=0.0,
                                       op0=ALU.mult, op1=ALU.add, accum_out=ph[:, n % 2, j:j + 1]).then_inc(sig("u_used"), 1)
                if n and j == 0:
                    weigh(i, n - 1)
                if n and j in ve_experts(n - 1):
                    sum_v(i, n - 1, j)

            def finish(i):
                weigh(i, UNITS - 1)
                for j in ve_experts(UNITS - 1):
                    sum_v(i, UNITS - 1, j)
                ve.wait_ge(sig("act_ready"), i * UNITS)
                ve.wait_ge(sig("vve_used"), summed(ve_experts, i, UNITS - 1))

            def peer_sample():
                for t in range(NS):
                    ve.wait_ge(sig(f"u{t}_full"), 16 * (NB * (UNITS // 2) + 1))
                    ve.wait_ge(sig(f"sxt{t}_loaded"), 16)
                    v.tensor_tensor_reduce(out=uring[:, t, :], in0=uring[:, t, :], in1=vring[:, t, :], scale=1.0, scalar=0.0,
                                           op0=ALU.mult, op1=ALU.add, accum_out=ph[:, t // UNIT, t % UNIT:t % UNIT + 1]).then_inc(sig("sxt_used"), 1)
                c = NB * UNITS
                ve.wait_ge(sig("gelu_ready"), c + 1)
                tt(pact[:, :, :].rearrange("p a b -> p (a b)"), pg[:, :, :].rearrange("p a b -> p (a b)"), pgate[:, 0:NS], ALU.mult).then_inc(sig("act_ready"), 1)
                ve.wait_ge(sig("act_ready"), c + 1)
                tt(sdg[:, :, :], diag8[:, :, :], bc(pact[:, :, :].rearrange("p a b -> p (a b)"), [P, NS, NS], 2), ALU.mult).then_inc(sig("diag_ready"), 1)

            drive(front, tail, expert, finish, handoff, peer_sample, ve)


_INS = ['x_prompt', 'x_sample', 'state_wkv', 'state_shift', 'p_prompt', 'p_sample', 'norm_mix_g', 'w_in', 'shift_mu', 'rwkv_w0',
        'rwkv_w2', 'rwkv_a0', 'rwkv_a2', 'rwkv_g2', 'rwkv_k_k', 'rwkv_k_a', 'rwkv_r_k', 'rwkv_ln_g', 'rwkv_ln_b', 'cmlp_ln_g',
        'cmlp_ln_b', 'cmlp_ws', 'cmlp_bs', 'w_out', 'norm_ffn_g', 'peer_wq', 'peer_subkeys', 'peer_u', 'peer_v', 'norm_ple_g',
        'ple_w', 'ple_gate_w', 'norm_final_g']
_OUTS = [((1, T_PROMPT, D), 'float32'), ((NS, 1, D), 'float32'), ((1, 1, H, HD, HD), 'float32'), ((1, 1, PA), 'float32'),
         ((1, NS, H, HD, HD), 'float32'), ((1, NS, PA), 'float32'), ((1, NS, 1, DA), 'float32')]


def kernel(**inputs):
    import numpy as _np
    import concourse.bacc as _bacc
    from concourse import mybir as _mybir
    from concourse.bass_utils import run_bass_kernel_spmd as _run

    nc = _bacc.Bacc("TRN2", target_bir_lowering=False, num_devices=1)
    arrays, args, outs = {}, {}, []
    for name in _INS:
        arr = _np.ascontiguousarray(inputs[name])
        arrays[f"in_{name}_dram"] = arr
        args[name] = nc.dram_tensor(f"in_{name}_dram", arr.shape, _mybir.dt.from_np(arr.dtype), kind="ExternalInput").ap()
    for i, (shape, dtype) in enumerate(_OUTS):
        outs.append(nc.dram_tensor(f"out_{i}_dram", shape, _mybir.dt.from_np(_np.dtype(dtype)), kind="ExternalOutput").ap())
    build(nc, args, outs)
    r = _run(nc, [arrays], core_ids=[0])
    return tuple(r.results[0][f"out_{i}_dram"] for i in range(len(_OUTS)))
```
